# Optimizing a Trainium2 kernel written in Bass

```python
import math
import jax
import jax.numpy as jnp
from jax import lax
import numpy as np

D_MODEL = 1024
BATCH = 1
SEQ = 256
DEPTH = 2

GRID_W = 64
CTX_LEN = 256
N_EVEN = (DEPTH + 1) // 2
N_ODD = DEPTH // 2
EPS = 1e-6

CONV_CH = D_MODEL // 2
CONV_W = 3
NA_HEADS = 8
NA_HEAD_DIM = D_MODEL // 2 // NA_HEADS
NA_DIM = NA_HEADS * NA_HEAD_DIM
WIN_H = 8
WIN_W = 16
EVEN_IN = 3 * CONV_CH + 3 * NA_DIM
EVEN_OUT = CONV_CH + NA_DIM

RET_HEADS = 4
RET_QK_DIM = D_MODEL // RET_HEADS
RET_V_DIM = 2 * RET_QK_DIM
RET_CHUNK = 128
RET_QK = RET_HEADS * RET_QK_DIM
RET_V = RET_HEADS * RET_V_DIM
ODD_IN = 2 * RET_QK + 2 * RET_V
ROPE_BASE = 10000.0

N_GROUPS = 4
EXPERTS_PER_GROUP = 8
EXPERT_HIDDEN = D_MODEL // 4
TOP_K_IN_GROUP = 2
GROUP_HIDDEN = EXPERTS_PER_GROUP * EXPERT_HIDDEN

kernel_name = 'hybrid_dit_shortconv_natten_retnet_hmoe'

def rmsnorm(x, g):
    xf = x.astype(jnp.float32)
    y = xf * lax.rsqrt(jnp.mean(xf * xf, axis=-1, keepdims=True) + EPS)
    return (y * g.astype(jnp.float32)).astype(x.dtype)

def modulate(h, shift, scale):
    return h * (1 + scale) + shift

def short_conv(u, w):
    up = jnp.pad(u, ((0, 0), (1, 1), (0, 0)))
    return up[:, :-2] * w[0] + up[:, 1:-1] * w[1] + up[:, 2:] * w[2]

def dense_attention(q, k, v):
    s = jnp.einsum('bqhd,bkhd->bhqk', q, k).astype(jnp.float32)
    p = jax.nn.softmax(s, axis=-1).astype(v.dtype)
    o = jnp.einsum('bhqk,bkhd->bqhd', p, v)
    return o.reshape(o.shape[0], o.shape[1], -1)

def neighborhood_attention(q, k, v, k_ctx, v_ctx, rpb):
    B, L, H, Dh = q.shape
    rows = L // GRID_W
    kh = min(WIN_H, rows)
    kw = min(WIN_W, GRID_W)
    qg = q.reshape(B, rows, GRID_W, H, Dh)
    kg = k.reshape(B, rows, GRID_W, H, Dh)
    vg = v.reshape(B, rows, GRID_W, H, Dh)
    cols = jnp.arange(GRID_W)
    col_idx = jnp.clip(cols - kw // 2, 0, GRID_W - kw)[:, None] + jnp.arange(kw)[None, :]
    rpb_cols = rpb.astype(jnp.float32)[:, :, col_idx - cols[:, None] + WIN_W - 1]

    def row_block(r):
        rs = jnp.clip(r - kh // 2, 0, rows - kh)
        q_r = lax.dynamic_index_in_dim(qg, r, axis=1, keepdims=False)
        k_win = lax.dynamic_slice_in_dim(kg, rs, kh, axis=1)[:, :, col_idx]
        v_win = lax.dynamic_slice_in_dim(vg, rs, kh, axis=1)[:, :, col_idx]
        dy = rs + jnp.arange(kh) - r + WIN_H - 1
        bias = jnp.take(rpb_cols, dy, axis=1).transpose(0, 2, 1, 3)
        s_loc = jnp.einsum('bchd,bicjhd->bhcij', q_r, k_win).astype(jnp.float32) + bias
        s_ctx = jnp.einsum('bchd,bnhd->bhcn', q_r, k_ctx).astype(jnp.float32)
        logits = jnp.concatenate([s_loc.reshape(B, H, GRID_W, kh * kw), s_ctx], axis=-1)
        p = jax.nn.softmax(logits, axis=-1).astype(v.dtype)
        p_loc = p[..., :kh * kw].reshape(B, H, GRID_W, kh, kw)
        return (jnp.einsum('bhcij,bicjhd->bchd', p_loc, v_win)
                + jnp.einsum('bhcn,bnhd->bchd', p[..., kh * kw:], v_ctx))

    out = lax.map(row_block, jnp.arange(rows))
    return jnp.moveaxis(out, 0, 1).reshape(B, L, H * Dh)

def rope_1d(t, pos):
    half = t.shape[-1] // 2
    freqs = ROPE_BASE ** (-jnp.arange(half, dtype=jnp.float32) / half)
    ang = pos.astype(jnp.float32)[:, None] * freqs[None, :]
    cos, sin = jnp.cos(ang), jnp.sin(ang)
    t1, t2 = t[..., :half], t[..., half:]
    return jnp.concatenate([t1 * cos - t2 * sin, t2 * cos + t1 * sin], axis=-1)

def axial_rope(t, n_tokens):
    pos = jnp.arange(n_tokens)
    half = t.shape[-1] // 2
    return jnp.concatenate([rope_1d(t[..., :half], pos // GRID_W),
                            rope_1d(t[..., half:], pos % GRID_W)], axis=-1)

def retention_scan(q, k, v, log_gamma, s0):
    B, H, L, _ = q.shape
    Dv = v.shape[-1]
    n = L // RET_CHUNK
    pos = jnp.arange(RET_CHUNK, dtype=jnp.float32)
    rel = pos[:, None] - pos[None, :]
    d_intra = jnp.where(rel >= 0, jnp.exp(log_gamma[:, None, None] * jnp.maximum(rel, 0.0)), 0.0)
    d_query = jnp.exp(log_gamma[:, None] * (pos + 1.0))[..., None]
    d_key = jnp.exp(log_gamma[:, None] * (RET_CHUNK - 1.0 - pos))[..., None]
    d_chunk = jnp.exp(log_gamma * RET_CHUNK)[:, None, None]

    def chunks(t):
        return jnp.moveaxis(t.reshape(B, H, n, RET_CHUNK, t.shape[-1]), 2, 0)

    def step(state, qkv):
        qc, kc, vc = qkv
        scores = jnp.einsum('bhid,bhjd->bhij', qc, kc) * d_intra
        out = (jnp.einsum('bhij,bhje->bhie', scores, vc)
               + jnp.einsum('bhid,bhde->bhie', qc, state) * d_query)
        state = state * d_chunk + jnp.einsum('bhjd,bhje->bhde', kc * d_key, vc)
        return state, out

    state, out = lax.scan(step, s0, (chunks(q), chunks(k), chunks(v)))
    return jnp.moveaxis(out, 0, 2).reshape(B, H, L, Dv), state

def even_mixer(h, hc, w_in, conv_w, rpb, w_out, with_ctx):
    cuts = [CONV_CH, 2 * CONV_CH, 3 * CONV_CH, 3 * CONV_CH + NA_DIM, 3 * CONV_CH + 2 * NA_DIM]
    a_b, a_c, a_x, q, k, v = jnp.split(h @ w_in, cuts, axis=-1)
    ca_b, ca_c, ca_x, cq, ck, cv = jnp.split(hc @ w_in, cuts, axis=-1)

    def heads(t):
        return t.reshape(t.shape[0], t.shape[1], NA_HEADS, NA_HEAD_DIM)

    scale = NA_HEAD_DIM ** -0.5
    ck, cv = heads(ck), heads(cv)
    y_conv = a_b * short_conv(a_c * a_x, conv_w)
    y_attn = neighborhood_attention(heads(q) * scale, heads(k), heads(v), ck, cv, rpb)
    y = jnp.concatenate([y_conv, y_attn], axis=-1) @ w_out
    if not with_ctx:
        return y, None
    yc_conv = ca_b * short_conv(ca_c * ca_x, conv_w)
    yc_attn = dense_attention(heads(cq) * scale, ck, cv)
    return y, jnp.concatenate([yc_conv, yc_attn], axis=-1) @ w_out

def odd_mixer(h, hc, w_in, decay_f, decay_b, w_out, with_ctx):
    B, L, _ = h.shape
    cuts = [RET_QK, 2 * RET_QK, 2 * RET_QK + RET_V]
    q, k, v, g = jnp.split(h @ w_in, cuts, axis=-1)
    qc, kc, vc, gc = jnp.split(hc @ w_in, cuts, axis=-1)

    def heads(t, d):
        return jnp.swapaxes(t.reshape(t.shape[0], t.shape[1], RET_HEADS, d), 1, 2).astype(jnp.float32)

    scale = RET_QK_DIM ** -0.5
    q = axial_rope(heads(q, RET_QK_DIM), L)
    k = axial_rope(heads(k, RET_QK_DIM), L) * scale
    v = heads(v, RET_V_DIM)
    qc = heads(qc, RET_QK_DIM)
    kc = heads(kc, RET_QK_DIM) * scale
    vc = heads(vc, RET_V_DIM)
    lg_f = jnp.log1p(-jnp.exp(decay_f.astype(jnp.float32)))
    lg_b = jnp.log1p(-jnp.exp(decay_b.astype(jnp.float32)))
    zero = jnp.zeros((B, RET_HEADS, RET_QK_DIM, RET_V_DIM), jnp.float32)
    flip = lambda t: jnp.flip(t, axis=2)
    yc_f, s_f = retention_scan(qc, kc, vc, lg_f, zero)
    yc_b, s_b = retention_scan(flip(qc), flip(kc), flip(vc), lg_b, zero)
    y_f, _ = retention_scan(q, k, v, lg_f, s_f)
    y_b, _ = retention_scan(flip(q), flip(k), flip(v), lg_b, s_b)

    def head_out(y, gate):
        y = y * lax.rsqrt(jnp.mean(y * y, axis=-1, keepdims=True) + EPS)
        y = jnp.swapaxes(y, 1, 2).reshape(gate.shape).astype(gate.dtype)
        return (jax.nn.silu(gate) * y) @ w_out

    y = head_out(y_f + flip(y_b), g)
    yc = head_out(yc_f + flip(yc_b), gc) if with_ctx else None
    return y, yc

def hier_moe(h, gw, gb, ew, eb, w1, w3, w2):
    B, L, _ = h.shape
    gp = jax.nn.softmax((h @ gw + gb).astype(jnp.float32), axis=-1)
    g_val, g_idx = lax.top_k(gp, 1)
    g_onehot = jax.nn.one_hot(g_idx[..., 0], N_GROUPS, dtype=jnp.float32)
    el = (h @ ew + eb).astype(jnp.float32).reshape(B, L, N_GROUPS, EXPERTS_PER_GROUP)
    ep = jax.nn.softmax(jnp.sum(el * g_onehot[..., None], axis=-2), axis=-1)
    e_val, e_idx = lax.top_k(ep, TOP_K_IN_GROUP)
    e_w = e_val / jnp.sum(e_val, axis=-1, keepdims=True) * g_val
    w_in_group = jnp.sum(jax.nn.one_hot(e_idx, EXPERTS_PER_GROUP, dtype=jnp.float32) * e_w[..., None], axis=-2)
    gates = (g_onehot[..., None] * w_in_group[..., None, :]).astype(h.dtype)
    out = jnp.zeros_like(h)
    for gi in range(N_GROUPS):
        hid = jax.nn.silu(h @ w1[gi]) * (h @ w3[gi])
        hid = hid.reshape(B, L, EXPERTS_PER_GROUP, EXPERT_HIDDEN) * gates[:, :, gi, :, None]
        out = out + hid.reshape(B, L, GROUP_HIDDEN) @ w2[gi]
    return out

def setup_inputs(seed: int = 0) -> dict:
    key = jax.random.key(seed)
    ks = jax.random.split(key, 24)
    f32 = jnp.float32
    D = D_MODEL

    def nrm(k, shape, s):
        return jax.random.normal(k, shape, f32) * s

    decay_base = -(5.0 + jnp.arange(RET_HEADS, dtype=f32)) * math.log(2.0)
    return {
        'x': nrm(ks[0], (BATCH, SEQ, D), 1.0),
        'c': nrm(ks[1], (BATCH, D), 1.0),
        'ctx': nrm(ks[2], (BATCH, CTX_LEN, D), 1.0),
        'c_ctx': nrm(ks[3], (D,), 1.0),
        'ada_w': nrm(ks[4], (DEPTH, D, 6 * D), 0.5 * D ** -0.5),
        'ada_b': nrm(ks[5], (DEPTH, 6 * D), 0.02),
        'norm1_g': 1.0 + nrm(ks[6], (DEPTH, D), 0.02),
        'norm2_g': 1.0 + nrm(ks[7], (DEPTH, D), 0.02),
        'w_in_e': nrm(ks[8], (N_EVEN, D, EVEN_IN), D ** -0.5),
        'conv_w': nrm(ks[9], (N_EVEN, CONV_W, CONV_CH), CONV_W ** -0.5),
        'na_rpb': nrm(ks[10], (N_EVEN, NA_HEADS, 2 * WIN_H - 1, 2 * WIN_W - 1), 0.1),
        'w_out_e': nrm(ks[11], (N_EVEN, EVEN_OUT, D), EVEN_OUT ** -0.5),
        'w_in_o': nrm(ks[12], (N_ODD, D, ODD_IN), D ** -0.5),
        'ret_decay_f': decay_base + nrm(ks[13], (N_ODD, RET_HEADS), 0.05),
        'ret_decay_b': decay_base + nrm(ks[14], (N_ODD, RET_HEADS), 0.05),
        'w_out_o': nrm(ks[15], (N_ODD, RET_V, D), RET_V ** -0.5),
        'router_gw': nrm(ks[16], (DEPTH, D, N_GROUPS), D ** -0.5),
        'router_gb': nrm(ks[17], (DEPTH, N_GROUPS), 0.01),
        'router_ew': nrm(ks[18], (DEPTH, D, N_GROUPS * EXPERTS_PER_GROUP), D ** -0.5),
        'router_eb': nrm(ks[19], (DEPTH, N_GROUPS * EXPERTS_PER_GROUP), 0.01),
        'moe_w1': nrm(ks[20], (DEPTH, N_GROUPS, D, GROUP_HIDDEN), D ** -0.5),
        'moe_w3': nrm(ks[21], (DEPTH, N_GROUPS, D, GROUP_HIDDEN), D ** -0.5),
        'moe_w2': nrm(ks[22], (DEPTH, N_GROUPS, GROUP_HIDDEN, D), EXPERT_HIDDEN ** -0.5),
        'final_g': 1.0 + nrm(ks[23], (D,), 0.02),
    }

def reference(x, c, ctx, c_ctx, ada_w, ada_b, norm1_g, norm2_g, w_in_e, conv_w, na_rpb, w_out_e,
              w_in_o, ret_decay_f, ret_decay_b, w_out_o, router_gw, router_gb, router_ew, router_eb,
              moe_w1, moe_w3, moe_w2, final_g):
    s_ctx = ctx
    for layer in range(DEPTH):
        with_ctx = layer < DEPTH - 1
        mod_x = (jax.nn.silu(c) @ ada_w[layer] + ada_b[layer])[:, None, :]
        mod_c = (jax.nn.silu(c_ctx) @ ada_w[layer] + ada_b[layer])[None, None, :]
        sh1, sc1, g1, sh2, sc2, g2 = jnp.split(mod_x, 6, axis=-1)
        csh1, csc1, cg1, csh2, csc2, cg2 = jnp.split(mod_c, 6, axis=-1)
        hx = modulate(rmsnorm(x, norm1_g[layer]), sh1, sc1)
        hc = modulate(rmsnorm(s_ctx, norm1_g[layer]), csh1, csc1)
        i = layer // 2
        if layer % 2 == 0:
            y, yc = even_mixer(hx, hc, w_in_e[i], conv_w[i], na_rpb[i], w_out_e[i], with_ctx)
        else:
            y, yc = odd_mixer(hx, hc, w_in_o[i], ret_decay_f[i], ret_decay_b[i], w_out_o[i], with_ctx)
        moe_w = (router_gw[layer], router_gb[layer], router_ew[layer], router_eb[layer],
                 moe_w1[layer], moe_w3[layer], moe_w2[layer])
        x = x + g1 * y
        x = x + g2 * hier_moe(modulate(rmsnorm(x, norm2_g[layer]), sh2, sc2), *moe_w)
        if with_ctx:
            s_ctx = s_ctx + cg1 * yc
            s_ctx = s_ctx + cg2 * hier_moe(modulate(rmsnorm(s_ctx, norm2_g[layer]), csh2, csc2), *moe_w)
    return rmsnorm(x, final_g)


_drawn_inputs = setup_inputs


def setup_inputs(seed=0):
    import zlib

    import numpy as np

    out = dict(_drawn_inputs(seed))
    spreads = {}
    factors = {'norm1_g': 3.565,
     'norm2_g': 3.814,
     'na_rpb': 36.029,
     'router_gb': 27.945,
     'router_eb': 18.453,
     'final_g': 8.645}
    for name, (base, spread) in spreads.items():
        noise = np.random.default_rng([zlib.crc32(name.encode()), seed]).standard_normal(out[name].shape)
        drawn = base * np.exp(spread * noise) if base else spread * noise
        out[name] = jnp.asarray(drawn.astype(out[name].dtype))
    for name, factor in factors.items():
        out[name] = (out[name] * factor).astype(out[name].dtype)
    return out
```

```python
from contextlib import ExitStack

import numpy as np
import concourse.bass as bass
from concourse import mybir

F32 = mybir.dt.float32
U32 = mybir.dt.uint32
I32 = mybir.dt.int32
ALU = mybir.AluOpType
ACT = mybir.ActivationFunctionType
AX_X = mybir.AxisListType.X

P = 128
D = 1024
KC = D // P
SEQ = 256
CTX = 256
GRID_W = 64
ROWS = SEQ // GRID_W
WIN_W = 16
HEADS = 8
HEAD_DIM = 64
R_HEADS = 4
R_QK = 256
R_V = 512
ROPE_BASE = 10000.0
GROUPS = 4
PER_GROUP = 8
EXPERTS = GROUPS * PER_GROUP
HIDDEN = 256
GROUP_HIDDEN = PER_GROUP * HIDDEN
EPS = 1e-6
BIG = 1.0e30
TILES = (4, 2)
SLOTS = 64

UNIT = 2048
RING = 12
BANKS = 8
EPI = 4
TURNS = EXPERTS // EPI
PER_EXPERT = 4

CONST_COLS = {}
_at = 0
for _name, _n in (("ident", P), ("upper", P), ("ones", P), ("window", GRID_W), ("idx_group", GROUPS),
                  ("idx_in_group", PER_GROUP), ("idx_expert", EXPERTS), ("half", 1)):
    CONST_COLS[_name] = (_at, _n)
    _at += _n
CONST_N = _at
RET_N = 2 * SEQ * 5 + 4 * SEQ


def shape_constants():
    c = np.zeros((P, CONST_N), np.float32)

    def put(name, a):
        o, n = CONST_COLS[name]
        c[:, o:o + n] = a

    i = np.arange(P)
    put("ident", np.eye(P))
    put("upper", i[:, None] < i[None, :])
    put("ones", 1.0)
    col = i % GRID_W
    first = np.clip(col - WIN_W // 2, 0, GRID_W - WIN_W)
    j = np.arange(GRID_W)
    inside = (j[None, :] >= first[:, None]) & (j[None, :] < first[:, None] + WIN_W)
    put("window", np.where(inside, 0.0, -BIG))
    put("idx_group", np.arange(GROUPS))
    put("idx_in_group", np.arange(PER_GROUP))
    put("idx_expert", np.arange(EXPERTS))
    put("half", (i >= SLOTS)[:, None])

    q = np.arange(SEQ, dtype=np.float32)
    dist = np.stack([q[None, :] - (t * P + i)[:, None] for t in range(2)], 1).astype(np.float32)
    parts = [dist, np.maximum(dist, 0), np.maximum(-dist, 0), dist >= 0, dist <= 0]
    freq = (np.float32(ROPE_BASE) ** (-np.arange(64, dtype=np.float32) / np.float32(64))).astype(np.float32)
    pos = np.arange(SEQ)
    sign = np.where(i < 64, -1.0, 1.0).astype(np.float32)[:, None]
    for axis in (pos // GRID_W, pos % GRID_W):
        ang = (axis.astype(np.float32)[None, :] * freq[i % 64][:, None]).astype(np.float32)
        parts += [np.cos(ang), np.sin(ang) * sign]
    ret = np.concatenate([p.reshape(P, -1) for p in parts], 1).astype(np.float32)
    ids = (2 * (np.arange(4)[None, :, None] * P + i[:, None, None]) + np.arange(2)[None, None, :])
    return c, ret, ids.reshape(P, 8).astype(np.uint32)


def plan_jobs():
    jobs = {}
    n = 0

    def add(*name):
        nonlocal n
        jobs[name] = n
        n += 1

    add("cT")
    add("cwT")
    for q in range(2):
        add("ada", 0, q)
    for q in range(2):
        add("modT", 0, q)
    for t in range(4):
        for half in range(2):
            add("hT", 0, t, half)
    for ch in range(4):
        add("ac", ch)
        add("ax", ch)
        add("ab", ch)
    for ch in range(4):
        add("q", ch)
    for ch in range(4):
        add("k", ch)
    for t in range(4):
        add("v", t)
    for q in range(2, 6):
        add("ada", 0, q)
    items = 4 * HEADS
    add("s", 0)
    add("s", 1)
    for i in range(items):
        if i + 2 < items:
            add("s", i + 2)
        add("pt", i)
        if i % 2 == 0 and i:
            add("pv", i // 2 - 1)
    add("pv", items // 2 - 1)
    for t in range(4):
        for half in range(2):
            add("wo", 0, t, half)
    for q in range(2):
        add("ada", 1, q)
    for q in range(2):
        add("modT", 1, q)
    for q in range(2, 6):
        add("ada", 1, q)

    def experts(layer):
        for t in range(TILES[layer]):
            for half in range(2):
                add("rT", layer, t, half)
        add("logits", layer)
        add("ranks", layer)
        nonlocal n
        jobs[("moe", layer)] = n
        n += EXPERTS * PER_EXPERT

    experts(0)
    for t in range(4):
        for half in range(2):
            add("hT", 1, t, half)
    for h in range(R_HEADS):
        add("rq", h)
        for c in range(2):
            add("rk", h, c)
        for t in range(4):
            add("rv", h, t)
        for a in range(2):
            add("rs", h, a)
        for t in range(2):
            add("rg", h, t)
        for t in range(2):
            add("ro", h, t)
        for t in range(2):
            add("ryT", h, t)
    for t in range(2):
        for half in range(2):
            add("wo", 1, t, half)
    experts(1)
    return jobs


JOBS = plan_jobs()

U_ADA0_A = 0
U_WIN_E = U_ADA0_A + 8
U_ADA0_B = U_WIN_E + 12
U_WOUT_E = U_ADA0_B + 16
U_ADA1 = U_WOUT_E + 4
U_MOE0 = U_ADA1 + 24
U_WIN_O = U_MOE0 + 3 * EXPERTS
U_WOUT_O = U_WIN_O + 24
U_MOE1 = U_WOUT_O + 8
UNITS = U_MOE1 + 3 * EXPERTS

ARENA = 15360
A_BCA, A_BCB = 0, 2048
A_BIAS = 0
A_Q, A_K, A_V, A_YC = 4096, 6144, 8192, 10240
A_P, A_PT = 12288, 13312
A_XN = 13312
A_CONV = 13312
A_TMP = 14336
A_H2 = 4096
A_XG, A_XGT, A_YS, A_SL, A_HID, A_HIDT, A_ROUTE = 4096, 8192, 9216, 11264, 11776, 12288, 12544
A_RQ, A_RK, A_RV, A_RG, A_RY, A_RD = 0, 512, 1536, 3584, 4608, 8704
A_RTAB, A_ROPE, A_RTMP, A_YSC, A_EXP = 9728, 12288, 13312, 14336, 14848
A_XN1 = 4608


def backbone(nc, ins, consts, out):
    (x, c, ctx_in, c_ctx, ada_w, ada_b, norm1_g, norm2_g, w_in_e, conv_w, rpb_rev, w_out_e, w_in_o,
     decay_f, decay_b, w_out_o, router_gw, router_gb, router_ew, router_eb, moe_w1, moe_w3, moe_w2,
     final_g) = ins
    shape_c, ret_c, ids_c = consts

    stack = ExitStack()
    with stack:
        def sb(name, shape, dt=F32):
            return stack.enter_context(nc.sbuf_tensor(name, shape, dt))

        def sem(name):
            return stack.enter_context(nc.semaphore(name))

        mod_rows_d = nc.dram_tensor("mod_rows_d", [12, 2, D], F32).ap()
        h2_d = [nc.dram_tensor(f"h2_d{l}", [TILES[l] * P, D], F32).ap() for l in range(2)]
        table_d = [nc.dram_tensor(f"table_d{l}", [TILES[l] * P * EXPERTS, 1], U32).ap() for l in range(2)]
        y_d = [nc.dram_tensor(f"y_d{l}", [TILES[l] * P * 4, D // 2], F32).ap() for l in range(2)]

        ring = sb("ring", [P, RING, UNIT])
        arena = sb("arena", [P, ARENA])
        res = sb("res", [P, 4, D])
        hT = sb("hT", [P, KC, 4 * P])
        bc_gate = sb("bc_gate", [P, 2, D])
        con = sb("con", [P, CONST_N])
        crow = bc_gate[0:16, 0, 0:P]
        csil = bc_gate[0:16, 0, P:2 * P]
        cwrow = bc_gate[0:12, 0, 2 * P:3 * P]
        cvec = sb("cvec", [P, KC, 32])
        cwT = sb("cwT", [P, 12])
        ada_rows = sb("ada_rows", [P, 2, 2, 256])
        mod_rows = sb("mod_rows", [P, 2, 256])
        modT = sb("modT", [P, 2, 2, KC, 2])
        stat = sb("stat", [P, 3, 4])
        rw = sb("rw", [P, KC, 36])
        rb = sb("rb", [P, 36])
        gates = sb("gates", [P, 2, 4])
        ids = sb("ids", [P, 8], U32)
        addr = sb("addr", [P, 2, 4], U32)
        table = sb("table", [P, EXPERTS], U32)
        gidx = sb("gidx", [SLOTS, EXPERTS], U32)
        sidx = sb("sidx", [P, EXPERTS], U32)
        gnow = sb("gnow", [SLOTS, 8], U32)
        snow = sb("snow", [P, 8], U32)
        ov_table = sb("ov_table", [P, 1], U32)
        ov_idx = sb("ov_idx", [P, 2], U32)
        fullest = sb("fullest", [P, 1], I32)
        soft = sb("soft", [P, 12])
        dec = sb("dec", [P, 8 * 5])

        def const(name):
            o, n = CONST_COLS[name]
            return con[:, o:o + n]

        ident = const("ident")

        def A(at, *shape):
            n = 1
            for s in shape:
                n *= s
            v = arena[:, at:at + n]
            if len(shape) == 2:
                v = v.rearrange("p (a b) -> p a b", b=shape[1])
            if len(shape) == 3:
                v = v.rearrange("p (a b c) -> p a b c", b=shape[1], c=shape[2])
            return v

        banks = [stack.enter_context(nc.psum_tensor(f"bank{b}", [P, 512], F32)) for b in range(BANKS)]

        arrived_s = [sem(f"weights_in{s}") for s in range(RING)]
        full_s = [sem(f"psum_full{b}") for b in range(BANKS)]
        free_s = [sem(f"psum_free{b}") for b in range(BANKS)]
        s_c, s_con, s_x, s_cw = sem("c_in"), sem("constants_in"), sem("x_in"), sem("conv_w_in")
        s_bias = sem("bias_in")
        s_csil, s_ms, s_root, s_rstd, s_xn = (sem("silu_c"), sem("mean_square"), sem("root"),
                                              sem("rstd_ready"), sem("normed_ready"))
        s_ada_in = [sem(f"ada_rows_in{i}") for i in range(2)]
        s_zero = sem("zeroed")
        s_stored = [sem(f"mod_rows_stored{i}") for i in range(2)]
        s_gate, s_ab = sem("gate_rows_in"), sem("scale_and_shift_in")
        s_bias_ready = sem("bias_ready")
        s_scores, s_exp, s_probs = sem("scores_ready"), sem("exp_ready"), sem("probs_ready")
        s_max = sem("max_ready")
        s_mixed = sem("mixer_added")
        s_h2, s_h2_out = sem("h2_ready"), sem("h2_stored")
        s_rw = sem("router_in")
        s_gap, s_rexp = sem("router_gap_ready"), sem("router_exp_ready")
        s_members, s_addr, s_flag = sem("members_ready"), sem("addresses_ready"), sem("fullest_ready")
        s_table_clear, s_table_set, s_table_in = sem("table_cleared"), sem("table_set"), sem("table_in")
        s_idx = sem("indices_ready")
        s_gath = [sem(f"rows_in{u}") for u in range(EPI)]
        s_scat = [sem(f"rows_out{u}") for u in range(EPI)]
        s_now = sem("index_column_ready")
        s_silu = sem("expert_silu_ready")
        s_hid = sem("expert_hidden_ready")
        s_y_in, s_comb = [sem("expert_rows_in0"), sem("expert_rows_in1")], sem("tile_combined")
        s_dec_in, s_dec, s_ret_in = sem("decay_in"), sem("decay_ready"), sem("retention_tables_in")
        s_pe_seen, s_pool_seen = sem("tensor_waits_seen"), sem("gpsimd_waits_seen")
        s_rexps = sem("decay_exp_ready")
        s_factors = sem("decay_factors_added")
        s_yms, s_yroot = sem("y_square_sum"), sem("y_root")
        s_ctx_keys = sem("context_keys_ready")
        s_fin, s_fin_g, s_out = sem("final_ready"), sem("final_g_in"), sem("output_stored")
        s_dve, s_pool = sem("vector_step"), sem("gpsimd_step")
        ov = {}
        for l in range(2):
            for k in ("w", "ix", "idx", "g", "p1", "a1", "p2", "a2", "d2", "p3", "a3", "y", "a4", "scat"):
                ov[l, k] = sem(f"over{l}_{k}")

        def bank(n):
            return banks[n % BANKS]

        def job(*name):
            return JOBS[name]

        def begin(eng, n, turn=0):
            if isinstance(turn, int):
                v = n // BANKS + 2 * turn
                if v > 0:
                    eng.wait_ge(free_s[n % BANKS], v)
            else:
                eng.wait_ge(free_s[n % BANKS], turn * 2 + n // BANKS)

        def done(eng, n, turn=0):
            eng.wait_ge(full_s[n % BANKS], turn * 2 + (n // BANKS + 1))

        def taken(eng, n, turn=0):
            eng.wait_ge(free_s[n % BANKS], turn * 2 + (n // BANKS + 1))

        def arrived(eng, n, turn=0):
            eng.wait_ge(arrived_s[n % RING], turn * 16 + 16 * (n // RING + 1))

        def unit(n):
            return ring[:, n % RING, :]

        def ada_name(a):
            return a // 6, a % 6

        ada_in_count = [0, 0]
        ada_in_value = []
        for a in range(12):
            ada_in_count[a % 2] += 16 * (4 if a % 6 in (1, 4) else 2)
            ada_in_value.append(ada_in_count[a % 2])
        stored_count = [0, 0]
        stored_value = []
        for a in range(12):
            if a % 6 >= 2:
                stored_count[a % 2] += 32
            stored_value.append(stored_count[a % 2])

        def last_reader(n):
            if n < U_WIN_E:
                return job("ada", 0, n // 4)
            if n < U_ADA0_B:
                m = n - U_WIN_E
                if m < 6:
                    ch = 2 * (m // 3) + 1
                    return job(("ab", "ac", "ax")[m % 3], ch)
                if m < 10:
                    return job("q" if m < 8 else "k", 2 * (m % 2) + 1)
                return job("v", 3)
            if n < U_WOUT_E:
                return job("ada", 0, 2 + (n - U_ADA0_B) // 4)
            if n < U_ADA1:
                return job("wo", 0, 3, 1)
            if n < U_MOE0:
                return job("ada", 1, (n - U_ADA1) // 4)
            if n < U_WIN_O:
                return moe_reader(0, n - U_MOE0)
            if n < U_WOUT_O:
                h, m = divmod(n - U_WIN_O, 6)
                return (job("rq", h), job("rk", h, 1), job("rv", h, 3), job("rv", h, 3),
                        job("rg", h, 1), job("rg", h, 1))[m]
            if n < U_MOE1:
                return job("wo", 1, 1, 1)
            return moe_reader(1, n - U_MOE1)

        def moe_reader(layer, m):
            e, part = divmod(m, 3)
            return job("moe", layer) + PER_EXPERT * e + (3 if part == 2 else 1)

        def room(eng, n):
            if n >= RING:
                done(eng, last_reader(n - RING))

        block = stack.enter_context(nc.Block())

        @block.sync
        def _(sp):
            sp.dma_start(crow[0:8, :], c.rearrange("a (k p) -> (a k) p", p=P)).then_inc(s_c, 16)
            sp.dma_start(crow[8:16, :], c_ctx.rearrange("(k p) -> k p", p=P)).then_inc(s_c, 16)
            sp.dma_start(con[:, :], shape_c).then_inc(s_con, 16)
            sp.dma_start(cwrow, conv_w[0].rearrange("w (k p) -> (w k) p", p=P)).then_inc(s_cw, 16)

            def ada_unit(layer, n, m):
                room(sp, n)
                sp.dma_start(unit(n).rearrange("p (k n) -> p k n", k=KC),
                             ada_w[layer, :, 256 * m:256 * m + 256].rearrange("(k p) n -> p k n", p=P)
                             ).then_inc(arrived_s[n % RING], 16)

            for m in range(8):
                ada_unit(0, U_ADA0_A + m, m)
                if m == 3:
                    sp.dma_start(res[:, 0:2, :], x[0].rearrange("(t p) d -> p t d", p=P)).then_inc(s_x, 16)
                    sp.dma_start(res[:, 2:4, :], ctx_in[0].rearrange("(t p) d -> p t d", p=P)).then_inc(s_x, 16)

            def columns(w, n, col):
                room(sp, n)
                sp.dma_start(unit(n).rearrange("p (k n) -> p k n", k=KC),
                             w[0, :, col:col + 256].rearrange("(k p) n -> p k n", p=P)
                             ).then_inc(arrived_s[n % RING], 16)

            def rows(w, n, row):
                room(sp, n)
                sp.dma_start(unit(n).rearrange("p (k n) -> p k n", k=2),
                             w[0, row:row + 256, :].rearrange("(k p) n -> p k n", p=P)
                             ).then_inc(arrived_s[n % RING], 16)

            for pair in range(2):
                for part in range(3):
                    columns(w_in_e, U_WIN_E + 3 * pair + part, 512 * part + 256 * pair)
            for m in range(6):
                columns(w_in_e, U_WIN_E + 6 + m, 1536 + 256 * m)
            for m in range(16):
                ada_unit(0, U_ADA0_B + m, 8 + m)
            for m in range(4):
                rows(w_out_e, U_WOUT_E + m, 256 * m)
            for m in range(24):
                ada_unit(1, U_ADA1 + m, m)

            def moe_stream(layer, u0):
                for m in range(24):
                    room(sp, u0 + m) if m < RING else done(sp, moe_reader(layer, m - RING))
                    e, part = divmod(m, 3)
                    load_part(layer, 0, e, part, u0 + m, 0)
                with sp.Fori(1, GROUPS) as g:
                    for m in range(24):
                        back = moe_reader(layer, m + 12) if m < 12 else moe_reader(layer, m - 12)
                        turn = (g - 1) * 2 if m < 12 else g * 2
                        done(sp, back, turn)
                        e, part = divmod(m, 3)
                        load_part(layer, g, e, part, u0 + m, g * 2)

            def load_part(layer, g, e, part, n, turn):
                u = unit(n)
                if part < 2:
                    w = (moe_w1, moe_w3)[part]
                    src = w[layer, bass.ds(g, 1), :, HIDDEN * e:HIDDEN * (e + 1)].rearrange(
                        "a (k p) n -> p (a k) n", p=P)
                    dst = u.rearrange("p (k n) -> p k n", k=KC)
                else:
                    src = moe_w2[layer, bass.ds(g, 1), HIDDEN * e:HIDDEN * (e + 1), :].rearrange(
                        "a (k p) n -> p (a k) n", p=P)
                    dst = u.rearrange("p (k n) -> p k n", k=2)
                sp.dma_start(dst, src).then_inc(arrived_s[n % RING], 16)

            def overflow(layer):
                sp.wait_ge(s_flag, layer + 1)
                count = sp.value_load(fullest[0:1, 0:1], min_val=0, max_val=4 * P)
                with sp.If(count > SLOTS):
                    done(sp, job("moe", layer) + EXPERTS * PER_EXPERT - 1)
                    with sp.Fori(0, TILES[layer] * P // SLOTS - 1) as b:
                        with sp.Fori(0, GROUPS) as g:
                            with sp.Fori(0, PER_GROUP) as e:
                                sp.wait_ge(ov[layer, "y"], b * EXPERTS + g * PER_GROUP + e + 1)
                                for w, place in ((moe_w1, 0), (moe_w3, 1)):
                                    sp.dma_start(
                                        unit(place).rearrange("p (k n) -> p k n", k=KC),
                                        w[layer, bass.ds(g, 1), :, bass.ds(e * HIDDEN, HIDDEN)].rearrange(
                                            "a (k p) n -> p (a k) n", p=P)).then_inc(ov[layer, "w"], 16)
                                sp.dma_start(
                                    unit(2).rearrange("p (k n) -> p k n", k=2),
                                    moe_w2[layer, bass.ds(g, 1), bass.ds(e * HIDDEN, HIDDEN), :].rearrange(
                                        "a (k p) n -> p (a k) n", p=P)).then_inc(ov[layer, "w"], 16)
                    sp.wait_ge(ov[layer, "y"], (TILES[layer] * P // SLOTS - 1) * EXPERTS + 1)

            moe_stream(0, U_MOE0)
            overflow(0)
            for h in range(R_HEADS):
                n = U_WIN_O + 6 * h
                columns(w_in_o, n, R_QK * h)
                columns(w_in_o, n + 1, D + R_QK * h)
                for m in range(2):
                    columns(w_in_o, n + 2 + m, 2 * D + R_V * h + 256 * m)
                for m in range(2):
                    columns(w_in_o, n + 4 + m, 2 * D + R_HEADS * R_V + R_V * h + 256 * m)
            for m in range(8):
                rows(w_out_o, U_WOUT_O + m, 256 * m)
            moe_stream(1, U_MOE1)
            overflow(1)
            for t in range(2):
                sp.wait_ge(s_fin, t + 1)
                sp.dma_start(out[0, t * P:(t + 1) * P, :], A(A_XG + t * D, D)).then_inc(s_out, 16)
            sp.wait_ge(s_out, 32)

        @block.gpsimd
        def _(pool):
            steps = [0]

            def step(ins):
                steps[0] += 1
                ins.then_inc(s_pool, 1)
                pool.wait_ge(s_pool, steps[0])

            pool.memset(ada_rows[:, :, :, :], 0.0).then_inc(s_zero, 1)
            pool.memset(cvec[:, :, :], 0.0).then_inc(s_zero, 1)
            pool.wait_ge(s_zero, 2)

            def load_ada_rows(a):
                layer, q = ada_name(a)
                for s in range(2):
                    pool.dma_start(ada_rows[s:P:32, a % 2, 0, :],
                                   ada_b[layer, q * D:(q + 1) * D].rearrange("(j n) -> j n", n=256)
                                   ).then_inc(s_ada_in[a % 2], 16)
                    if q in (1, 4):
                        g = (norm1_g if q == 1 else norm2_g)[layer]
                        pool.dma_start(ada_rows[s:P:32, a % 2, 1, :], g.rearrange("(j n) -> j n", n=256)
                                       ).then_inc(s_ada_in[a % 2], 16)

            def store_mod_rows(a):
                taken(pool, job("ada", *ada_name(a)))
                if a % 6 >= 2:
                    for s in range(2):
                        pool.dma_start(mod_rows_d[a, s].rearrange("(j n) -> j n", n=256),
                                       mod_rows[s:P:32, a % 2, :]).then_inc(s_stored[a % 2], 16)

            def broadcast(to, a, landed):
                pool.wait_ge(s_stored[a % 2], stored_value[a])
                src = bass.AP(mod_rows_d.tensor, a * 2 * D, [[0, P], [1, 2 * D]])
                pool.dma_start(to, src).then_inc(landed, 16)

            load_ada_rows(0)
            load_ada_rows(1)
            for a in range(6):
                store_mod_rows(a)
                if a + 2 < 6:
                    load_ada_rows(a + 2)
            gate_rows = bc_gate[:, :, :].rearrange("p s d -> p (s d)")
            broadcast(gate_rows, 2, s_gate)

            def router_weights(layer):
                pool.dma_start(rw[:, :, 0:GROUPS], router_gw[layer].rearrange("(k p) n -> p k n", p=P)
                               ).then_inc(s_rw, 16)
                pool.dma_start(rw[:, :, GROUPS:36], router_ew[layer].rearrange("(k p) n -> p k n", p=P)
                               ).then_inc(s_rw, 16)
                pool.dma_start(rb[:, 0:GROUPS], bass.AP(router_gb.tensor, layer * GROUPS, [[0, P], [1, GROUPS]])
                               ).then_inc(s_rw, 16)
                pool.dma_start(rb[:, GROUPS:36], bass.AP(router_eb.tensor, layer * EXPERTS, [[0, P], [1, EXPERTS]])
                               ).then_inc(s_rw, 16)

            step(pool.memset(table[:, :], 2 * TILES[0] * P))
            for layer in range(2):
                for m in range(TILES[layer]):
                    pool.dma_start(table_d[layer][m * P * EXPERTS:(m + 1) * P * EXPERTS, :].rearrange(
                        "(p n) a -> p (n a)", p=P), table[:, :]).then_inc(s_table_clear, 16)
            router_weights(0)
            for u in range(EPI):
                pool.dma_start(ids[:, 2 * u:2 * u + 2], ids_c[:, 2 * u:2 * u + 2]).then_inc(s_scat[u], 16)

            def scale_and_shift(layer):
                if layer == 0:
                    taken(pool, job("s", 4 * HEADS - 1))
                else:
                    done(pool, job("ryT", R_HEADS - 1, 1))
                broadcast(A(A_BCA, 2 * D), 6 * layer + 4, s_ab)
                broadcast(A(A_BCB, 2 * D), 6 * layer + 3, s_ab)

            def second_gate(layer):
                pool.wait_ge(s_mixed, 4 if layer == 0 else 6)
                broadcast(gate_rows, 6 * layer + 5, s_gate)

            def route(layer):
                nt = TILES[layer]
                for t in range(nt):
                    pool.wait_ge(s_h2, (0 if layer == 0 else 4) + t + 1)
                    pool.dma_start(h2_d[layer][t * P:(t + 1) * P, :], A(A_H2 + t * D, D)).then_inc(s_h2_out, 16)
                pool.wait_ge(s_addr, layer + 1)
                pool.wait_ge(s_table_clear, 16 * sum(TILES))
                for u in range(EPI):
                    pool.wait_ge(s_scat[u], 16)
                for t in range(nt):
                    for k in range(2):
                        pool.indirect_dma_start(table_d[layer], bass.IndirectOffsetOnAxis(addr[:, k, t:t + 1], 0),
                                                ids[:, 2 * t + k:2 * t + k + 1], None,
                                                bounds_check=nt * P * EXPERTS - 1, oob_is_err=False
                                                ).then_inc(s_table_set, 16)
                pool.wait_ge(s_table_set, 128 if layer == 0 else 192)
                for half in range(2):
                    pool.dma_start(table[half * SLOTS:(half + 1) * SLOTS, :],
                                   table_d[layer][0:SLOTS * EXPERTS, :].rearrange("(r e) a -> r (e a)", e=EXPERTS)
                                   ).then_inc(s_table_in, 16)
                pool.wait_ge(s_h2_out, 64 if layer == 0 else 96)
                pool.wait_ge(s_idx, layer + 1)

            def experts(layer):
                nt = TILES[layer]
                n0 = job("moe", layer)
                rows_out = nt * P * 4
                done(pool, job("rT", layer, nt - 1, 1))

                def gather(expert, u, copies):
                    pool.tensor_copy(gnow[:, u:u + 1], gidx[:, bass.ds(expert, 1)]).then_inc(s_now, 1)
                    pool.wait_ge(s_now, copies)
                    pool.sem_inc(s_pool_seen, 1)
                    pool.indirect_dma_start(
                        A(A_XG + u * D, D)[0:SLOTS, :], None, h2_d[layer],
                        bass.IndirectOffsetOnAxis(gnow[:, u:u + 1], 0),
                        bounds_check=nt * P - 1, oob_is_err=False).then_inc(s_gath[u], 16)

                def scatter(expert, u, turn, copies):
                    taken(pool, n0 + PER_EXPERT * u + 3, turn)
                    pool.tensor_copy(snow[:, u:u + 1], sidx[:, bass.ds(expert, 1)]).then_inc(s_now, 1)
                    pool.wait_ge(s_now, copies)
                    pool.sem_inc(s_pool_seen, 1)
                    pool.indirect_dma_start(
                        y_d[layer], bass.IndirectOffsetOnAxis(snow[:, u:u + 1], 0),
                        A(A_YS + u * 512, 512), None,
                        bounds_check=rows_out - 1, oob_is_err=False).then_inc(s_scat[u], 16)

                base = layer * 2 * EXPERTS
                for u in range(EPI):
                    gather(u, u, base + u + 1)
                base += EPI
                with pool.Fori(0, TURNS - 1) as it:
                    for u in range(EPI):
                        scatter(it * EPI + u, u, it, it * 2 * EPI + (base + 2 * u + 1))
                        gather(it * EPI + (EPI + u), u, it * 2 * EPI + (base + 2 * u + 2))
                base += (TURNS - 1) * 2 * EPI
                for u in range(EPI):
                    scatter(EXPERTS - EPI + u, u, TURNS - 1, base + u + 1)
                for u in range(EPI):
                    pool.wait_ge(s_scat[u], 16 * (TURNS * (layer + 1) + 1))

            def overflow(layer):
                nt = TILES[layer]
                pool.wait_ge(s_flag, layer + 1)
                count = pool.value_load(fullest[0:1, 0:1], min_val=0, max_val=4 * P)
                passes = nt * P // SLOTS - 1
                with pool.If(count > SLOTS):
                    with pool.Fori(0, passes) as b:
                        with pool.Fori(0, EXPERTS) as e:
                            n = b * EXPERTS + e
                            for half in range(2):
                                pool.dma_start(
                                    ov_table[half * SLOTS:(half + 1) * SLOTS, :],
                                    table_d[layer].rearrange("(r e) a -> r (e a)", e=EXPERTS)[
                                        bass.ds(b * SLOTS + SLOTS, SLOTS), bass.ds(e, 1)],
                                    allow_slow_non_contiguous=True).then_inc(ov[layer, "ix"], 16)
                            pool.wait_ge(ov[layer, "idx"], n + 1)
                            pool.sem_inc(s_pool_seen, 1)
                            pool.indirect_dma_start(A(A_XG, D)[0:SLOTS, :], None, h2_d[layer],
                                                    bass.IndirectOffsetOnAxis(ov_idx[0:SLOTS, 0:1], 0),
                                                    bounds_check=nt * P - 1, oob_is_err=False
                                                    ).then_inc(ov[layer, "g"], 16)
                            pool.wait_ge(ov[layer, "a4"], n + 1)
                            pool.sem_inc(s_pool_seen, 1)
                            pool.indirect_dma_start(y_d[layer], bass.IndirectOffsetOnAxis(ov_idx[:, 1:2], 0),
                                                    A(A_YS, 512), None,
                                                    bounds_check=nt * P * 4 - 1, oob_is_err=False
                                                    ).then_inc(ov[layer, "scat"], 16)
                            pool.wait_ge(ov[layer, "scat"], n * 16 + 16)
                            pool.sem_inc(s_pool_seen, 1)

            def load_results(layer):
                nt = TILES[layer]
                for t in range(nt):
                    tt = t if layer == 0 else 4 + t
                    if tt >= 2:
                        pool.wait_ge(s_comb, tt - 1)
                    pool.dma_start(A(A_XG + (t % 2) * 2 * D, 2 * D),
                                   y_d[layer][t * P * 4:(t + 1) * P * 4, :].rearrange("(p a) n -> p (a n)", a=4)
                                   ).then_inc(s_y_in[t % 2], 16)

            scale_and_shift(0)
            load_ada_rows(6)
            load_ada_rows(7)
            for a in range(6, 12):
                store_mod_rows(a)
                if a + 2 < 12:
                    load_ada_rows(a + 2)
                if a == 6:
                    second_gate(0)
            route(0)
            experts(0)
            overflow(0)
            load_results(0)
            for i, d in enumerate((decay_f, decay_b)):
                pool.dma_start(dec[:, 4 * i:4 * i + 4], bass.AP(d.tensor, 0, [[0, P], [1, R_HEADS]])
                               ).then_inc(s_dec_in, 16)
            pool.wait_ge(s_comb, 4)
            pool.dma_start(A(A_RTAB, RET_N), ret_c).then_inc(s_ret_in, 16)
            broadcast(gate_rows, 8, s_gate)
            router_weights(1)
            scale_and_shift(1)
            second_gate(1)
            route(1)
            experts(1)
            overflow(1)
            load_results(1)
            pool.wait_ge(s_comb, 6)
            pool.dma_start(A(A_BCA, D), bass.AP(final_g.tensor, 0, [[0, P], [1, D]])).then_inc(s_fin_g, 16)

        @block.scalar
        def _(act):
            for r in range(ROWS):
                for i in range(ROWS):
                    src = bass.AP(rpb_rev.tensor, (i - r + 7) * 31 - 48, [[1, GRID_W], [15 * 31, HEADS], [1, GRID_W]])
                    dst = A(A_Q + (r // 2) * 2048, HEADS, ROWS, GRID_W)[
                        GRID_W * (r % 2):GRID_W * (r % 2) + GRID_W, :, i, :]
                    act.dma_start(dst, src).then_inc(s_bias, 16)

            act.wait_ge(s_c, 32)
            act.activation(csil, crow, ACT.Silu).then_inc(s_csil, 1)

            ms_count = [0]
            root_count = [0]

            def mean_squares(tiles, wait=None):
                for t in tiles:
                    if wait:
                        wait(t)
                    act.activation(hT[:, 4:6, :].rearrange("p a b -> p (a b)"), res[:, t, :], ACT.Square,
                                   accum_out=stat[:, 0, t:t + 1]).then_inc(s_ms, 1)
                    ms_count[0] += 1
                    act.wait_ge(s_ms, ms_count[0])

            def roots(a, b, value):
                act.wait_ge(s_rstd, value)
                act.activation(stat[:, 1, a:b], stat[:, 0, a:b], ACT.Sqrt).then_inc(s_root, 1)

            act.wait_ge(s_x, 32)
            mean_squares(range(4))
            roots(0, 4, 1)

            def turn_rows(layer):
                for t in (range(4)):
                    n = job("hT", layer, t, 0)
                    taken(act, job("modT", layer, 1))
                    done(act, n)
                    s = t // 2
                    for k in range(4):
                        ins = act.activation(hT[:, k, t * P:(t + 1) * P], bank(n)[:, k * P:(k + 1) * P], ACT.Identity,
                                             bias=modT[:, layer, 0, k, s:s + 1], scale=modT[:, layer, 1, k, s:s + 1])
                    ins.then_inc(free_s[n % BANKS], 1)

            turn_rows(0)
            for ch in range(4):
                n = job("ac", ch)
                done(act, n)
                if ch:
                    taken(act, job("ax", ch - 1))
                act.activation(A(A_CONV, 512), bank(n)[:, :], ACT.Copy).then_inc(free_s[n % BANKS], 1)
            act.wait_ge(s_bias_ready, 1)
            for ch in range(4):
                n = job("q", ch)
                done(act, n)
                act.activation(A(A_Q, 4, 512)[:, ch, :], bank(n)[:, :], ACT.Copy).then_inc(free_s[n % BANKS], 1)
            for ch in range(4):
                n = job("k", ch)
                done(act, n)
                act.activation(A(A_K, 4, 512)[:, ch, :], bank(n)[:, :], ACT.Copy).then_inc(free_s[n % BANKS], 1)
            for t in range(4):
                n = job("v", t)
                done(act, n)
                act.activation(A(A_V, 4, 512)[:, t, :], bank(n)[:, :], ACT.Copy).then_inc(free_s[n % BANKS], 1)

            def turned(i):
                n = job("pt", i)
                h, qt = divmod(i, 4)
                keys = 4 if qt < 2 else 2
                done(act, n)
                act.activation(A(A_PT + (i // 2 % 2) * 1024, 4, SEQ)[:, 0:keys, (qt % 2) * P:(qt % 2 + 1) * P],
                               bank(n)[:, 0:keys * P].rearrange("p (k q) -> p k q", q=P), ACT.Copy
                               ).then_inc(free_s[n % BANKS], 1)

            for i in range(4 * HEADS):
                qt = i % 4
                w = 512 if qt < 2 else 256
                p = A(A_P, 2, 512)[:, i % 2, 0:w]
                act.wait_ge(s_max, i + 1)
                act.activation(p, p, ACT.Exp, bias=soft[:, 4 * (i % 3):4 * (i % 3) + 1],
                               accum_out=soft[:, 4 * (i % 3) + 1:4 * (i % 3) + 2]).then_inc(s_exp, 1)
                if i:
                    turned(i - 1)
            turned(4 * HEADS - 1)

            def expert_rows_turned(layer):
                nt = TILES[layer]
                base = 0 if layer == 0 else 4
                mean_squares(range(nt), wait=lambda t: act.wait_ge(s_mixed, base + t + 1))
                roots(0, nt, 2 if layer == 0 else 4)
                for t in range(nt):
                    n = job("rT", layer, t, 0)
                    done(act, n)
                    act.activation(hT[:, 0:4, t * P:(t + 1) * P],
                                   bank(n)[:, :].rearrange("p (k q) -> p k q", q=P), ACT.Copy
                                   ).then_inc(free_s[n % BANKS], 1)
                for k in range(2):
                    act.wait_ge(s_gap, 2 * layer + k + 1)
                    src, dst = ((A_ROUTE + 1408, A_ROUTE + 1424), (A_ROUTE + 1500, A_ROUTE + 1504))[k]
                    w = (nt * GROUPS, nt)[k]
                    act.activation(A(dst, w), A(src, w), ACT.Exp).then_inc(s_rexp, 1)

            def experts(layer):
                n0 = job("moe", layer)
                with act.Fori(0, TURNS) as it:
                    for u in range(EPI):
                        n = n0 + PER_EXPERT * u
                        b = u % 2
                        done(act, n, it)
                        act.activation(A(A_XGT + b * 512, 512), bank(n)[:, :], ACT.Copy).then_inc(free_s[n % BANKS], 1)
                        done(act, n + 1, it)
                        act.activation(A(A_SL + b * 256, 256)[0:SLOTS, :], bank(n + 1)[0:SLOTS, 0:HIDDEN], ACT.Silu
                                       ).then_inc(s_silu, 1)
                        done(act, n + 2, it)
                        act.activation(A(A_HIDT + b * 128, 128), bank(n + 2)[:, 0:2 * SLOTS], ACT.Copy
                                       ).then_inc(free_s[(n + 2) % BANKS], 1)

            def overflow(layer):
                act.wait_ge(s_flag, layer + 1)
                count = act.value_load(fullest[0:1, 0:1], min_val=0, max_val=4 * P)
                o = lambda k: ov[layer, k]
                with act.If(count > SLOTS):
                    for u in range(EPI):
                        act.wait_ge(s_scat[u], 16 * (TURNS * (layer + 1) + 1))
                    with act.Fori(0, (TILES[layer] * P // SLOTS - 1) * EXPERTS) as n:
                        act.wait_ge(o("p1"), n + 1)
                        act.activation(A(A_XGT, 512), banks[0][:, :], ACT.Copy).then_inc(o("a1"), 1)
                        act.wait_ge(o("p2"), n + 1)
                        act.activation(A(A_SL, 256)[0:SLOTS, :], banks[1][0:SLOTS, 0:HIDDEN], ACT.Silu
                                       ).then_inc(o("a2"), 1)
                        act.wait_ge(o("p3"), n + 1)
                        act.activation(A(A_HIDT, 128), banks[2][:, 0:2 * SLOTS], ACT.Copy).then_inc(o("a3"), 1)
                        act.wait_ge(o("y"), n + 2)
                        act.activation(A(A_YS, 512), banks[3][:, :], ACT.Copy).then_inc(o("a4"), 1)

            expert_rows_turned(0)
            experts(0)
            overflow(0)

            mean_squares(range(4), wait=lambda t: act.wait_ge(s_comb, t + 1))
            roots(0, 4, 3)
            act.wait_ge(s_dec_in, 32)
            act.activation(dec[:, 8:16], dec[:, 0:8], ACT.Exp).then_inc(s_dec, 1)
            act.wait_ge(s_dec, 2)
            act.activation(dec[:, 24:32], dec[:, 16:24], ACT.Ln).then_inc(s_dec, 1)
            turn_rows(1)

            acts = [0]

            def mark(ins):
                acts[0] += 1
                ins.then_inc(s_rexps, 1)

            tab = lambda k: A(A_RTAB + 512 * k, 512)
            for h in range(R_HEADS):
                for ch in range(2):
                    n = job("rk", h, ch)
                    done(act, n)
                    act.activation(A(A_RK, 2, 512)[:, ch, SEQ:512], bank(n)[:, SEQ:512], ACT.Copy).then_inc(s_ctx_keys, 1)
                if h == 0:
                    act.wait_ge(s_ret_in, 16)
                    act.wait_ge(s_dec, 6)
                else:
                    done(act, job("ro", h - 1, 1))
                    act.wait_ge(s_yms, 2 * h)
                mark(act.activation(A(A_RD, 512), tab(1), ACT.Exp, scale=dec[:, 24 + h:25 + h]))
                mark(act.activation(A(A_EXP, 512), tab(2), ACT.Exp, scale=dec[:, 28 + h:29 + h]))
                act.wait_ge(s_factors, 2 * h + 1)
                mark(act.activation(A(A_RD + 512, 512), tab(0), ACT.Exp, scale=dec[:, 24 + h:25 + h],
                                    bias=dec[:, 32 + h:33 + h]))
                mark(act.activation(A(A_EXP, 512), tab(0), ACT.Exp, scale=dec[:, h:h + 1],
                                    bias=dec[:, 36 + h:37 + h]))
                for t in range(4):
                    n = job("rv", h, t)
                    done(act, n)
                    act.activation(A(A_RV, 4, 512)[:, t, :], bank(n)[:, :], ACT.Copy).then_inc(free_s[n % BANKS], 1)
                for t in range(2):
                    n = job("rg", h, t)
                    done(act, n)
                    act.activation(A(A_RG, 2, 512)[:, t, :], bank(n)[:, :], ACT.Silu).then_inc(free_s[n % BANKS], 1)
                for t in range(2):
                    i = 2 * h + t
                    n = job("ro", h, t)
                    done(act, n)
                    if t:
                        act.wait_ge(s_yms, i)
                    act.activation(A(A_EXP, 512), bank(n)[:, :], ACT.Square, accum_out=soft[:, t:t + 1]).then_inc(s_yms, 1)
                    act.wait_ge(s_yroot, 2 * i + 1)
                    act.activation(soft[:, 4 + t:5 + t], soft[:, 2 + t:3 + t], ACT.Sqrt).then_inc(s_yroot, 1)
                for t in range(2):
                    n = job("ryT", h, t)
                    done(act, n)
                    act.activation(A(A_RY, 16, SEQ)[:, 4 * h:4 * h + 4, t * P:(t + 1) * P],
                                   bank(n)[:, :].rearrange("p (k q) -> p k q", q=P), ACT.Copy
                                   ).then_inc(free_s[n % BANKS], 1)
            expert_rows_turned(1)
            experts(1)
            overflow(1)
            mean_squares(range(2), wait=lambda t: act.wait_ge(s_comb, 4 + t + 1))
            roots(0, 2, 5)

        @block.tensor
        def _(pe):
            def product(n, where, pairs, start=True, last=True, mark=True):
                for i, (stationary, moving) in enumerate(pairs):
                    ins = pe.matmul(where, stationary, moving, start=(start and i == 0), stop=(last and i == len(pairs) - 1))
                if mark:
                    ins.then_inc(full_s[n % BANKS], 1)

            def turn(n, to, what, size, mark):
                ins = pe.transpose(to, what, ident[0:size, 0:size])
                if mark:
                    ins.then_inc(full_s[n % BANKS], 1)

            pe.wait_ge(s_con, 16)
            pe.wait_ge(s_csil, 1)
            n = job("cT")
            turn(n, bank(n)[:, 0:16], csil, 16, True)
            n = job("cwT")
            pe.wait_ge(s_cw, 16)
            turn(n, bank(n)[:, 0:12], cwrow, 12, True)

            def ada(layer, q, u0):
                n = job("ada", layer, q)
                begin(pe, n)
                for j in range(4):
                    arrived(pe, u0 + j)
                for k in range(KC):
                    for j in range(4):
                        ins = pe.matmul(bank(n)[32 * j:32 * j + 32, 0:256], cvec[:, k, :],
                                        unit(u0 + j)[:, 256 * k:256 * k + 256], start=(k == 0), stop=(k == KC - 1))
                ins.then_inc(full_s[n % BANKS], 1)

            def mod_turn(layer, q):
                a = 6 * layer + q
                n = job("modT", layer, q)
                begin(pe, n)
                taken(pe, job("ada", layer, q))
                for half in range(2):
                    turn(n, bank(n)[:, half * P:(half + 1) * P], mod_rows[:, a % 2, half * P:(half + 1) * P], P, half == 1)

            taken(pe, job("cT"))
            for q in range(2):
                ada(0, q, U_ADA0_A + 4 * q)
            for q in range(2):
                mod_turn(0, q)

            def turn_rows(layer):
                for t in range(4):
                    pe.wait_ge(s_xn, 4 * layer + t + 1)
                    for half in range(2):
                        n = job("hT", layer, t, half)
                        begin(pe, n)
                        xn = A((A_XN, A_XN1)[layer] + (t % 2) * D, D)
                        for k in range(4):
                            turn(n, bank(n)[:, k * P:(k + 1) * P], xn[:, (4 * half + k) * P:(4 * half + k + 1) * P], P, k == 3)

            def rows_ready(layer):
                for t in range(4):
                    for half in range(2):
                        taken(pe, job("hT", layer, t, half))

            turn_rows(0)
            rows_ready(0)

            def w_cols(n, k, c0, w):
                return unit(n)[:, 256 * k + c0:256 * k + c0 + w]

            for ch in range(4):
                u0 = U_WIN_E + 3 * (ch // 2)
                for name, m in (("ac", 1), ("ax", 2), ("ab", 0)):
                    n = job(name, ch)
                    begin(pe, n)
                    arrived(pe, u0 + m)
                    product(n, bank(n)[:, :], [(w_cols(u0 + m, k, P * (ch % 2), P), hT[:, k, :]) for k in range(KC)])
            for name, u0 in (("q", U_WIN_E + 6), ("k", U_WIN_E + 8)):
                for ch in range(4):
                    n = job(name, ch)
                    begin(pe, n)
                    arrived(pe, u0 + ch // 2)
                    product(n, bank(n)[:, :], [(w_cols(u0 + ch // 2, k, P * (ch % 2), P), hT[:, k, :]) for k in range(KC)])

            def two_units(u0, k):
                a = u0 % RING
                return ring[:, a:a + 2, 256 * k:256 * k + 256]

            for t in range(4):
                n = job("v", t)
                begin(pe, n)
                for m in range(2):
                    arrived(pe, U_WIN_E + 10 + m)
                product(n, bank(n)[:, :], [(hT[:, k, t * P:(t + 1) * P], two_units(U_WIN_E + 10, k)) for k in range(KC)])
            for q in range(2, 6):
                ada(0, q, U_ADA0_B + 4 * (q - 2))

            def scores(i):
                h, qt = divmod(i, 4)
                b = HEAD_DIM * (h % 2)
                n = job("s", i)
                begin(pe, n)
                k0 = 0 if qt < 2 else SEQ
                product(n, bank(n)[:, 0:512 - k0],
                        [(A(A_Q, 4, 512)[b:b + HEAD_DIM, h // 2, qt * P:(qt + 1) * P],
                          A(A_K, 4, 512)[b:b + HEAD_DIM, h // 2, k0:512])])

            def turn_probs(i):
                n = job("pt", i)
                begin(pe, n)
                pe.wait_ge(s_probs, i + 1)
                keys = 4 if i % 4 < 2 else 2
                for k in range(keys):
                    turn(n, bank(n)[:, k * P:(k + 1) * P], A(A_P, 2, 512)[:, i % 2, k * P:(k + 1) * P], P, k == keys - 1)

            def mix_values(j):
                h, s = divmod(j, 2)
                n = job("pv", j)
                begin(pe, n)
                taken(pe, job("pt", 2 * j))
                taken(pe, job("pt", 2 * j + 1))
                b = HEAD_DIM * (h % 2)
                kts = range(4) if s == 0 else range(2, 4)
                product(n, bank(n)[b:b + HEAD_DIM, 0:SEQ],
                        [(A(A_V, 4, 512)[:, kt, h * HEAD_DIM:(h + 1) * HEAD_DIM],
                          A(A_PT + (j % 2) * 1024, 4, SEQ)[:, kt - kts[0], :]) for kt in kts])

            for ch in range(4):
                taken(pe, job("q", ch))
                taken(pe, job("k", ch))
                taken(pe, job("v", ch))
            scores(0)
            scores(1)
            items = 4 * HEADS
            for i in range(items):
                if i + 2 < items:
                    scores(i + 2)
                turn_probs(i)
                if i % 2 == 0 and i:
                    mix_values(i // 2 - 1)
            mix_values(items // 2 - 1)

            def mixed(k):
                return A(A_YC, 4, 512)[:, k, :] if k < 4 else hT[:, k - 4, :]

            def project_out(layer, u0, chunks, source):
                for m in range(chunks // 2):
                    arrived(pe, u0 + m)
                for t in range(4 if layer == 0 else 2):
                    for half in range(2):
                        n = job("wo", layer, t, half)
                        begin(pe, n)
                        product(n, bank(n)[:, :],
                                [(source(k)[:, t * P:(t + 1) * P],
                                  unit(u0 + k // 2)[:, D * (k % 2) + 512 * half:D * (k % 2) + 512 * half + 512])
                                 for k in range(chunks)])

            for ch in range(4):
                taken(pe, job("ab", ch))
            for j in range(2 * HEADS):
                taken(pe, job("pv", j))
            project_out(0, U_WOUT_E, 8, mixed)
            for q in range(2):
                ada(1, q, U_ADA1 + 4 * q)
            for q in range(2):
                mod_turn(1, q)
            for q in range(2, 6):
                ada(1, q, U_ADA1 + 4 * q)

            def route(layer):
                nt = TILES[layer]
                for t in range(nt):
                    pe.wait_ge(s_h2, (0 if layer == 0 else 4) + t + 1)
                    for half in range(2):
                        n = job("rT", layer, t, half)
                        begin(pe, n)
                        for k in range(4):
                            at = (4 * half + k) * P
                            turn(n, bank(n)[:, k * P:(k + 1) * P], A(A_H2 + t * D, D)[:, at:at + P], P, k == 3)
                n = job("logits", layer)
                begin(pe, n)
                pe.wait_ge(s_rw, 64 * (layer + 1))
                for t in range(nt):
                    for half in range(2):
                        taken(pe, job("rT", layer, t, half))
                for t in range(nt):
                    product(n, bank(n)[:, 64 * t:64 * t + 36],
                            [(hT[:, k, t * P:(t + 1) * P], rw[:, k, :]) for k in range(KC)], mark=(t == nt - 1))
                n = job("ranks", layer)
                begin(pe, n)
                pe.wait_ge(s_members, layer + 1)
                member = lambda t: A(A_ROUTE + 640, 4, EXPERTS)[:, t, :]
                for t in range(nt):
                    product(n, bank(n)[:, 32 * t:32 * t + 32],
                            [(const("ones"), member(m)) for m in range(t)] + [(const("upper"), member(t))], mark=False)
                product(n, bank(n)[:, 128:160], [(const("ones"), member(t)) for t in range(nt)])

            def experts(layer):
                n0 = job("moe", layer)
                u0 = (U_MOE0, U_MOE1)[layer]
                with pe.Fori(0, TURNS) as it:
                    for u in range(EPI):
                        n = n0 + PER_EXPERT * u
                        b = u % 2
                        begin(pe, n, it)
                        pe.wait_ge(s_gath[u], it * 16 + 16 * (TURNS * layer + 1))
                        pe.sem_inc(s_pe_seen, 1)
                        for k in range(KC):
                            turn(n, bank(n)[:, SLOTS * k:SLOTS * (k + 1)],
                                 A(A_XG + u * D, D)[0:SLOTS, k * P:(k + 1) * P], SLOTS, k == KC - 1)
                        begin(pe, n + 1, it)
                        arrived(pe, u0 + 3 * u, it)
                        arrived(pe, u0 + 3 * u + 1, it)
                        taken(pe, n, it)
                        for k in range(KC):
                            for w in range(2):
                                ins = pe.matmul(bank(n + 1)[SLOTS * w:SLOTS * (w + 1), 0:HIDDEN],
                                                A(A_XGT + b * 512 + SLOTS * k, SLOTS),
                                                unit(u0 + 3 * u + w)[:, 256 * k:256 * (k + 1)],
                                                start=(k == 0), stop=(k == KC - 1))
                        ins.then_inc(full_s[(n + 1) % BANKS], 1)
                        begin(pe, n + 2, it)
                        taken(pe, n + 1, it)
                        pe.sem_inc(s_pe_seen, 1)
                        for k in range(2):
                            turn(n + 2, bank(n + 2)[:, SLOTS * k:SLOTS * (k + 1)],
                                 A(A_HID + b * 256, 256)[0:SLOTS, k * P:(k + 1) * P], SLOTS, k == 1)
                        begin(pe, n + 3, it)
                        arrived(pe, u0 + 3 * u + 2, it)
                        taken(pe, n + 2, it)
                        for k in range(2):
                            for w in range(2):
                                ins = pe.matmul(bank(n + 3)[SLOTS * w:SLOTS * (w + 1), :],
                                                A(A_HIDT + b * 128 + SLOTS * k, SLOTS),
                                                unit(u0 + 3 * u + 2)[:, D * k + 512 * w:D * k + 512 * (w + 1)],
                                                start=(k == 0), stop=(k == 1))
                        ins.then_inc(full_s[(n + 3) % BANKS], 1)

            def overflow(layer):
                n0 = job("moe", layer)
                pe.wait_ge(s_flag, layer + 1)
                count = pe.value_load(fullest[0:1, 0:1], min_val=0, max_val=4 * P)
                o = lambda k: ov[layer, k]
                total = (TILES[layer] * P // SLOTS - 1) * EXPERTS
                with pe.If(count > SLOTS):
                    for b in range(BANKS):
                        taken(pe, n0 + EXPERTS * PER_EXPERT - BANKS + b)
                    pe.nop().then_inc(o("y"), 1)
                    with pe.Fori(0, total) as n:
                        pe.wait_ge(o("g"), n * 16 + 16)
                        pe.sem_inc(s_pe_seen, 1)
                        for k in range(KC):
                            ins = pe.transpose(banks[0][:, SLOTS * k:SLOTS * (k + 1)],
                                               A(A_XG, D)[0:SLOTS, k * P:(k + 1) * P], ident[0:SLOTS, 0:SLOTS])
                        ins.then_inc(o("p1"), 1)
                        pe.wait_ge(o("w"), n * 48 + 48)
                        pe.wait_ge(o("a1"), n + 1)
                        for k in range(KC):
                            for w in range(2):
                                ins = pe.matmul(banks[1][SLOTS * w:SLOTS * (w + 1), 0:HIDDEN],
                                                A(A_XGT + SLOTS * k, SLOTS), unit(w)[:, 256 * k:256 * (k + 1)],
                                                start=(k == 0), stop=(k == KC - 1))
                        ins.then_inc(o("p2"), 1)
                        pe.wait_ge(o("d2"), n + 1)
                        pe.sem_inc(s_pe_seen, 1)
                        for k in range(2):
                            ins = pe.transpose(banks[2][:, SLOTS * k:SLOTS * (k + 1)],
                                               A(A_HID, 256)[0:SLOTS, k * P:(k + 1) * P], ident[0:SLOTS, 0:SLOTS])
                        ins.then_inc(o("p3"), 1)
                        pe.wait_ge(o("a3"), n + 1)
                        for k in range(2):
                            for w in range(2):
                                ins = pe.matmul(banks[3][SLOTS * w:SLOTS * (w + 1), :], A(A_HIDT + SLOTS * k, SLOTS),
                                                unit(2)[:, D * k + 512 * w:D * k + 512 * (w + 1)],
                                                start=(k == 0), stop=(k == 1))
                        ins.then_inc(o("y"), 1)
                        pe.wait_ge(o("a4"), n + 1)

            route(0)
            experts(0)
            overflow(0)
            turn_rows(1)
            rows_ready(1)

            for h in range(R_HEADS):
                u0 = U_WIN_O + 6 * h
                n = job("rq", h)
                begin(pe, n)
                arrived(pe, u0)
                for ch in range(2):
                    product(n, bank(n)[:, SEQ * ch:SEQ * (ch + 1)],
                            [(w_cols(u0, k, P * ch, P), hT[:, k, 0:SEQ]) for k in range(KC)], mark=(ch == 1))
                arrived(pe, u0 + 1)
                for ch in range(2):
                    n = job("rk", h, ch)
                    begin(pe, n)
                    product(n, bank(n)[:, :], [(w_cols(u0 + 1, k, P * ch, P), hT[:, k, :]) for k in range(KC)])
                for m in range(2):
                    arrived(pe, u0 + 2 + m)
                for t in range(4):
                    n = job("rv", h, t)
                    begin(pe, n)
                    product(n, bank(n)[:, :], [(hT[:, k, t * P:(t + 1) * P], two_units(u0 + 2, k)) for k in range(KC)])
                taken(pe, job("rq", h))
                for ch in range(2):
                    taken(pe, job("rk", h, ch))
                pe.wait_ge(s_ctx_keys, 2 * (h + 1))
                for a in range(2):
                    n = job("rs", h, a)
                    begin(pe, n)
                    for b in range(2):
                        kt = 2 * a + b
                        product(n, bank(n)[:, SEQ * b:SEQ * (b + 1)],
                                [(A(A_RK, 2, 512)[:, ch, kt * P:(kt + 1) * P], A(A_RQ, 2, SEQ)[:, ch, :])
                                 for ch in range(2)], mark=(b == 1))
                for m in range(2):
                    arrived(pe, u0 + 4 + m)
                for t in range(2):
                    n = job("rg", h, t)
                    begin(pe, n)
                    product(n, bank(n)[:, :], [(hT[:, k, t * P:(t + 1) * P], two_units(u0 + 4, k)) for k in range(KC)])
                for t in range(4):
                    taken(pe, job("rv", h, t))
                for a in range(2):
                    taken(pe, job("rs", h, a))
                for t in range(2):
                    n = job("ro", h, t)
                    begin(pe, n)
                    product(n, bank(n)[:, :], [(A(A_RD, 4, SEQ)[:, kt, t * P:(t + 1) * P], A(A_RV, 4, 512)[:, kt, :])
                                               for kt in range(4)])
                for t in range(2):
                    n = job("ryT", h, t)
                    begin(pe, n)
                    taken(pe, job("ro", h, t))
                    for k in range(4):
                        turn(n, bank(n)[:, k * P:(k + 1) * P], A(A_RG, 2, 512)[:, t, k * P:(k + 1) * P], P, k == 3)
            for h in range(R_HEADS):
                for t in range(2):
                    taken(pe, job("ryT", h, t))
            project_out(1, U_WOUT_O, 16, lambda k: A(A_RY, 16, SEQ)[:, k, :])
            route(1)
            experts(1)
            overflow(1)

        @block.vector
        def _(dve):
            steps = [0]

            def step(ins):
                steps[0] += 1
                ins.then_inc(s_dve, 1)
                dve.wait_ge(s_dve, steps[0])

            tt, ts, stt = dve.tensor_tensor, dve.tensor_scalar, dve.scalar_tensor_tensor

            dve.wait_ge(s_zero, 2)
            n = job("cT")
            done(dve, n)
            dve.tensor_copy(cvec[:, :, 0:2], bank(n)[:, 0:16].rearrange("p (s k) -> p k s", s=2)).then_inc(free_s[n % BANKS], 1)
            n = job("cwT")
            done(dve, n)
            dve.tensor_copy(cwT[:, :], bank(n)[:, 0:12]).then_inc(free_s[n % BANKS], 1)
            taken(dve, n)

            def reciprocal_roots(a, b, squares, roots_done, inv=1.0 / D):
                dve.wait_ge(s_ms, squares)
                ts(stat[:, 0, a:b], stat[:, 0, a:b], inv, EPS, ALU.mult, ALU.add).then_inc(s_rstd, 1)
                dve.wait_ge(s_root, roots_done)
                step(dve.reciprocal(stat[:, 2, a:b], stat[:, 1, a:b]))
                step(tt(stat[:, 1, a:b], stat[:, 2, a:b], stat[:, 2, a:b], ALU.mult))
                step(tt(stat[:, 1, a:b], stat[:, 1, a:b], stat[:, 0, a:b], ALU.mult))
                step(ts(stat[:, 1, a:b], stat[:, 1, a:b], -0.5, 1.5, ALU.mult, ALU.add))
                step(tt(stat[:, 2, a:b], stat[:, 2, a:b], stat[:, 1, a:b], ALU.mult))

            reciprocal_roots(0, 4, 4, 1)

            def mod_block(layer, q):
                a = 6 * layer + q
                n = job("ada", layer, q)
                rows = mod_rows[:, a % 2, :]
                bias = ada_rows[:, a % 2, 0, :]
                done(dve, n)
                dve.wait_ge(s_ada_in[a % 2], ada_in_value[a])
                if a >= 2 and stored_value[a - 2]:
                    dve.wait_ge(s_stored[a % 2], stored_value[a - 2])
                if q in (2, 3):
                    done(dve, job("modT", layer, q - 2))
                if q in (1, 4):
                    step(stt(rows, bank(n)[:, 0:256], 1.0, bias, ALU.add, ALU.add))
                    tt(rows, rows, ada_rows[:, a % 2, 1, :], ALU.mult).then_inc(free_s[n % BANKS], 1)
                else:
                    tt(rows, bank(n)[:, 0:256], bias, ALU.add).then_inc(free_s[n % BANKS], 1)

            def mod_columns(layer, q):
                n = job("modT", layer, q)
                done(dve, n)
                dve.tensor_copy(modT[:, layer, q, :, :].rearrange("p (j h) s -> p h j s", h=2),
                                bank(n)[:, 0:256].rearrange("p (h j r) -> p h j r", h=2, j=4)[:, :, :, 0:2]
                                ).then_inc(free_s[n % BANKS], 1)

            mod_block(0, 0)
            mod_block(0, 1)
            mod_columns(0, 0)
            mod_columns(0, 1)

            def norm_and_turn(layer):
                base = (A_XN, A_XN1)[layer]

                def normed(t):
                    if t >= 2:
                        done(dve, job("hT", layer, t - 2, 1))
                    ts(A(base + (t % 2) * D, D), res[:, t, :], stat[:, 2, t:t + 1], None, ALU.mult).then_inc(s_xn, 1)

                normed(0)
                normed(1)
                for t in range(4):
                    n = job("hT", layer, t, 1)
                    s = t // 2
                    if t == 0:
                        taken(dve, job("modT", layer, 1))
                    done(dve, n)
                    for k in range(4):
                        ins = ts(hT[:, 4 + k, t * P:(t + 1) * P], bank(n)[:, k * P:(k + 1) * P],
                                 modT[:, layer, 1, 4 + k, s:s + 1], modT[:, layer, 0, 4 + k, s:s + 1], ALU.mult, ALU.add)
                    ins.then_inc(free_s[n % BANKS], 1)
                    if t + 2 < 4:
                        normed(t + 2)

            norm_and_turn(0)

            dve.wait_ge(s_bias, 16 * ROWS * ROWS)
            dve.wait_ge(s_con, 16)
            for qt in range(2):
                for h in range(HEADS):
                    ins = tt(A(A_BIAS + qt * 2048, HEADS, ROWS, GRID_W)[:, h],
                             A(A_Q + qt * 2048, HEADS, ROWS, GRID_W)[:, h, :, ::-1],
                             const("window").unsqueeze(1).to_broadcast([P, ROWS, GRID_W]), ALU.add)
            ins.then_inc(s_bias_ready, 1)

            padded = A(A_CONV + 512, 2, SEQ + 2)
            total = A(A_CONV + 1028, 2, SEQ)
            for t in range(4):
                done(dve, job("hT", 0, t, 1))
            step(dve.memset(padded[:, :, 0:SEQ + 2:SEQ + 1], 0.0))
            for ch in range(4):
                taken(dve, job("ac", ch))
                n = job("ax", ch)
                done(dve, n)
                tt(padded[:, :, 1:SEQ + 1], A(A_CONV, 2, SEQ), bank(n)[:, :].rearrange("p (s t) -> p s t", s=2),
                   ALU.mult).then_inc(free_s[n % BANKS], 1)
                taken(dve, n)
                step(ts(total, padded[:, :, 0:SEQ], cwT[:, ch:ch + 1], None, ALU.mult))
                step(stt(total, padded[:, :, 1:SEQ + 1], cwT[:, 4 + ch:5 + ch], total, ALU.mult, ALU.add))
                step(stt(total, padded[:, :, 2:SEQ + 2], cwT[:, 8 + ch:9 + ch], total, ALU.mult, ALU.add))
                n = job("ab", ch)
                done(dve, n)
                tt(A(A_YC, 4, 512)[:, ch, :], total.rearrange("p s t -> p (s t)"), bank(n)[:, :], ALU.mult
                   ).then_inc(free_s[n % BANKS], 1)
            for q in range(2, 6):
                mod_block(0, q)

            scale = float(HEAD_DIM) ** -0.5

            def attention_scores(i):
                h, qt = divmod(i, 4)
                n = job("s", i)
                w = 512 if qt < 2 else 256
                p = A(A_P, 2, 512)[:, i % 2, 0:w]
                s0 = 4 * (i % 3)
                done(dve, n)
                if i >= 2:
                    done(dve, job("pt", i - 2))
                if qt < 2:
                    step(stt(p[:, 0:SEQ], bank(n)[:, 0:SEQ], scale,
                             A(A_BIAS + qt * 2048, HEADS, SEQ)[:, h, :], ALU.mult, ALU.add))
                    ts(p[:, SEQ:512], bank(n)[:, SEQ:512], scale, None, ALU.mult).then_inc(free_s[n % BANKS], 1)
                else:
                    ts(p, bank(n)[:, 0:SEQ], scale, None, ALU.mult).then_inc(free_s[n % BANKS], 1)
                taken(dve, n)
                dve.tensor_reduce(soft[:, s0:s0 + 1], p, AX_X, ALU.max, negate=True).then_inc(s_max, 1)

            def attention_divide(i):
                w = 512 if i % 4 < 2 else 256
                p = A(A_P, 2, 512)[:, i % 2, 0:w]
                s0 = 4 * (i % 3)
                dve.wait_ge(s_exp, i + 1)
                step(dve.reciprocal(soft[:, s0 + 2:s0 + 3], soft[:, s0 + 1:s0 + 2]))
                ts(p, p, soft[:, s0 + 2:s0 + 3], None, ALU.mult).then_inc(s_probs, 1)

            def head_out(j):
                h, s = divmod(j, 2)
                n = job("pv", j)
                b = HEAD_DIM * (h % 2)
                done(dve, n)
                dve.tensor_copy(hT[b:b + HEAD_DIM, h // 2, s * SEQ:(s + 1) * SEQ], bank(n)[b:b + HEAD_DIM, 0:SEQ]
                                ).then_inc(free_s[n % BANKS], 1)

            items = 4 * HEADS
            attention_scores(0)
            for i in range(items):
                if i + 1 < items:
                    attention_scores(i + 1)
                attention_divide(i)
                if i % 2 == 0 and i >= 4:
                    head_out(i // 2 - 2)
            head_out(items // 2 - 2)
            head_out(items // 2 - 1)

            def add_mixer(layer):
                dve.wait_ge(s_gate, 32 * layer + 16)
                for t in range(4 if layer == 0 else 2):
                    for half in range(2):
                        n = job("wo", layer, t, half)
                        s = t // 2
                        done(dve, n)
                        cols = slice(512 * half, 512 * half + 512)
                        tmp = A(A_TMP + 512 * half, 512)
                        tt(tmp, bank(n)[:, :], bc_gate[:, s, cols], ALU.mult).then_inc(free_s[n % BANKS], 1)
                        taken(dve, n)
                        ins = tt(res[:, t, cols], res[:, t, cols], tmp, ALU.add)
                        if half == 0:
                            step(ins)
                    ins.then_inc(s_mixed, 1)

            def modulated(layer):
                nt = TILES[layer]
                dve.wait_ge(s_ab, 32 * (layer + 1))
                for t in range(nt):
                    s = t // 2
                    h2 = A(A_H2 + t * D, D)
                    step(stt(h2, res[:, t, :], stat[:, 2, t:t + 1], A(A_BCA + s * D, D), ALU.mult, ALU.mult))
                    tt(h2, h2, A(A_BCB + s * D, D), ALU.add).then_inc(s_h2, 1)
                for t in range(nt):
                    n = job("rT", layer, t, 1)
                    done(dve, n)
                    dve.tensor_copy(hT[:, 4:8, t * P:(t + 1) * P], bank(n)[:, :].rearrange("p (k q) -> p k q", q=P)
                                    ).then_inc(free_s[n % BANKS], 1)

            def route(layer):
                nt = TILES[layer]
                R = A_ROUTE
                logit = A(R, 4, 36)[:, 0:nt, :]
                in_group = A(R + 160, 4, EXPERTS)[:, 0:nt, :]
                first = A(R + 288, 4, EXPERTS)[:, 0:nt, :]
                second = A(R + 416, 4, EXPERTS)[:, 0:nt, :]
                member = A(R + 640, 4, EXPERTS)[:, 0:nt, :]
                place = A(R + 768, 4, EXPERTS)[:, 0:nt, :]
                scratch = A(R + 896, 4, EXPERTS)[:, 0:nt, :]
                el = A(R + 1024, 4, PER_GROUP)[:, 0:nt, :]
                cand = A(R + 1056, 4, PER_GROUP)[:, 0:nt, :]
                hot1 = A(R + 1088, 4, PER_GROUP)[:, 0:nt, :]
                hot2 = A(R + 1120, 4, PER_GROUP)[:, 0:nt, :]
                hotg = A(R + 1152, 4, GROUPS)[:, 0:nt, :]
                candg = A(R + 1168, 4, GROUPS)[:, 0:nt, :]
                m0, m1, m2, m3 = (A(R + 1200 + 4 * i, 4)[:, 0:nt] for i in range(4))
                sumg, rsum, den, where1, where2 = (A(R + 1220 + 4 * i, 4)[:, 0:nt] for i in range(5))
                count = A(R + 1260, 1)
                gap = A(R + 1408, nt, GROUPS)
                eg = A(R + 1424, nt, GROUPS)
                gap2, t2 = A(R + 1500, nt), A(R + 1504, nt)

                def wide(v, k):
                    return v.unsqueeze(2).to_broadcast([P, nt, k])

                def pick(hot, cand, values, best, idx, k):
                    step(tt(cand, values, wide(best, k), ALU.is_lt))
                    step(stt(cand, cand, BIG, idx.unsqueeze(1).to_broadcast([P, nt, k]), ALU.mult, ALU.add))
                    step(dve.tensor_reduce(m3, cand, AX_X, ALU.min))
                    step(tt(hot, cand, wide(m3, k), ALU.is_equal))

                n = job("logits", layer)
                done(dve, n)
                tt(logit, bank(n)[:, 0:64 * nt].rearrange("p (t c) -> p t c", c=64)[:, :, 0:36],
                   rb[:, :].unsqueeze(1).to_broadcast([P, nt, 36]), ALU.add).then_inc(free_s[n % BANKS], 1)
                taken(dve, n)
                step(dve.tensor_reduce(m0, logit[:, :, 0:GROUPS], AX_X, ALU.max))
                tt(gap, logit[:, :, 0:GROUPS], wide(m0, GROUPS), ALU.subtract).then_inc(s_gap, 1)
                pick(hotg, candg, logit[:, :, 0:GROUPS], m0, const("idx_group"), GROUPS)
                step(tt(in_group.rearrange("p t (g e) -> p t g e", g=GROUPS),
                        logit[:, :, GROUPS:36].rearrange("p t (g e) -> p t g e", g=GROUPS),
                        hotg.unsqueeze(3).to_broadcast([P, nt, GROUPS, PER_GROUP]), ALU.mult))
                step(dve.tensor_reduce(el, in_group.rearrange("p t (g e) -> p t e g", g=GROUPS), AX_X, ALU.add))
                step(dve.tensor_reduce(m1, el, AX_X, ALU.max))
                pick(hot1, cand, el, m1, const("idx_in_group"), PER_GROUP)
                step(stt(el, hot1, -BIG, el, ALU.mult, ALU.add))
                step(dve.tensor_reduce(m2, el, AX_X, ALU.max))
                tt(gap2, m2, m1, ALU.subtract).then_inc(s_gap, 1)
                pick(hot2, cand, el, m2, const("idx_in_group"), PER_GROUP)
                for hot, to in ((hot1, first), (hot2, second)):
                    step(tt(to.rearrange("p t (g e) -> p t g e", g=GROUPS),
                            hotg.unsqueeze(3).to_broadcast([P, nt, GROUPS, PER_GROUP]),
                            hot.unsqueeze(2).to_broadcast([P, nt, GROUPS, PER_GROUP]), ALU.mult))
                tt(member, first, second, ALU.add).then_inc(s_members, 1)
                dve.wait_ge(s_rexp, 2 * layer + 2)
                step(dve.tensor_reduce(sumg, eg, AX_X, ALU.add))
                step(ts(den, t2, 1.0, None, ALU.add))
                step(tt(den, den, sumg, ALU.mult))
                step(dve.reciprocal(gates[:, 0, 0:nt], den))
                step(tt(gates[:, 1, 0:nt], gates[:, 0, 0:nt], t2, ALU.mult))
                n = job("ranks", layer)
                done(dve, n)
                step(dve.tensor_reduce(count, bank(n)[:, 128:160], AX_X, ALU.max))
                stt(place, bank(n)[:, 0:32 * nt].rearrange("p (t e) -> p t e", e=EXPERTS), float(EXPERTS),
                    const("idx_expert").unsqueeze(1).to_broadcast([P, nt, EXPERTS]), ALU.mult, ALU.add
                    ).then_inc(free_s[n % BANKS], 1)
                taken(dve, n)
                dve.tensor_copy(fullest[:, :], count).then_inc(s_flag, 1)
                for k, (hot, to) in enumerate(((first, where1), (second, where2))):
                    step(tt(scratch, place, hot, ALU.mult))
                    step(dve.tensor_reduce(to, scratch, AX_X, ALU.add))
                step(dve.tensor_copy(addr[:, 0, 0:nt], where1))
                dve.tensor_copy(addr[:, 1, 0:nt], where2).then_inc(s_addr, 1)
                dve.wait_ge(s_table_in, 32 * (layer + 1))
                step(ts(gidx[:, :], table[0:SLOTS, :], 1, None, ALU.logical_shift_right))
                ts(sidx[:, :], table[:, :], 2.0, const("half"), ALU.mult, ALU.add).then_inc(s_idx, 1)

            def experts(layer):
                n0 = job("moe", layer)
                with dve.Fori(0, TURNS) as it:
                    for u in range(EPI):
                        n = n0 + PER_EXPERT * u
                        b = u % 2
                        dve.wait_ge(s_silu, it * EPI + (EXPERTS * layer + u + 1))
                        tt(A(A_HID + b * 256, 256)[0:SLOTS, :], bank(n + 1)[SLOTS:P, 0:HIDDEN],
                           A(A_SL + b * 256, 256)[0:SLOTS, :], ALU.mult).then_inc(free_s[(n + 1) % BANKS], 1)
                        done(dve, n + 3, it)
                        dve.wait_ge(s_scat[u], it * 16 + 16 * (TURNS * layer + 1))
                        dve.tensor_copy(A(A_YS + u * 512, 512), bank(n + 3)[:, :]).then_inc(free_s[(n + 3) % BANKS], 1)

            def overflow(layer):
                dve.wait_ge(s_flag, layer + 1)
                count = dve.value_load(fullest[0:1, 0:1], min_val=0, max_val=4 * P)
                o = lambda k: ov[layer, k]
                with dve.If(count > SLOTS):
                    with dve.Fori(0, (TILES[layer] * P // SLOTS - 1) * EXPERTS) as n:
                        dve.wait_ge(o("ix"), n * 32 + 32)
                        ts(ov_idx[0:SLOTS, 0:1], ov_table[0:SLOTS, :], 1, None, ALU.logical_shift_right)
                        ts(ov_idx[:, 1:2], ov_table[:, :], 2.0, const("half"), ALU.mult, ALU.add).then_inc(o("idx"), 1)
                        dve.wait_ge(o("a2"), n + 1)
                        tt(A(A_HID, 256)[0:SLOTS, :], banks[1][SLOTS:P, 0:HIDDEN], A(A_SL, 256)[0:SLOTS, :], ALU.mult
                           ).then_inc(o("d2"), 1)

            def combine(layer):
                nt = TILES[layer]
                dve.wait_ge(s_gate, 32 * (layer + 1))
                for t in range(nt):
                    s = t // 2
                    dve.wait_ge(s_y_in[t % 2], 16 * (t // 2 + 1) + (0 if layer == 0 else 32))
                    y = A(A_XG + (t % 2) * 2 * D, 2, D)
                    step(ts(y[:, 0, :], y[:, 0, :], gates[:, 0, t:t + 1], None, ALU.mult))
                    step(stt(y[:, 0, :], y[:, 1, :], gates[:, 1, t:t + 1], y[:, 0, :], ALU.mult, ALU.add))
                    step(tt(y[:, 0, :], y[:, 0, :], bc_gate[:, s, :], ALU.mult))
                    tt(res[:, t, :], res[:, t, :], y[:, 0, :], ALU.add).then_inc(s_comb, 1)

            add_mixer(0)
            mod_block(1, 0)
            mod_block(1, 1)
            mod_columns(1, 0)
            mod_columns(1, 1)
            for q in range(2, 6):
                mod_block(1, q)
            reciprocal_roots(0, 4, 8, 2)
            modulated(0)
            route(0)
            experts(0)
            overflow(0)
            combine(0)

            reciprocal_roots(0, 4, 12, 3)
            dve.wait_ge(s_dec, 1)
            ts(dec[:, 16:24], dec[:, 8:16], -1.0, 1.0, ALU.mult, ALU.add).then_inc(s_dec, 1)
            dve.wait_ge(s_dec, 3)
            step(ts(dec[:, 32:40], dec[:, 16:24], -1.0, 1.0, ALU.mult, ALU.add))
            step(ts(dec[:, 32:40], dec[:, 32:40], 1.0e-30, None, ALU.max))
            step(dve.reciprocal(dec[:, 32:40], dec[:, 32:40]))
            step(tt(dec[:, 32:40], dec[:, 32:40], dec[:, 8:16], ALU.mult))
            tt(dec[:, 24:32], dec[:, 24:32], dec[:, 32:40], ALU.mult).then_inc(s_dec, 1)
            dve.wait_ge(s_dec, 4)
            ts(dec[:, 32:40], dec[:, 24:32], float(SEQ), None, ALU.mult).then_inc(s_dec, 1)
            ts(dec[:, 0:4], dec[:, 28:32], -1.0, None, ALU.mult).then_inc(s_dec, 1)
            norm_and_turn(1)

            tab = lambda k: A(A_RTAB + 512 * k, 512)
            rope = lambda ch, k: A(A_ROPE + (2 * ch + k) * SEQ, SEQ)

            def rotate(to, ps, ch, n, last):
                ra, rb_ = A(A_RTMP, SEQ), A(A_RTMP + SEQ, SEQ)
                step(tt(ra, ps, rope(ch, 0), ALU.mult))
                step(tt(rb_[0:64, :], ps[64:128, :], rope(ch, 1)[0:64, :], ALU.mult))
                ins = tt(rb_[64:128, :], ps[0:64, :], rope(ch, 1)[64:128, :], ALU.mult)
                step(ins)
                ins = tt(to, ra, rb_, ALU.add)
                if last:
                    ins.then_inc(free_s[n % BANKS], 1)
                    taken(dve, n)
                else:
                    step(ins)

            dve.wait_ge(s_ret_in, 16)
            for h in range(R_HEADS):
                n = job("rq", h)
                done(dve, n)
                for ch in range(2):
                    rotate(A(A_RQ, 2, SEQ)[:, ch, :], bank(n)[:, SEQ * ch:SEQ * (ch + 1)], ch, n, ch == 1)
                for ch in range(2):
                    n = job("rk", h, ch)
                    done(dve, n)
                    dve.wait_ge(s_ctx_keys, 2 * h + ch + 1)
                    rotate(A(A_RK, 2, 512)[:, ch, 0:SEQ], bank(n)[:, 0:SEQ], ch, n, True)
                dk, e = A(A_RD, 512), A(A_EXP, 512)
                dve.wait_ge(s_rexps, 4 * h + 2)
                step(tt(dk, dk, tab(3), ALU.mult))
                step(tt(e, e, tab(4), ALU.mult))
                tt(dk, dk, e, ALU.add).then_inc(s_factors, 1)
                dc = A(A_RD + 512, 512)
                dve.wait_ge(s_rexps, 4 * h + 4)
                tt(dc, dc, e, ALU.add).then_inc(s_factors, 1)
                dve.wait_ge(s_factors, 2 * h + 2)
                for a in range(2):
                    n = job("rs", h, a)
                    d = A(A_RD + 512 * a, 512)
                    done(dve, n)
                    stt(d, bank(n)[:, :], float(R_QK) ** -0.5, d, ALU.mult, ALU.mult).then_inc(free_s[n % BANKS], 1)
                for t in range(2):
                    i = 2 * h + t
                    n = job("ro", h, t)
                    dve.wait_ge(s_yms, i + 1)
                    ts(soft[:, 2 + t:3 + t], soft[:, t:t + 1], 1.0 / R_V, EPS, ALU.mult, ALU.add).then_inc(s_yroot, 1)
                    dve.wait_ge(s_yroot, 2 * i + 2)
                    step(dve.reciprocal(soft[:, 6 + t:7 + t], soft[:, 4 + t:5 + t]))
                    g = A(A_RG, 2, 512)[:, t, :]
                    taken(dve, job("rg", h, t))
                    stt(g, bank(n)[:, :], soft[:, 6 + t:7 + t], g, ALU.mult, ALU.mult).then_inc(free_s[n % BANKS], 1)
            add_mixer(1)
            reciprocal_roots(0, 2, 14, 4)
            modulated(1)
            route(1)
            experts(1)
            overflow(1)
            combine(1)
            reciprocal_roots(0, 2, 16, 5)
            dve.wait_ge(s_fin_g, 16)
            for t in range(2):
                stt(A(A_XG + t * D, D), res[:, t, :], stat[:, 2, t:t + 1], A(A_BCA, D), ALU.mult, ALU.mult
                    ).then_inc(s_fin, 1)


_INS = ["x", "c", "ctx", "c_ctx", "ada_w", "ada_b", "norm1_g", "norm2_g", "w_in_e", "conv_w", "na_rpb", "w_out_e",
        "w_in_o", "ret_decay_f", "ret_decay_b", "w_out_o", "router_gw", "router_gb", "router_ew", "router_eb",
        "moe_w1", "moe_w3", "moe_w2", "final_g"]


def kernel(**inputs):
    import numpy as _np
    import concourse.bacc as _bacc
    from concourse import mybir as _mybir
    from concourse.bass_utils import run_bass_kernel_spmd as _run

    nc = _bacc.Bacc("TRN2", target_bir_lowering=False, num_devices=1)
    arrays, args, consts = {}, [], []

    def declare(name, a):
        arrays[name] = a
        return nc.dram_tensor(name, a.shape, _mybir.dt.from_np(a.dtype), kind="ExternalInput").ap()

    for name in _INS:
        a = inputs[name]
        if name == "na_rpb":
            a = a[..., ::-1]
        args.append(declare(f"in_{name}_dram", _np.ascontiguousarray(a)))
    for i, a in enumerate(shape_constants()):
        consts.append(declare(f"const_{i}_dram", _np.ascontiguousarray(a)))
    out = nc.dram_tensor("out_0_dram", (1, SEQ, D), _mybir.dt.from_np(_np.dtype("float32")), kind="ExternalOutput").ap()
    backbone(nc, args, consts, out)
    r = _run(nc, [arrays], core_ids=[0])
    return r.results[0]["out_0_dram"]
```

```python
from contextlib import ExitStack

import numpy as np
import concourse.bass as bass
from concourse import mybir

F32 = mybir.dt.float32
U32 = mybir.dt.uint32
I32 = mybir.dt.int32
ALU = mybir.AluOpType
ACT = mybir.ActivationFunctionType
AX_X = mybir.AxisListType.X

P = 128
D = 1024
KC = D // P
SEQ = 256
CTX = 256
GRID_W = 64
ROWS = SEQ // GRID_W
WIN_W = 16
HEADS = 8
HEAD_DIM = 64
R_HEADS = 4
R_QK = 256
R_V = 512
ROPE_BASE = 10000.0
GROUPS = 4
PER_GROUP = 8
EXPERTS = GROUPS * PER_GROUP
HIDDEN = 256
GROUP_HIDDEN = PER_GROUP * HIDDEN
EPS = 1e-6
BIG = 1.0e30
TILES = (4, 2)
SLOTS = 64
NO_ID = 2 * TILES[0] * P

UNIT = 2048
RING = 12
BANKS = 8
EPI = 4
TURNS = EXPERTS // EPI
PER_EXPERT = 4

CONST_COLS = {}
_at = 0
for _name, _n in (("ident", P), ("upper", P), ("ones", P), ("window", GRID_W), ("idx_group", GROUPS),
                  ("idx_in_group", PER_GROUP), ("idx_expert", EXPERTS), ("half", 1), ("ids", 8)):
    CONST_COLS[_name] = (_at, _n)
    _at += _n
CONST_N = _at
RET_N = 2 * SEQ * 5 + 4 * SEQ


def shape_constants():
    c = np.zeros((P, CONST_N), np.float32)

    def put(name, a):
        o, n = CONST_COLS[name]
        c[:, o:o + n] = a

    i = np.arange(P)
    put("ident", np.eye(P))
    put("upper", i[:, None] < i[None, :])
    put("ones", 1.0)
    col = i % GRID_W
    first = np.clip(col - WIN_W // 2, 0, GRID_W - WIN_W)
    j = np.arange(GRID_W)
    inside = (j[None, :] >= first[:, None]) & (j[None, :] < first[:, None] + WIN_W)
    put("window", np.where(inside, 0.0, -BIG))
    put("idx_group", np.arange(GROUPS))
    put("idx_in_group", np.arange(PER_GROUP))
    put("idx_expert", np.arange(EXPERTS))
    put("half", 2 * NO_ID + (i >= SLOTS)[:, None])
    ids = 2 * (np.arange(4)[None, None, :] * P + i[:, None, None]) + np.arange(2)[None, :, None]
    put("ids", ids.reshape(P, 8) - NO_ID)

    q = np.arange(SEQ, dtype=np.float32)
    dist = np.stack([q[None, :] - (t * P + i)[:, None] for t in range(2)], 1).astype(np.float32)
    parts = [dist, np.maximum(dist, 0), np.maximum(-dist, 0), dist >= 0, dist <= 0]
    freq = (np.float32(ROPE_BASE) ** (-np.arange(64, dtype=np.float32) / np.float32(64))).astype(np.float32)
    pos = np.arange(SEQ)
    sign = np.where(i < 64, -1.0, 1.0).astype(np.float32)[:, None]
    for axis in (pos // GRID_W, pos % GRID_W):
        ang = (axis.astype(np.float32)[None, :] * freq[i % 64][:, None]).astype(np.float32)
        parts += [np.cos(ang), np.sin(ang) * sign]
    ret = np.concatenate([p.reshape(P, -1) for p in parts], 1).astype(np.float32)
    return c, ret


ITEMS = 4 * HEADS
AFTER_ITEM = {3: (0, 2), 8: (0, 3), 13: (0, 4), 18: (0, 5), 23: (1, 0), 28: (1, 1)}
AFTER_WO = {1: (1, 2), 3: (1, 3)}


NORM2_GROUPS = (((0, 1), (2, 3)), ((0,), (1,)))


def plan_jobs():
    jobs = {}
    n = 0

    def add(*name):
        nonlocal n
        jobs[name] = n
        n += 1

    add("cT")
    add("cwT")
    for q in range(2):
        add("ada", 0, q)
    for q in range(2):
        add("modT", 0, q)
    for t in range(4):
        for half in range(2):
            add("hT", 0, t, half)
    for ch in range(4):
        add("ac", ch)
        add("ax", ch)
        add("ab", ch)
    for ch in range(4):
        add("q", ch)
    for ch in range(4):
        add("k", ch)
    for t in range(4):
        add("v", t)
    for i in range(3):
        add("s", i)
    for i in range(ITEMS):
        if i + 3 < ITEMS:
            add("s", i + 3)
        add("pt", i)
        if i % 2 and i > 1:
            add("pv", (i - 3) // 2)
        if i in AFTER_ITEM:
            add("ada", *AFTER_ITEM[i])
    add("pv", ITEMS // 2 - 1)
    for q in range(2):
        add("modT", 1, q)
    for i in range(8):
        add("wo", 0, i // 2, i % 2)
        if i in AFTER_WO:
            add("ada", *AFTER_WO[i])

    def experts(layer):
        for t in range(TILES[layer]):
            for half in range(2):
                add("rT", layer, t, half)
            if layer == 0 and t == 1:
                add("ada", 1, 4)
        add("logits", layer)
        add("ranks", layer)
        add("table", layer)
        if layer == 0:
            add("ada", 1, 5)
        nonlocal n
        jobs[("moe", layer)] = n
        n += EXPERTS * PER_EXPERT

    experts(0)
    for t in range(2):
        for half in range(2):
            add("hT", 1, t, half)
    add("rq", 0)
    for t in range(2):
        add("rg", 0, t)
    for t in range(2, 4):
        for half in range(2):
            add("hT", 1, t, half)
    for h in range(R_HEADS):
        for c in range(2):
            add("rk", h, c)
        for t in range(4):
            add("rv", h, t)
        for a in range(2):
            add("rs", h, a)
        if h + 1 < R_HEADS:
            add("rq", h + 1)
        for t in range(2):
            add("ro", h, t)
        if h + 1 < R_HEADS:
            for t in range(2):
                add("rg", h + 1, t)
        else:
            add("wo", 1, 0, 0)
        for t in range(2):
            add("ryT", h, t)
    for i in range(1, 4):
        add("wo", 1, i // 2, i % 2)
    experts(1)
    return jobs


JOBS = plan_jobs()

U_ADA_A = 0
U_WIN_E = U_ADA_A + 8
U_ADA_B = U_WIN_E + 12
U_WOUT_E = U_ADA_B + 24
U_ADA_C = U_WOUT_E + 4
U_MOE0 = U_ADA_C + 16
U_WIN_O = U_MOE0 + 3 * EXPERTS
U_WOUT_O = U_WIN_O + 24
U_MOE1 = U_WOUT_O + 8


def ada_units(layer, q):
    a = 6 * layer + q
    return U_ADA_A + 4 * a if a < 2 else U_ADA_B + 4 * (a - 2) if a < 8 else U_ADA_C + 4 * (a - 8)

ARENA = 15360
A_BCA, A_BCB = 0, 2048
A_BIAS = 0
A_Q, A_K, A_V, A_YC = 4096, 6144, 8192, 10240
A_PT = 13312
A_XN = 13312
A_CONV = 13312
A_TMP = 14336
A_H2 = (4096, 10496)
A_XG, A_XGT, A_YS, A_SL, A_HID, A_HIDT, A_ROUTE = 4096, 8192, 9216, 11264, 11776, 12288, 12544
A_SQUARES = 13312
A_HOT, A_VALUED = 9216, 10240
A_RQ, A_RK, A_RV, A_RG, A_RY, A_RD = 0, 512, 1536, 3584, 4608, 8704
A_RTAB, A_ROPE, A_RTMP, A_RG_ODD, A_EXP = 9728, 12288, 13312, 13824, 14848
A_XN1 = 4608


def backbone(nc, ins, consts, out):
    (x, c, ctx_in, c_ctx, ada_w, ada_b, norm1_g, norm2_g, w_in_e, conv_w, rpb_rev, w_out_e, w_in_o,
     decay_f, decay_b, w_out_o, router_gw, router_gb, router_ew, router_eb, moe_w1, moe_w3, moe_w2,
     final_g) = ins
    shape_c, ret_c = consts

    stack = ExitStack()
    with stack:
        def sb(name, shape, dt=F32):
            return stack.enter_context(nc.sbuf_tensor(name, shape, dt))

        def sem(name):
            return stack.enter_context(nc.semaphore(name))

        mod_rows_d = nc.dram_tensor("mod_rows_d", [12, 2, D], F32).ap()
        h2_d = [nc.dram_tensor(f"h2_d{l}", [TILES[l] * P, D], F32).ap() for l in range(2)]
        table_d = [nc.dram_tensor(f"table_d{l}", [TILES[l] * P * EXPERTS, 1], U32).ap() for l in range(2)]
        y_d = [nc.dram_tensor(f"y_d{l}", [TILES[l] * P * 4, D // 2], F32).ap() for l in range(2)]

        ring = sb("ring", [P, RING, UNIT])
        arena = sb("arena", [P, ARENA])
        res = sb("res", [P, 4, D])
        hT = sb("hT", [P, KC, 4 * P])
        bc_gate = sb("bc_gate", [P, 2, D])
        con = sb("con", [P, CONST_N])
        crow = bc_gate[0:16, 0, 0:P]
        csil = bc_gate[0:16, 0, P:2 * P]
        cwrow = bc_gate[0:12, 0, 2 * P:3 * P]
        cvec = sb("cvec", [P, KC, 32])
        cwT = sb("cwT", [P, 12])
        ada_rows = sb("ada_rows", [P, 2, 2, 256])
        mod_rows = sb("mod_rows", [P, 2, 256])
        modT = sb("modT", [P, 2, 2, KC, 2])
        stat = sb("stat", [P, 3, 4])
        rw = sb("rw", [P, KC, 36])
        rb = sb("rb", [P, 36])
        gates = sb("gates", [P, 2, 4])
        addr = sb("addr", [P, 2, 4], U32)
        table = sb("table", [P, EXPERTS], U32)
        gidx = sb("gidx", [SLOTS, EXPERTS], U32)
        sidx = sb("sidx", [P, EXPERTS], U32)
        gnow = sb("gnow", [SLOTS, 8], U32)
        snow = sb("snow", [P, 8], U32)
        ov_table = sb("ov_table", [P, 1], U32)
        ov_idx = sb("ov_idx", [P, 2], U32)
        fullest = sb("fullest", [P, 1], I32)
        soft = sb("soft", [P, 16])
        dec = sb("dec", [P, 8 * 5])

        def const(name):
            o, n = CONST_COLS[name]
            return con[:, o:o + n]

        ident = const("ident")

        def A(at, *shape):
            n = 1
            for s in shape:
                n *= s
            v = arena[:, at:at + n]
            if len(shape) == 2:
                v = v.rearrange("p (a b) -> p a b", b=shape[1])
            if len(shape) == 3:
                v = v.rearrange("p (a b c) -> p a b c", b=shape[1], c=shape[2])
            return v

        banks = [stack.enter_context(nc.psum_tensor(f"bank{b}", [P, 512], F32)) for b in range(BANKS)]

        arrived_s = [sem(f"weights_in{s}") for s in range(RING)]
        full_s = [sem(f"psum_full{b}") for b in range(BANKS)]
        free_s = [sem(f"psum_free{b}") for b in range(BANKS)]
        s_c, s_con, s_x, s_cw = sem("c_in"), sem("constants_in"), sem("x_in"), sem("conv_w_in")
        s_bias = sem("bias_in")
        s_csil, s_ms, s_root, s_rstd, s_xn = (sem("silu_c"), sem("mean_square"), sem("root"),
                                              sem("rstd_ready"), sem("normed_ready"))
        s_ada_in = [sem(f"ada_rows_in{i}") for i in range(2)]
        s_zero = sem("zeroed")
        s_stored = [sem(f"mod_rows_stored{i}") for i in range(2)]
        s_gate, s_ab = sem("gate_rows_in"), sem("scale_and_shift_in")
        s_bias_ready = sem("bias_ready")
        s_scores, s_exp, s_probs = sem("scores_ready"), sem("exp_ready"), sem("probs_ready")
        s_max = sem("max_ready")
        s_mixed = sem("mixer_added")
        s_h2, s_h2_out = sem("h2_ready"), sem("h2_stored")
        s_rw = sem("router_in")
        s_gap, s_rexp = sem("router_gap_ready"), sem("router_exp_ready")
        s_members, s_addr = sem("members_ready"), sem("addresses_ready")
        s_table_clear, s_hot = sem("table_cleared"), sem("slot_one_hots_ready")
        s_idx = sem("indices_ready")
        s_gath = [sem(f"rows_in{u}") for u in range(EPI)]
        s_scat = [sem(f"rows_out{u}") for u in range(EPI)]
        s_now = sem("index_column_ready")
        s_silu = sem("expert_silu_ready")
        s_hid = sem("expert_hidden_ready")
        s_y_in, s_comb = [sem(f"expert_rows_in{t}") for t in range(4)], sem("tile_combined")
        s_first = sem("first_expert_weighted")
        s_dec_in, s_dec = sem("decay_in"), sem("decay_ready")
        s_rope_in, s_ret_in = sem("rotary_tables_in"), sem("distances_in")
        s_pe_seen, s_pool_seen = sem("tensor_waits_seen"), sem("gpsimd_waits_seen")
        s_rexps = sem("decay_exp_ready")
        s_factors = sem("decay_factors_added")
        s_yms, s_yroot = sem("y_square_sum"), sem("y_root")
        s_ctx_keys = sem("context_keys_ready")
        s_fin, s_fin_g, s_out = sem("final_ready"), sem("final_g_in"), sem("output_stored")
        s_dve, s_pool = sem("vector_step"), sem("gpsimd_step")
        ov = {}
        for l in range(2):
            for k in ("set", "w", "ix", "idx", "g", "p1", "a1", "p2", "a2", "d2", "p3", "a3", "y", "a4", "scat"):
                ov[l, k] = sem(f"over{l}_{k}")

        def bank(n):
            return banks[n % BANKS]

        def job(*name):
            return JOBS[name]

        def begin(eng, n, turn=0):
            if isinstance(turn, int):
                v = n // BANKS + 2 * turn
                if v > 0:
                    eng.wait_ge(free_s[n % BANKS], v)
            else:
                eng.wait_ge(free_s[n % BANKS], turn * 2 + n // BANKS)

        def done(eng, n, turn=0):
            eng.wait_ge(full_s[n % BANKS], turn * 2 + (n // BANKS + 1))

        def taken(eng, n, turn=0):
            eng.wait_ge(free_s[n % BANKS], turn * 2 + (n // BANKS + 1))

        def arrived(eng, n, turn=0):
            eng.wait_ge(arrived_s[n % RING], turn * 16 + 16 * (n // RING + 1))

        def unit(n):
            return ring[:, n % RING, :]

        def ada_name(a):
            return a // 6, a % 6

        ada_in_count = [0, 0]
        ada_in_value = []
        for a in range(12):
            ada_in_count[a % 2] += 16 * (4 if a % 6 in (1, 4) else 2)
            ada_in_value.append(ada_in_count[a % 2])
        stored_count = [0, 0]
        stored_value = []
        for a in range(12):
            if a % 6 >= 2:
                stored_count[a % 2] += 32
            stored_value.append(stored_count[a % 2])

        def last_reader(n):
            if n < U_WIN_E:
                return job("ada", 0, n // 4)
            if n < U_ADA_B:
                m = n - U_WIN_E
                if m < 6:
                    ch = 2 * (m // 3) + 1
                    return job(("ab", "ac", "ax")[m % 3], ch)
                if m < 10:
                    return job("q" if m < 8 else "k", 2 * (m % 2) + 1)
                return job("v", 3)
            if n < U_WOUT_E:
                return job("ada", *ada_name(2 + (n - U_ADA_B) // 4))
            if n < U_ADA_C:
                return job("wo", 0, 3, 1)
            if n < U_MOE0:
                return job("ada", 1, 2 + (n - U_ADA_C) // 4)
            if n < U_WIN_O:
                return moe_reader(0, n - U_MOE0)
            if n < U_WOUT_O:
                h, m = divmod(n - U_WIN_O, 6)
                return (job("rg", h, 1), job("rg", h, 1), job("rq", h), job("rv", h, 3), job("rv", h, 3),
                        job("rk", h, 1))[m]
            if n < U_MOE1:
                return job("wo", 1, 1, 1)
            return moe_reader(1, n - U_MOE1)

        def moe_reader(layer, m):
            e, part = divmod(m, 3)
            return job("moe", layer) + PER_EXPERT * e + (3 if part == 2 else 1)

        def room(eng, n):
            if n >= RING:
                done(eng, last_reader(n - RING))

        def probs(i):
            return hT[:, 4 + i % 4, 0:512 if i % 4 < 2 else 256]

        def ret_gate(h):
            return A((A_RG, A_RG_ODD)[h % 2], 2, 512)

        block = stack.enter_context(nc.Block())

        @block.sync
        def _(sp):
            sp.dma_start(crow[0:8, :], c.rearrange("a (k p) -> (a k) p", p=P)).then_inc(s_c, 16)
            sp.dma_start(crow[8:16, :], c_ctx.rearrange("(k p) -> k p", p=P)).then_inc(s_c, 16)
            sp.dma_start(con[:, :], shape_c).then_inc(s_con, 16)
            sp.dma_start(cwrow, conv_w[0].rearrange("w (k p) -> (w k) p", p=P)).then_inc(s_cw, 16)

            def ada_unit(layer, n, m):
                room(sp, n)
                sp.dma_start(unit(n).rearrange("p (k n) -> p k n", k=KC),
                             ada_w[layer, :, 256 * m:256 * m + 256].rearrange("(k p) n -> p k n", p=P)
                             ).then_inc(arrived_s[n % RING], 16)

            for m in range(8):
                ada_unit(0, U_ADA_A + m, m)
                if m == 3:
                    sp.dma_start(res[:, 0:2, :], x[0].rearrange("(t p) d -> p t d", p=P)).then_inc(s_x, 16)
                    sp.dma_start(res[:, 2:4, :], ctx_in[0].rearrange("(t p) d -> p t d", p=P)).then_inc(s_x, 16)

            def columns(w, n, col):
                room(sp, n)
                sp.dma_start(unit(n).rearrange("p (k n) -> p k n", k=KC),
                             w[0, :, col:col + 256].rearrange("(k p) n -> p k n", p=P)
                             ).then_inc(arrived_s[n % RING], 16)

            def rows(w, n, row):
                room(sp, n)
                sp.dma_start(unit(n).rearrange("p (k n) -> p k n", k=2),
                             w[0, row:row + 256, :].rearrange("(k p) n -> p k n", p=P)
                             ).then_inc(arrived_s[n % RING], 16)

            for pair in range(2):
                for part in range(3):
                    columns(w_in_e, U_WIN_E + 3 * pair + part, 512 * part + 256 * pair)
            for m in range(6):
                columns(w_in_e, U_WIN_E + 6 + m, 1536 + 256 * m)
            for m in range(24):
                ada_unit((8 + m) // 24, U_ADA_B + m, (8 + m) % 24)
            for m in range(4):
                rows(w_out_e, U_WOUT_E + m, 256 * m)
            for m in range(16):
                ada_unit(1, U_ADA_C + m, 8 + m)

            def moe_stream(layer, u0):
                for m in range(24):
                    room(sp, u0 + m) if m < RING else done(sp, moe_reader(layer, m - RING))
                    e, part = divmod(m, 3)
                    load_part(layer, 0, e, part, u0 + m, 0)
                with sp.Fori(1, GROUPS) as g:
                    for m in range(24):
                        back = moe_reader(layer, m + 12) if m < 12 else moe_reader(layer, m - 12)
                        turn = (g - 1) * 2 if m < 12 else g * 2
                        done(sp, back, turn)
                        e, part = divmod(m, 3)
                        load_part(layer, g, e, part, u0 + m, g * 2)

            def load_part(layer, g, e, part, n, turn):
                u = unit(n)
                if part < 2:
                    w = (moe_w1, moe_w3)[part]
                    src = w[layer, bass.ds(g, 1), :, HIDDEN * e:HIDDEN * (e + 1)].rearrange(
                        "a (k p) n -> p (a k) n", p=P)
                    dst = u.rearrange("p (k n) -> p k n", k=KC)
                else:
                    src = moe_w2[layer, bass.ds(g, 1), HIDDEN * e:HIDDEN * (e + 1), :].rearrange(
                        "a (k p) n -> p (a k) n", p=P)
                    dst = u.rearrange("p (k n) -> p k n", k=2)
                sp.dma_start(dst, src).then_inc(arrived_s[n % RING], 16)

            def overflow(layer):
                sp.wait_ge(s_idx, layer + 1)
                count = sp.value_load(fullest[0:1, 0:1], min_val=0, max_val=4 * P)
                with sp.If(count > SLOTS):
                    done(sp, job("moe", layer) + EXPERTS * PER_EXPERT - 1)
                    with sp.Fori(0, TILES[layer] * P // SLOTS - 1) as b:
                        with sp.Fori(0, GROUPS) as g:
                            with sp.Fori(0, PER_GROUP) as e:
                                sp.wait_ge(ov[layer, "y"], b * EXPERTS + g * PER_GROUP + e + 1)
                                for w, place in ((moe_w1, 0), (moe_w3, 1)):
                                    sp.dma_start(
                                        unit(place).rearrange("p (k n) -> p k n", k=KC),
                                        w[layer, bass.ds(g, 1), :, bass.ds(e * HIDDEN, HIDDEN)].rearrange(
                                            "a (k p) n -> p (a k) n", p=P)).then_inc(ov[layer, "w"], 16)
                                sp.dma_start(
                                    unit(2).rearrange("p (k n) -> p k n", k=2),
                                    moe_w2[layer, bass.ds(g, 1), bass.ds(e * HIDDEN, HIDDEN), :].rearrange(
                                        "a (k p) n -> p (a k) n", p=P)).then_inc(ov[layer, "w"], 16)
                    sp.wait_ge(ov[layer, "y"], (TILES[layer] * P // SLOTS - 1) * EXPERTS + 1)
                    sp.wait_ge(ov[layer, "scat"], 16 * (TILES[layer] * P // SLOTS - 1) * EXPERTS)

            def load_results(layer):
                for u in range(EPI):
                    sp.wait_ge(s_scat[u], 16 * (TURNS * (layer + 1) + 1))
                for t in range(TILES[layer]):
                    sp.dma_start(A(A_XG + t * 2 * D, 2 * D),
                                 y_d[layer][t * P * 4:(t + 1) * P * 4, :].rearrange("(p a) n -> p (a n)", a=4)
                                 ).then_inc(s_y_in[t], 16)

            moe_stream(0, U_MOE0)
            overflow(0)
            for h in range(R_HEADS):
                n = U_WIN_O + 6 * h
                for m in range(2):
                    columns(w_in_o, n + m, 2 * D + R_HEADS * R_V + R_V * h + 256 * m)
                    if h == 0 and m == 1:
                        load_results(0)
                columns(w_in_o, n + 2, R_QK * h)
                for m in range(2):
                    columns(w_in_o, n + 3 + m, 2 * D + R_V * h + 256 * m)
                columns(w_in_o, n + 5, D + R_QK * h)
            for m in range(8):
                rows(w_out_o, U_WOUT_O + m, 256 * m)
            moe_stream(1, U_MOE1)
            overflow(1)
            load_results(1)
            for t in range(2):
                sp.wait_ge(s_fin, t + 1)
                sp.dma_start(out[0, t * P:(t + 1) * P, :], A(A_XG + t * D, D)).then_inc(s_out, 16)
            sp.wait_ge(s_out, 32)

        @block.gpsimd
        def _(pool):
            steps = [0]

            def step(ins):
                steps[0] += 1
                ins.then_inc(s_pool, 1)
                pool.wait_ge(s_pool, steps[0])

            pool.memset(ada_rows[:, :, :, :], 0.0).then_inc(s_zero, 1)
            pool.memset(cvec[:, :, :], 0.0).then_inc(s_zero, 1)
            pool.wait_ge(s_zero, 2)

            def load_ada_rows(a):
                layer, q = ada_name(a)
                for s in range(2):
                    pool.dma_start(ada_rows[s:P:32, a % 2, 0, :],
                                   ada_b[layer, q * D:(q + 1) * D].rearrange("(j n) -> j n", n=256)
                                   ).then_inc(s_ada_in[a % 2], 16)
                    if q in (1, 4):
                        g = (norm1_g if q == 1 else norm2_g)[layer]
                        pool.dma_start(ada_rows[s:P:32, a % 2, 1, :], g.rearrange("(j n) -> j n", n=256)
                                       ).then_inc(s_ada_in[a % 2], 16)

            def store_mod_rows(a):
                taken(pool, job("ada", *ada_name(a)))
                if a % 6 >= 2:
                    for s in range(2):
                        pool.dma_start(mod_rows_d[a, s].rearrange("(j n) -> j n", n=256),
                                       mod_rows[s:P:32, a % 2, :]).then_inc(s_stored[a % 2], 16)

            def broadcast(to, a, landed):
                pool.wait_ge(s_stored[a % 2], stored_value[a])
                src = bass.AP(mod_rows_d.tensor, a * 2 * D, [[0, P], [1, 2 * D]])
                pool.dma_start(to, src).then_inc(landed, 16)

            load_ada_rows(0)
            load_ada_rows(1)
            for i, d in enumerate((decay_f, decay_b)):
                pool.dma_start(dec[:, 4 * i:4 * i + 4], bass.AP(d.tensor, 0, [[0, P], [1, R_HEADS]])
                               ).then_inc(s_dec_in, 16)
            for a in range(2):
                store_mod_rows(a)
                load_ada_rows(a + 2)
            for r in range(ROWS):
                for i in range(ROWS):
                    src = bass.AP(rpb_rev.tensor, (i - r + 7) * 31 - 48, [[1, GRID_W], [15 * 31, HEADS], [1, GRID_W]])
                    dst = A(A_Q + (r // 2) * 2048, HEADS, ROWS, GRID_W)[
                        GRID_W * (r % 2):GRID_W * (r % 2) + GRID_W, :, i, :]
                    pool.dma_start(dst, src).then_inc(s_bias, 16)
            for a in range(2, 5):
                store_mod_rows(a)
                load_ada_rows(a + 2)
            gate_rows = bc_gate[:, :, :].rearrange("p s d -> p (s d)")
            broadcast(gate_rows, 2, s_gate)

            def router_weights(layer):
                pool.dma_start(rw[:, :, 0:GROUPS], router_gw[layer].rearrange("(k p) n -> p k n", p=P)
                               ).then_inc(s_rw, 16)
                pool.dma_start(rw[:, :, GROUPS:36], router_ew[layer].rearrange("(k p) n -> p k n", p=P)
                               ).then_inc(s_rw, 16)
                pool.dma_start(rb[:, 0:GROUPS], bass.AP(router_gb.tensor, layer * GROUPS, [[0, P], [1, GROUPS]])
                               ).then_inc(s_rw, 16)
                pool.dma_start(rb[:, GROUPS:36], bass.AP(router_eb.tensor, layer * EXPERTS, [[0, P], [1, EXPERTS]])
                               ).then_inc(s_rw, 16)

            step(pool.memset(table[:, :], NO_ID))
            for layer in range(2):
                for m in range(TILES[layer]):
                    pool.dma_start(table_d[layer][m * P * EXPERTS:(m + 1) * P * EXPERTS, :].rearrange(
                        "(p n) a -> p (n a)", p=P), table[:, :]).then_inc(s_table_clear if layer else s_scat[m], 16)
            router_weights(0)

            def scale_and_shift(layer):
                if layer == 0:
                    taken(pool, job("s", 4 * HEADS - 1))
                else:
                    done(pool, job("ryT", R_HEADS - 1, 1))
                broadcast(A(A_BCA, 2 * D), 6 * layer + 4, s_ab)
                broadcast(A(A_BCB, 2 * D), 6 * layer + 3, s_ab)

            def second_gate(layer):
                pool.wait_ge(s_mixed, 4 if layer == 0 else 6)
                broadcast(gate_rows, 6 * layer + 5, s_gate)

            def store_h2(layer, t):
                pool.wait_ge(s_h2, (0 if layer == 0 else 4) + t + 1)
                pool.dma_start(h2_d[layer][t * P:(t + 1) * P, :], A(A_H2[layer] + t * D, D)).then_inc(s_h2_out, 16)

            def experts(layer):
                nt = TILES[layer]
                n0 = job("moe", layer)
                rows_out = nt * P * 4
                done(pool, job("rT", layer, nt - 1, 1))
                pool.wait_ge(s_h2_out, 64 if layer == 0 else 96)
                pool.wait_ge(s_idx, layer + 1)

                def gather(expert, u, copies):
                    pool.tensor_copy(gnow[:, u:u + 1], gidx[:, bass.ds(expert, 1)]).then_inc(s_now, 1)
                    pool.wait_ge(s_now, copies)
                    pool.sem_inc(s_pool_seen, 1)
                    pool.indirect_dma_start(
                        A(A_XG + u * D, D)[0:SLOTS, :], None, h2_d[layer],
                        bass.IndirectOffsetOnAxis(gnow[:, u:u + 1], 0),
                        bounds_check=nt * P - 1, oob_is_err=False).then_inc(s_gath[u], 16)

                def scatter(expert, u, turn, copies):
                    taken(pool, n0 + PER_EXPERT * u + 3, turn)
                    pool.tensor_copy(snow[:, u:u + 1], sidx[:, bass.ds(expert, 1)]).then_inc(s_now, 1)
                    pool.wait_ge(s_now, copies)
                    pool.sem_inc(s_pool_seen, 1)
                    pool.indirect_dma_start(
                        y_d[layer], bass.IndirectOffsetOnAxis(snow[:, u:u + 1], 0),
                        A(A_YS + u * 512, 512), None,
                        bounds_check=rows_out - 1, oob_is_err=False).then_inc(s_scat[u], 16)

                base = layer * 2 * EXPERTS
                for u in range(EPI):
                    gather(u, u, base + u + 1)
                base += EPI
                if layer == 0:
                    store_mod_rows(11)
                second_gate(layer)
                with pool.Fori(0, TURNS - 1) as it:
                    for u in range(EPI):
                        scatter(it * EPI + u, u, it, it * 2 * EPI + (base + 2 * u + 1))
                        gather(it * EPI + (EPI + u), u, it * 2 * EPI + (base + 2 * u + 2))
                base += (TURNS - 1) * 2 * EPI
                for u in range(EPI):
                    scatter(EXPERTS - EPI + u, u, TURNS - 1, base + u + 1)
                for u in range(EPI):
                    pool.wait_ge(s_scat[u], 16 * (TURNS * (layer + 1) + 1))

            def overflow(layer):
                nt = TILES[layer]
                pool.wait_ge(s_idx, layer + 1)
                count = pool.value_load(fullest[0:1, 0:1], min_val=0, max_val=4 * P)
                passes = nt * P // SLOTS - 1
                with pool.If(count > SLOTS):
                    pool.wait_ge(s_addr, layer + 1)
                    pool.wait_ge(s_table_clear, 16 * TILES[1])
                    for t in range(nt):
                        for k in range(2):
                            pool.indirect_dma_start(table_d[layer], bass.IndirectOffsetOnAxis(addr[:, k, t:t + 1], 0),
                                                    table[:, 4 * k + t:4 * k + t + 1], None,
                                                    bounds_check=nt * P * EXPERTS - 1, oob_is_err=False
                                                    ).then_inc(ov[layer, "set"], 16)
                    pool.wait_ge(ov[layer, "set"], 16 * 2 * nt)
                    with pool.Fori(0, passes) as b:
                        with pool.Fori(0, EXPERTS) as e:
                            n = b * EXPERTS + e
                            for half in range(2):
                                pool.dma_start(
                                    ov_table[half * SLOTS:(half + 1) * SLOTS, :],
                                    table_d[layer].rearrange("(r e) a -> r (e a)", e=EXPERTS)[
                                        bass.ds(b * SLOTS + SLOTS, SLOTS), bass.ds(e, 1)],
                                    allow_slow_non_contiguous=True).then_inc(ov[layer, "ix"], 16)
                            pool.wait_ge(ov[layer, "idx"], n + 1)
                            pool.sem_inc(s_pool_seen, 1)
                            pool.indirect_dma_start(A(A_XG, D)[0:SLOTS, :], None, h2_d[layer],
                                                    bass.IndirectOffsetOnAxis(ov_idx[0:SLOTS, 0:1], 0),
                                                    bounds_check=nt * P - 1, oob_is_err=False
                                                    ).then_inc(ov[layer, "g"], 16)
                            pool.wait_ge(ov[layer, "a4"], n + 1)
                            pool.sem_inc(s_pool_seen, 1)
                            pool.indirect_dma_start(y_d[layer], bass.IndirectOffsetOnAxis(ov_idx[:, 1:2], 0),
                                                    A(A_YS, 512), None,
                                                    bounds_check=nt * P * 4 - 1, oob_is_err=False
                                                    ).then_inc(ov[layer, "scat"], 16)
                            pool.wait_ge(ov[layer, "scat"], n * 16 + 16)
                            pool.sem_inc(s_pool_seen, 1)

            for a in range(5, 8):
                store_mod_rows(a)
                load_ada_rows(a + 2)
            scale_and_shift(0)
            for a in range(8, 10):
                store_mod_rows(a)
                load_ada_rows(a + 2)
            for t in range(TILES[0]):
                store_h2(0, t)
            store_mod_rows(10)
            experts(0)
            overflow(0)
            pool.dma_start(A(A_ROPE, 4 * SEQ), ret_c[:, 10 * SEQ:RET_N]).then_inc(s_rope_in, 16)
            pool.wait_ge(s_comb, 4)
            pool.dma_start(A(A_RTAB, 10 * SEQ), ret_c[:, 0:10 * SEQ]).then_inc(s_ret_in, 16)
            broadcast(gate_rows, 8, s_gate)
            router_weights(1)
            scale_and_shift(1)
            store_h2(1, 0)
            store_h2(1, 1)
            experts(1)
            overflow(1)
            pool.wait_ge(s_comb, 6)
            pool.dma_start(A(A_BCA, D), bass.AP(final_g.tensor, 0, [[0, P], [1, D]])).then_inc(s_fin_g, 16)

        @block.scalar
        def _(act):
            act.wait_ge(s_c, 32)
            act.activation(csil, crow, ACT.Silu).then_inc(s_csil, 1)

            act.wait_ge(s_dec_in, 32)
            act.activation(dec[:, 8:16], dec[:, 0:8], ACT.Exp).then_inc(s_dec, 1)
            act.wait_ge(s_dec, 2)
            act.activation(dec[:, 24:32], dec[:, 16:24], ACT.Ln).then_inc(s_dec, 1)

            ms_count = [0]
            root_count = [0]

            def mean_squares(tiles, squares, wait=None):
                for t in tiles:
                    if wait:
                        wait(t)
                    act.activation(squares, res[:, t, :], ACT.Square, accum_out=stat[:, 0, t:t + 1]).then_inc(s_ms, 1)
                    ms_count[0] += 1
                    act.wait_ge(s_ms, ms_count[0])

            def roots(a, b):
                root_count[0] += 1
                act.wait_ge(s_rstd, root_count[0])
                act.activation(stat[:, 1, a:b], stat[:, 0, a:b], ACT.Sqrt).then_inc(s_root, 1)

            idle_hT = hT[:, 4:6, :].rearrange("p a b -> p (a b)")
            act.wait_ge(s_x, 32)
            mean_squares(range(4), idle_hT)
            roots(0, 4)

            def turn_rows(layer, tiles):
                for t in tiles:
                    n = job("hT", layer, t, 0)
                    taken(act, job("modT", layer, 1))
                    done(act, n)
                    s = t // 2
                    for k in range(4):
                        ins = act.activation(hT[:, k, t * P:(t + 1) * P], bank(n)[:, k * P:(k + 1) * P], ACT.Identity,
                                             bias=modT[:, layer, 0, k, s:s + 1], scale=modT[:, layer, 1, k, s:s + 1])
                    ins.then_inc(free_s[n % BANKS], 1)

            turn_rows(0, range(4))
            for ch in range(4):
                n = job("ac", ch)
                done(act, n)
                if ch:
                    taken(act, job("ax", ch - 1))
                act.activation(A(A_CONV, 512), bank(n)[:, :], ACT.Copy).then_inc(free_s[n % BANKS], 1)
            act.wait_ge(s_bias_ready, 1)
            for ch in range(4):
                n = job("q", ch)
                done(act, n)
                act.activation(A(A_Q, 4, 512)[:, ch, :], bank(n)[:, :], ACT.Copy).then_inc(free_s[n % BANKS], 1)
            for ch in range(4):
                n = job("k", ch)
                done(act, n)
                act.activation(A(A_K, 4, 512)[:, ch, :], bank(n)[:, :], ACT.Copy).then_inc(free_s[n % BANKS], 1)
            for t in range(4):
                n = job("v", t)
                done(act, n)
                act.activation(A(A_V, 4, 512)[:, t, :], bank(n)[:, :], ACT.Copy).then_inc(free_s[n % BANKS], 1)

            def turned(i):
                n = job("pt", i)
                h, qt = divmod(i, 4)
                keys = 4 if qt < 2 else 2
                done(act, n)
                act.activation(A(A_PT + (i // 2 % 2) * 1024, 4, SEQ)[:, 0:keys, (qt % 2) * P:(qt % 2 + 1) * P],
                               bank(n)[:, 0:keys * P].rearrange("p (k q) -> p k q", q=P), ACT.Copy
                               ).then_inc(free_s[n % BANKS], 1)

            for i in range(ITEMS):
                p, s0 = probs(i), 4 * (i % 4)
                act.wait_ge(s_max, i + 1)
                act.activation(p, p, ACT.Exp, bias=soft[:, s0:s0 + 1], accum_out=soft[:, s0 + 1:s0 + 2]
                               ).then_inc(s_exp, 1)
                if i:
                    turned(i - 1)
            turned(ITEMS - 1)

            def expert_rows_turned(layer):
                nt = TILES[layer]
                base = 0 if layer == 0 else 4
                for tiles in NORM2_GROUPS[layer]:
                    mean_squares(tiles, A(A_SQUARES, D), wait=lambda t: act.wait_ge(s_mixed, base + t + 1))
                    roots(tiles[0], tiles[-1] + 1)
                for t in range(nt):
                    n = job("rT", layer, t, 0)
                    done(act, n)
                    act.activation(hT[:, 0:4, t * P:(t + 1) * P],
                                   bank(n)[:, :].rearrange("p (k q) -> p k q", q=P), ACT.Copy
                                   ).then_inc(free_s[n % BANKS], 1)
                for k in range(2):
                    act.wait_ge(s_gap, 2 * layer + k + 1)
                    src, dst = ((A_ROUTE + 1408, A_ROUTE + 1424), (A_ROUTE + 1500, A_ROUTE + 1504))[k]
                    w = (nt * GROUPS, nt)[k]
                    act.activation(A(dst, w), A(src, w), ACT.Exp).then_inc(s_rexp, 1)

            def experts(layer):
                n0 = job("moe", layer)
                with act.Fori(0, TURNS) as it:
                    for u in range(EPI):
                        n = n0 + PER_EXPERT * u
                        b = u % 2
                        done(act, n, it)
                        act.activation(A(A_XGT + b * 512, 512), bank(n)[:, :], ACT.Copy).then_inc(free_s[n % BANKS], 1)
                        done(act, n + 1, it)
                        act.activation(A(A_SL + b * 256, 256)[0:SLOTS, :], bank(n + 1)[0:SLOTS, 0:HIDDEN], ACT.Silu
                                       ).then_inc(s_silu, 1)
                        done(act, n + 2, it)
                        act.activation(A(A_HIDT + b * 128, 128), bank(n + 2)[:, 0:2 * SLOTS], ACT.Copy
                                       ).then_inc(free_s[(n + 2) % BANKS], 1)

            def overflow(layer):
                act.wait_ge(s_idx, layer + 1)
                count = act.value_load(fullest[0:1, 0:1], min_val=0, max_val=4 * P)
                o = lambda k: ov[layer, k]
                with act.If(count > SLOTS):
                    for u in range(EPI):
                        act.wait_ge(s_scat[u], 16 * (TURNS * (layer + 1) + 1))
                    with act.Fori(0, (TILES[layer] * P // SLOTS - 1) * EXPERTS) as n:
                        act.wait_ge(o("p1"), n + 1)
                        act.activation(A(A_XGT, 512), banks[0][:, :], ACT.Copy).then_inc(o("a1"), 1)
                        act.wait_ge(o("p2"), n + 1)
                        act.activation(A(A_SL, 256)[0:SLOTS, :], banks[1][0:SLOTS, 0:HIDDEN], ACT.Silu
                                       ).then_inc(o("a2"), 1)
                        act.wait_ge(o("p3"), n + 1)
                        act.activation(A(A_HIDT, 128), banks[2][:, 0:2 * SLOTS], ACT.Copy).then_inc(o("a3"), 1)
                        act.wait_ge(o("y"), n + 2)
                        act.activation(A(A_YS, 512), banks[3][:, :], ACT.Copy).then_inc(o("a4"), 1)

            expert_rows_turned(0)
            experts(0)
            overflow(0)

            def weigh_first(layer, t):
                act.wait_ge(s_y_in[t], 16 * (layer + 1))
                y = A(A_XG + t * 2 * D, D)
                act.activation(y, y, ACT.Copy, scale=gates[:, 0, t:t + 1]).then_inc(s_first, 1)

            def combined(base):
                return lambda t: act.wait_ge(s_comb, base + t + 1)

            for t in range(3):
                weigh_first(0, t)
            squares = A(A_RG_ODD, D)
            mean_squares(range(2), squares, combined(0))
            roots(0, 2)
            weigh_first(0, 3)
            turn_rows(1, range(2))
            mean_squares(range(2, 4), squares, combined(0))
            roots(2, 4)

            def silu_gate(h):
                for t in range(2):
                    n = job("rg", h, t)
                    done(act, n)
                    act.activation(ret_gate(h)[:, t, :], bank(n)[:, :], ACT.Silu).then_inc(free_s[n % BANKS], 1)

            silu_gate(0)
            turn_rows(1, range(2, 4))

            acts = [0]

            def mark(ins):
                acts[0] += 1
                ins.then_inc(s_rexps, 1)

            tab = lambda k: A(A_RTAB + 512 * k, 512)
            for h in range(R_HEADS):
                for ch in range(2):
                    n = job("rk", h, ch)
                    done(act, n)
                    act.activation(A(A_RK, 2, 512)[:, ch, SEQ:512], bank(n)[:, SEQ:512], ACT.Copy).then_inc(s_ctx_keys, 1)
                if h == 0:
                    act.wait_ge(s_ret_in, 16)
                    act.wait_ge(s_dec, 6)
                else:
                    done(act, job("ro", h - 1, 1))
                    act.wait_ge(s_yms, 2 * h)
                mark(act.activation(A(A_RD, 512), tab(1), ACT.Exp, scale=dec[:, 24 + h:25 + h]))
                mark(act.activation(A(A_EXP, 512), tab(2), ACT.Exp, scale=dec[:, 28 + h:29 + h]))
                act.wait_ge(s_factors, 2 * h + 1)
                mark(act.activation(A(A_RD + 512, 512), tab(0), ACT.Exp, scale=dec[:, 24 + h:25 + h],
                                    bias=dec[:, 32 + h:33 + h]))
                mark(act.activation(A(A_EXP, 512), tab(0), ACT.Exp, scale=dec[:, h:h + 1],
                                    bias=dec[:, 36 + h:37 + h]))
                for t in range(4):
                    n = job("rv", h, t)
                    done(act, n)
                    act.activation(A(A_RV, 4, 512)[:, t, :], bank(n)[:, :], ACT.Copy).then_inc(free_s[n % BANKS], 1)
                for t in range(2):
                    i = 2 * h + t
                    n = job("ro", h, t)
                    done(act, n)
                    if t:
                        act.wait_ge(s_yms, i)
                    act.activation(A(A_EXP, 512), bank(n)[:, :], ACT.Square, accum_out=soft[:, t:t + 1]).then_inc(s_yms, 1)
                    act.wait_ge(s_yroot, 2 * i + 1)
                    act.activation(soft[:, 4 + t:5 + t], soft[:, 2 + t:3 + t], ACT.Sqrt).then_inc(s_yroot, 1)
                if h + 1 < R_HEADS:
                    silu_gate(h + 1)
                for t in range(2):
                    n = job("ryT", h, t)
                    done(act, n)
                    act.activation(A(A_RY, 16, SEQ)[:, 4 * h:4 * h + 4, t * P:(t + 1) * P],
                                   bank(n)[:, :].rearrange("p (k q) -> p k q", q=P), ACT.Copy
                                   ).then_inc(free_s[n % BANKS], 1)
            expert_rows_turned(1)
            experts(1)
            overflow(1)
            for t in range(2):
                weigh_first(1, t)
            for t in range(2):
                mean_squares([t], idle_hT, combined(4))
                roots(t, t + 1)

        @block.tensor
        def _(pe):
            def product(n, where, pairs, start=True, last=True, mark=True):
                for i, (stationary, moving) in enumerate(pairs):
                    ins = pe.matmul(where, stationary, moving, start=(start and i == 0), stop=(last and i == len(pairs) - 1))
                if mark:
                    ins.then_inc(full_s[n % BANKS], 1)

            def turn(n, to, what, size, mark):
                ins = pe.transpose(to, what, ident[0:size, 0:size])
                if mark:
                    ins.then_inc(full_s[n % BANKS], 1)

            pe.wait_ge(s_con, 16)
            pe.wait_ge(s_csil, 1)
            n = job("cT")
            turn(n, bank(n)[:, 0:16], csil, 16, True)
            n = job("cwT")
            pe.wait_ge(s_cw, 16)
            turn(n, bank(n)[:, 0:12], cwrow, 12, True)

            def ada(layer, q):
                u0 = ada_units(layer, q)
                n = job("ada", layer, q)
                begin(pe, n)
                for j in range(4):
                    arrived(pe, u0 + j)
                for k in range(KC):
                    for j in range(4):
                        ins = pe.matmul(bank(n)[32 * j:32 * j + 32, 0:256], cvec[:, k, :],
                                        unit(u0 + j)[:, 256 * k:256 * k + 256], start=(k == 0), stop=(k == KC - 1))
                ins.then_inc(full_s[n % BANKS], 1)

            def mod_turn(layer, q):
                a = 6 * layer + q
                n = job("modT", layer, q)
                begin(pe, n)
                taken(pe, job("ada", layer, q))
                for half in range(2):
                    turn(n, bank(n)[:, half * P:(half + 1) * P], mod_rows[:, a % 2, half * P:(half + 1) * P], P, half == 1)

            taken(pe, job("cT"))
            for q in range(2):
                ada(0, q)
            for q in range(2):
                mod_turn(0, q)

            def turn_rows(layer, tiles):
                for t in tiles:
                    pe.wait_ge(s_xn, 4 * layer + t + 1)
                    for half in range(2):
                        n = job("hT", layer, t, half)
                        begin(pe, n)
                        xn = A((A_XN, A_XN1)[layer] + (t % 2) * D, D)
                        for k in range(4):
                            turn(n, bank(n)[:, k * P:(k + 1) * P], xn[:, (4 * half + k) * P:(4 * half + k + 1) * P], P, k == 3)

            def rows_ready(layer, tiles):
                for t in tiles:
                    for half in range(2):
                        taken(pe, job("hT", layer, t, half))

            turn_rows(0, range(4))
            rows_ready(0, range(4))

            def w_cols(n, k, c0, w):
                return unit(n)[:, 256 * k + c0:256 * k + c0 + w]

            for ch in range(4):
                u0 = U_WIN_E + 3 * (ch // 2)
                for name, m in (("ac", 1), ("ax", 2), ("ab", 0)):
                    n = job(name, ch)
                    begin(pe, n)
                    arrived(pe, u0 + m)
                    product(n, bank(n)[:, :], [(w_cols(u0 + m, k, P * (ch % 2), P), hT[:, k, :]) for k in range(KC)])
            for name, u0 in (("q", U_WIN_E + 6), ("k", U_WIN_E + 8)):
                for ch in range(4):
                    n = job(name, ch)
                    begin(pe, n)
                    arrived(pe, u0 + ch // 2)
                    product(n, bank(n)[:, :], [(w_cols(u0 + ch // 2, k, P * (ch % 2), P), hT[:, k, :]) for k in range(KC)])

            def two_units(u0, k):
                a = u0 % RING
                return ring[:, a:a + 2, 256 * k:256 * k + 256]

            for t in range(4):
                n = job("v", t)
                begin(pe, n)
                for m in range(2):
                    arrived(pe, U_WIN_E + 10 + m)
                product(n, bank(n)[:, :], [(hT[:, k, t * P:(t + 1) * P], two_units(U_WIN_E + 10, k)) for k in range(KC)])

            def scores(i):
                h, qt = divmod(i, 4)
                b = HEAD_DIM * (h % 2)
                n = job("s", i)
                begin(pe, n)
                k0 = 0 if qt < 2 else SEQ
                product(n, bank(n)[:, 0:512 - k0],
                        [(A(A_Q, 4, 512)[b:b + HEAD_DIM, h // 2, qt * P:(qt + 1) * P],
                          A(A_K, 4, 512)[b:b + HEAD_DIM, h // 2, k0:512])])

            def turn_probs(i):
                n = job("pt", i)
                begin(pe, n)
                pe.wait_ge(s_probs, i + 1)
                keys = 4 if i % 4 < 2 else 2
                for k in range(keys):
                    turn(n, bank(n)[:, k * P:(k + 1) * P], probs(i)[:, k * P:(k + 1) * P], P, k == keys - 1)

            def mix_values(j):
                h, s = divmod(j, 2)
                n = job("pv", j)
                begin(pe, n)
                taken(pe, job("pt", 2 * j))
                taken(pe, job("pt", 2 * j + 1))
                b = HEAD_DIM * (h % 2)
                kts = range(4) if s == 0 else range(2, 4)
                product(n, bank(n)[b:b + HEAD_DIM, 0:SEQ],
                        [(A(A_V, 4, 512)[:, kt, h * HEAD_DIM:(h + 1) * HEAD_DIM],
                          A(A_PT + (j % 2) * 1024, 4, SEQ)[:, kt - kts[0], :]) for kt in kts])

            for ch in range(4):
                taken(pe, job("q", ch))
                taken(pe, job("k", ch))
                taken(pe, job("v", ch))
            for i in range(3):
                scores(i)
            for i in range(ITEMS):
                if i + 3 < ITEMS:
                    scores(i + 3)
                turn_probs(i)
                if i % 2 and i > 1:
                    mix_values((i - 3) // 2)
                if i in AFTER_ITEM:
                    ada(*AFTER_ITEM[i])
            mix_values(ITEMS // 2 - 1)
            for q in range(2):
                mod_turn(1, q)

            def mixed(k):
                return A(A_YC, 4, 512)[:, k, :] if k < 4 else hT[:, k - 4, :]

            def project_out(layer, i, u0, source, chunks, last=True):
                t, half = divmod(i, 2)
                n = job("wo", layer, t, half)
                if chunks[0] == 0:
                    begin(pe, n)
                for m in range(chunks[0] // 2, (chunks[-1] + 1) // 2):
                    arrived(pe, u0 + m)
                product(n, bank(n)[:, :],
                        [(source(k)[:, t * P:(t + 1) * P],
                          unit(u0 + k // 2)[:, D * (k % 2) + 512 * half:D * (k % 2) + 512 * half + 512])
                         for k in chunks], start=chunks[0] == 0, last=last, mark=last)

            for ch in range(4):
                taken(pe, job("ab", ch))
            for j in range(2 * HEADS):
                taken(pe, job("pv", j))
            for i in range(8):
                project_out(0, i, U_WOUT_E, mixed, range(8))
                if i in AFTER_WO:
                    ada(*AFTER_WO[i])

            def route(layer):
                nt = TILES[layer]
                for t in range(nt):
                    pe.wait_ge(s_h2, (0 if layer == 0 else 4) + t + 1)
                    for half in range(2):
                        n = job("rT", layer, t, half)
                        begin(pe, n)
                        for k in range(4):
                            at = (4 * half + k) * P
                            turn(n, bank(n)[:, k * P:(k + 1) * P], A(A_H2[layer] + t * D, D)[:, at:at + P], P, k == 3)
                    if layer == 0 and t == 1:
                        ada(1, 4)
                n = job("logits", layer)
                begin(pe, n)
                pe.wait_ge(s_rw, 64 * (layer + 1))
                for t in range(nt):
                    for half in range(2):
                        taken(pe, job("rT", layer, t, half))
                for t in range(nt):
                    product(n, bank(n)[:, 64 * t:64 * t + 36],
                            [(hT[:, k, t * P:(t + 1) * P], rw[:, k, :]) for k in range(KC)], mark=(t == nt - 1))
                n = job("ranks", layer)
                begin(pe, n)
                pe.wait_ge(s_members, layer + 1)
                member = A(A_ROUTE + 640, 5 * EXPERTS)
                w = (nt + 1) * EXPERTS
                product(n, bank(n)[:, 0:w], [(const("upper"), member[:, 0:w])], last=False, mark=False)
                for back in range(1, nt + 1):
                    product(n, bank(n)[:, EXPERTS * back:w], [(const("ones"), member[:, 0:w - EXPERTS * back])],
                            start=False, last=back == nt, mark=back == nt)
                n = job("table", layer)
                begin(pe, n)
                pe.wait_ge(s_hot, layer + 1)
                hot, valued = A(A_HOT, 8, SLOTS), A(A_VALUED, 8, EXPERTS)
                for i in range(2 * nt):
                    for half in range(2):
                        at = 4 * (i // nt) + i % nt
                        ins = pe.matmul(bank(n)[SLOTS * half:SLOTS * (half + 1), 0:EXPERTS], hot[:, at, :],
                                        valued[:, at, :], start=(i == 0), stop=(i == 2 * nt - 1))
                ins.then_inc(full_s[n % BANKS], 1)
                if layer == 0:
                    ada(1, 5)

            def experts(layer):
                n0 = job("moe", layer)
                u0 = (U_MOE0, U_MOE1)[layer]
                with pe.Fori(0, TURNS) as it:
                    for u in range(EPI):
                        n = n0 + PER_EXPERT * u
                        b = u % 2
                        begin(pe, n, it)
                        pe.wait_ge(s_gath[u], it * 16 + 16 * (TURNS * layer + 1))
                        pe.sem_inc(s_pe_seen, 1)
                        for k in range(KC):
                            turn(n, bank(n)[:, SLOTS * k:SLOTS * (k + 1)],
                                 A(A_XG + u * D, D)[0:SLOTS, k * P:(k + 1) * P], SLOTS, k == KC - 1)
                        begin(pe, n + 1, it)
                        arrived(pe, u0 + 3 * u, it)
                        arrived(pe, u0 + 3 * u + 1, it)
                        taken(pe, n, it)
                        for k in range(KC):
                            for w in range(2):
                                ins = pe.matmul(bank(n + 1)[SLOTS * w:SLOTS * (w + 1), 0:HIDDEN],
                                                A(A_XGT + b * 512 + SLOTS * k, SLOTS),
                                                unit(u0 + 3 * u + w)[:, 256 * k:256 * (k + 1)],
                                                start=(k == 0), stop=(k == KC - 1))
                        ins.then_inc(full_s[(n + 1) % BANKS], 1)
                        begin(pe, n + 2, it)
                        taken(pe, n + 1, it)
                        pe.sem_inc(s_pe_seen, 1)
                        for k in range(2):
                            turn(n + 2, bank(n + 2)[:, SLOTS * k:SLOTS * (k + 1)],
                                 A(A_HID + b * 256, 256)[0:SLOTS, k * P:(k + 1) * P], SLOTS, k == 1)
                        begin(pe, n + 3, it)
                        arrived(pe, u0 + 3 * u + 2, it)
                        taken(pe, n + 2, it)
                        for k in range(2):
                            for w in range(2):
                                ins = pe.matmul(bank(n + 3)[SLOTS * w:SLOTS * (w + 1), :],
                                                A(A_HIDT + b * 128 + SLOTS * k, SLOTS),
                                                unit(u0 + 3 * u + 2)[:, D * k + 512 * w:D * k + 512 * (w + 1)],
                                                start=(k == 0), stop=(k == 1))
                        ins.then_inc(full_s[(n + 3) % BANKS], 1)

            def overflow(layer):
                n0 = job("moe", layer)
                pe.wait_ge(s_idx, layer + 1)
                count = pe.value_load(fullest[0:1, 0:1], min_val=0, max_val=4 * P)
                o = lambda k: ov[layer, k]
                total = (TILES[layer] * P // SLOTS - 1) * EXPERTS
                with pe.If(count > SLOTS):
                    for b in range(BANKS):
                        taken(pe, n0 + EXPERTS * PER_EXPERT - BANKS + b)
                    pe.nop().then_inc(o("y"), 1)
                    with pe.Fori(0, total) as n:
                        pe.wait_ge(o("g"), n * 16 + 16)
                        pe.sem_inc(s_pe_seen, 1)
                        for k in range(KC):
                            ins = pe.transpose(banks[0][:, SLOTS * k:SLOTS * (k + 1)],
                                               A(A_XG, D)[0:SLOTS, k * P:(k + 1) * P], ident[0:SLOTS, 0:SLOTS])
                        ins.then_inc(o("p1"), 1)
                        pe.wait_ge(o("w"), n * 48 + 48)
                        pe.wait_ge(o("a1"), n + 1)
                        for k in range(KC):
                            for w in range(2):
                                ins = pe.matmul(banks[1][SLOTS * w:SLOTS * (w + 1), 0:HIDDEN],
                                                A(A_XGT + SLOTS * k, SLOTS), unit(w)[:, 256 * k:256 * (k + 1)],
                                                start=(k == 0), stop=(k == KC - 1))
                        ins.then_inc(o("p2"), 1)
                        pe.wait_ge(o("d2"), n + 1)
                        pe.sem_inc(s_pe_seen, 1)
                        for k in range(2):
                            ins = pe.transpose(banks[2][:, SLOTS * k:SLOTS * (k + 1)],
                                               A(A_HID, 256)[0:SLOTS, k * P:(k + 1) * P], ident[0:SLOTS, 0:SLOTS])
                        ins.then_inc(o("p3"), 1)
                        pe.wait_ge(o("a3"), n + 1)
                        for k in range(2):
                            for w in range(2):
                                ins = pe.matmul(banks[3][SLOTS * w:SLOTS * (w + 1), :], A(A_HIDT + SLOTS * k, SLOTS),
                                                unit(2)[:, D * k + 512 * w:D * k + 512 * (w + 1)],
                                                start=(k == 0), stop=(k == 1))
                        ins.then_inc(o("y"), 1)
                        pe.wait_ge(o("a4"), n + 1)

            route(0)
            experts(0)
            overflow(0)
            def ret_q(h):
                u = U_WIN_O + 6 * h + 2
                n = job("rq", h)
                begin(pe, n)
                arrived(pe, u)
                for ch in range(2):
                    product(n, bank(n)[:, SEQ * ch:SEQ * (ch + 1)],
                            [(w_cols(u, k, P * ch, P), hT[:, k, 0:SEQ]) for k in range(KC)], mark=(ch == 1))

            def ret_g(h):
                u = U_WIN_O + 6 * h
                for m in range(2):
                    arrived(pe, u + m)
                for t in range(2):
                    n = job("rg", h, t)
                    begin(pe, n)
                    product(n, bank(n)[:, :], [(hT[:, k, t * P:(t + 1) * P], two_units(u, k)) for k in range(KC)])

            turn_rows(1, range(2))
            rows_ready(1, range(2))
            ret_q(0)
            ret_g(0)
            turn_rows(1, range(2, 4))
            rows_ready(1, range(2, 4))
            turned_out = lambda k: A(A_RY, 16, SEQ)[:, k, :]
            for h in range(R_HEADS):
                u0 = U_WIN_O + 6 * h
                arrived(pe, u0 + 5)
                for ch in range(2):
                    n = job("rk", h, ch)
                    begin(pe, n)
                    product(n, bank(n)[:, :], [(w_cols(u0 + 5, k, P * ch, P), hT[:, k, :]) for k in range(KC)])
                for m in range(2):
                    arrived(pe, u0 + 3 + m)
                for t in range(4):
                    n = job("rv", h, t)
                    begin(pe, n)
                    product(n, bank(n)[:, :], [(hT[:, k, t * P:(t + 1) * P], two_units(u0 + 3, k)) for k in range(KC)])
                taken(pe, job("rq", h))
                for ch in range(2):
                    taken(pe, job("rk", h, ch))
                pe.wait_ge(s_ctx_keys, 2 * (h + 1))
                for a in range(2):
                    n = job("rs", h, a)
                    begin(pe, n)
                    for b in range(2):
                        kt = 2 * a + b
                        product(n, bank(n)[:, SEQ * b:SEQ * (b + 1)],
                                [(A(A_RK, 2, 512)[:, ch, kt * P:(kt + 1) * P], A(A_RQ, 2, SEQ)[:, ch, :])
                                 for ch in range(2)], mark=(b == 1))
                if h + 1 < R_HEADS:
                    ret_q(h + 1)
                for t in range(4):
                    taken(pe, job("rv", h, t))
                for a in range(2):
                    taken(pe, job("rs", h, a))
                for t in range(2):
                    n = job("ro", h, t)
                    begin(pe, n)
                    product(n, bank(n)[:, :], [(A(A_RD, 4, SEQ)[:, kt, t * P:(t + 1) * P], A(A_RV, 4, 512)[:, kt, :])
                                               for kt in range(4)])
                if h + 1 < R_HEADS:
                    ret_g(h + 1)
                else:
                    for hh in range(h):
                        for t in range(2):
                            taken(pe, job("ryT", hh, t))
                    project_out(1, 0, U_WOUT_O, turned_out, range(12), last=False)
                for t in range(2):
                    n = job("ryT", h, t)
                    begin(pe, n)
                    taken(pe, job("ro", h, t))
                    for k in range(4):
                        turn(n, bank(n)[:, k * P:(k + 1) * P], ret_gate(h)[:, t, k * P:(k + 1) * P], P, k == 3)
            for t in range(2):
                taken(pe, job("ryT", R_HEADS - 1, t))
            project_out(1, 0, U_WOUT_O, turned_out, range(12, 16))
            for i in range(1, 4):
                project_out(1, i, U_WOUT_O, turned_out, range(16))
            route(1)
            experts(1)
            overflow(1)

        @block.vector
        def _(dve):
            steps = [0]

            def step(ins):
                steps[0] += 1
                ins.then_inc(s_dve, 1)
                dve.wait_ge(s_dve, steps[0])

            tt, ts, stt = dve.tensor_tensor, dve.tensor_scalar, dve.scalar_tensor_tensor

            dve.wait_ge(s_zero, 2)
            n = job("cT")
            done(dve, n)
            dve.tensor_copy(cvec[:, :, 0:2], bank(n)[:, 0:16].rearrange("p (s k) -> p k s", s=2)).then_inc(free_s[n % BANKS], 1)
            n = job("cwT")
            done(dve, n)
            dve.tensor_copy(cwT[:, :], bank(n)[:, 0:12]).then_inc(free_s[n % BANKS], 1)
            taken(dve, n)

            dve.wait_ge(s_dec, 1)
            ts(dec[:, 16:24], dec[:, 8:16], -1.0, 1.0, ALU.mult, ALU.add).then_inc(s_dec, 1)
            dve.wait_ge(s_dec, 3)
            step(ts(dec[:, 32:40], dec[:, 16:24], -1.0, 1.0, ALU.mult, ALU.add))
            step(ts(dec[:, 32:40], dec[:, 32:40], 1.0e-30, None, ALU.max))
            step(dve.reciprocal(dec[:, 32:40], dec[:, 32:40]))
            step(tt(dec[:, 32:40], dec[:, 32:40], dec[:, 8:16], ALU.mult))
            tt(dec[:, 24:32], dec[:, 24:32], dec[:, 32:40], ALU.mult).then_inc(s_dec, 1)
            dve.wait_ge(s_dec, 4)
            ts(dec[:, 32:40], dec[:, 24:32], float(SEQ), None, ALU.mult).then_inc(s_dec, 1)
            ts(dec[:, 0:4], dec[:, 28:32], -1.0, None, ALU.mult).then_inc(s_dec, 1)

            ms_count = [0]
            root_count = [0]

            def reciprocal_roots(a, b):
                ms_count[0] += b - a
                root_count[0] += 1
                dve.wait_ge(s_ms, ms_count[0])
                ts(stat[:, 0, a:b], stat[:, 0, a:b], 1.0 / D, EPS, ALU.mult, ALU.add).then_inc(s_rstd, 1)
                dve.wait_ge(s_root, root_count[0])
                step(dve.reciprocal(stat[:, 2, a:b], stat[:, 1, a:b]))
                step(tt(stat[:, 1, a:b], stat[:, 2, a:b], stat[:, 2, a:b], ALU.mult))
                step(tt(stat[:, 1, a:b], stat[:, 1, a:b], stat[:, 0, a:b], ALU.mult))
                step(ts(stat[:, 1, a:b], stat[:, 1, a:b], -0.5, 1.5, ALU.mult, ALU.add))
                step(tt(stat[:, 2, a:b], stat[:, 2, a:b], stat[:, 1, a:b], ALU.mult))

            reciprocal_roots(0, 4)

            def mod_block(layer, q):
                a = 6 * layer + q
                n = job("ada", layer, q)
                rows = mod_rows[:, a % 2, :]
                bias = ada_rows[:, a % 2, 0, :]
                done(dve, n)
                dve.wait_ge(s_ada_in[a % 2], ada_in_value[a])
                if a >= 2 and stored_value[a - 2]:
                    dve.wait_ge(s_stored[a % 2], stored_value[a - 2])
                if q in (2, 3):
                    done(dve, job("modT", layer, q - 2))
                if q in (1, 4):
                    step(stt(rows, bank(n)[:, 0:256], 1.0, bias, ALU.add, ALU.add))
                    tt(rows, rows, ada_rows[:, a % 2, 1, :], ALU.mult).then_inc(free_s[n % BANKS], 1)
                else:
                    tt(rows, bank(n)[:, 0:256], bias, ALU.add).then_inc(free_s[n % BANKS], 1)

            def mod_columns(layer, q):
                n = job("modT", layer, q)
                done(dve, n)
                dve.tensor_copy(modT[:, layer, q, :, :].rearrange("p (j h) s -> p h j s", h=2),
                                bank(n)[:, 0:256].rearrange("p (h j r) -> p h j r", h=2, j=4)[:, :, :, 0:2]
                                ).then_inc(free_s[n % BANKS], 1)

            mod_block(0, 0)
            mod_block(0, 1)
            mod_columns(0, 0)
            mod_columns(0, 1)

            def normed(layer, t):
                if t >= 2:
                    done(dve, job("hT", layer, t - 2, 1))
                ts(A((A_XN, A_XN1)[layer] + (t % 2) * D, D), res[:, t, :], stat[:, 2, t:t + 1], None, ALU.mult
                   ).then_inc(s_xn, 1)

            def turn_rows(layer, t):
                n = job("hT", layer, t, 1)
                s = t // 2
                if t == 0:
                    taken(dve, job("modT", layer, 1))
                done(dve, n)
                for k in range(4):
                    ins = ts(hT[:, 4 + k, t * P:(t + 1) * P], bank(n)[:, k * P:(k + 1) * P],
                             modT[:, layer, 1, 4 + k, s:s + 1], modT[:, layer, 0, 4 + k, s:s + 1], ALU.mult, ALU.add)
                ins.then_inc(free_s[n % BANKS], 1)

            normed(0, 0)
            normed(0, 1)
            for t in range(4):
                turn_rows(0, t)
                if t + 2 < 4:
                    normed(0, t + 2)

            padded = A(A_CONV + 512, 2, SEQ + 2)
            total = A(A_CONV + 1028, 2, SEQ)
            for t in range(4):
                done(dve, job("hT", 0, t, 1))
            step(dve.memset(padded[:, :, 0:SEQ + 2:SEQ + 1], 0.0))
            for ch in range(4):
                taken(dve, job("ac", ch))
                n = job("ax", ch)
                done(dve, n)
                tt(padded[:, :, 1:SEQ + 1], A(A_CONV, 2, SEQ), bank(n)[:, :].rearrange("p (s t) -> p s t", s=2),
                   ALU.mult).then_inc(free_s[n % BANKS], 1)
                taken(dve, n)
                step(ts(total, padded[:, :, 0:SEQ], cwT[:, ch:ch + 1], None, ALU.mult))
                step(stt(total, padded[:, :, 1:SEQ + 1], cwT[:, 4 + ch:5 + ch], total, ALU.mult, ALU.add))
                step(stt(total, padded[:, :, 2:SEQ + 2], cwT[:, 8 + ch:9 + ch], total, ALU.mult, ALU.add))
                n = job("ab", ch)
                done(dve, n)
                tt(A(A_YC, 4, 512)[:, ch, :], total.rearrange("p s t -> p (s t)"), bank(n)[:, :], ALU.mult
                   ).then_inc(free_s[n % BANKS], 1)
            dve.wait_ge(s_bias, 16 * ROWS * ROWS)
            dve.wait_ge(s_con, 16)
            for qt in range(2):
                for h in range(HEADS):
                    ins = tt(A(A_BIAS + qt * 2048, HEADS, ROWS, GRID_W)[:, h],
                             A(A_Q + qt * 2048, HEADS, ROWS, GRID_W)[:, h, :, ::-1],
                             const("window").unsqueeze(1).to_broadcast([P, ROWS, GRID_W]), ALU.add)
            ins.then_inc(s_bias_ready, 1)

            scale = float(HEAD_DIM) ** -0.5

            def attention_scores(i):
                h, qt = divmod(i, 4)
                n = job("s", i)
                p, s0 = probs(i), 4 * (i % 4)
                done(dve, n)
                if i >= 4:
                    done(dve, job("pt", i - 4))
                if qt < 2:
                    step(stt(p[:, 0:SEQ], bank(n)[:, 0:SEQ], scale,
                             A(A_BIAS + qt * 2048, HEADS, SEQ)[:, h, :], ALU.mult, ALU.add))
                    ts(p[:, SEQ:512], bank(n)[:, SEQ:512], scale, None, ALU.mult).then_inc(free_s[n % BANKS], 1)
                else:
                    ts(p, bank(n)[:, 0:SEQ], scale, None, ALU.mult).then_inc(free_s[n % BANKS], 1)
                taken(dve, n)
                dve.tensor_reduce(soft[:, s0:s0 + 1], p, AX_X, ALU.max, negate=True).then_inc(s_max, 1)

            def attention_divide(i):
                p, s0 = probs(i), 4 * (i % 4)
                dve.wait_ge(s_exp, i + 1)
                step(dve.reciprocal(soft[:, s0 + 2:s0 + 3], soft[:, s0 + 1:s0 + 2]))
                ts(p, p, soft[:, s0 + 2:s0 + 3], None, ALU.mult).then_inc(s_probs, 1)

            def head_out(j):
                h, s = divmod(j, 2)
                n = job("pv", j)
                b = HEAD_DIM * (h % 2)
                done(dve, n)
                dve.tensor_copy(hT[b:b + HEAD_DIM, h // 2, s * SEQ:(s + 1) * SEQ], bank(n)[b:b + HEAD_DIM, 0:SEQ]
                                ).then_inc(free_s[n % BANKS], 1)

            attention_scores(0)
            attention_scores(1)
            for i in range(ITEMS):
                if i + 2 < ITEMS:
                    attention_scores(i + 2)
                attention_divide(i)
                if i % 2 == 0 and i >= 4:
                    head_out(i // 2 - 2)
                if i - 2 in AFTER_ITEM:
                    mod_block(*AFTER_ITEM[i - 2])
            head_out(ITEMS // 2 - 2)
            head_out(ITEMS // 2 - 1)
            mod_columns(1, 0)
            mod_columns(1, 1)

            def add_mixer(layer, i):
                t, half = divmod(i, 2)
                n = job("wo", layer, t, half)
                done(dve, n)
                cols = slice(512 * half, 512 * half + 512)
                tmp = A(A_TMP + 512 * half, 512)
                tt(tmp, bank(n)[:, :], bc_gate[:, t // 2, cols], ALU.mult).then_inc(free_s[n % BANKS], 1)
                taken(dve, n)
                ins = tt(res[:, t, cols], res[:, t, cols], tmp, ALU.add)
                if half == 0:
                    step(ins)
                else:
                    ins.then_inc(s_mixed, 1)

            def modulated(layer, t):
                h2 = A(A_H2[layer] + t * D, D)
                step(stt(h2, res[:, t, :], stat[:, 2, t:t + 1], A(A_BCA + t // 2 * D, D), ALU.mult, ALU.mult))
                tt(h2, h2, A(A_BCB + t // 2 * D, D), ALU.add).then_inc(s_h2, 1)

            def h2_turned(layer, t):
                n = job("rT", layer, t, 1)
                done(dve, n)
                dve.tensor_copy(hT[:, 4:8, t * P:(t + 1) * P], bank(n)[:, :].rearrange("p (k q) -> p k q", q=P)
                                ).then_inc(free_s[n % BANKS], 1)

            def route(layer):
                nt = TILES[layer]
                R = A_ROUTE
                logit = A(R, 4, 36)[:, 0:nt, :]
                in_group = A(R + 160, 4, EXPERTS)[:, 0:nt, :]
                first = A(R + 288, 4, EXPERTS)[:, 0:nt, :]
                second = A(R + 416, 4, EXPERTS)[:, 0:nt, :]
                member = A(R + 640, 4, EXPERTS)[:, 0:nt, :]
                none = A(R + 640, 5, EXPERTS)[:, nt, :]
                both = A(R + 288, 8, EXPERTS).rearrange("p (k t) e -> p k t e", k=2)[:, :, 0:nt, :]
                place = A(R + 1536, 4, EXPERTS)[:, 0:nt, :]
                scratch = A(R + 1664, 8, EXPERTS).rearrange("p (k t) e -> p k t e", k=2)[:, :, 0:nt, :]
                valued = A(A_VALUED, 8, EXPERTS).rearrange("p (k t) e -> p k t e", k=2)[:, :, 0:nt, :]
                el = A(R + 1024, 4, PER_GROUP)[:, 0:nt, :]
                cand = A(R + 1056, 4, PER_GROUP)[:, 0:nt, :]
                hot1 = A(R + 1088, 4, PER_GROUP)[:, 0:nt, :]
                hot2 = A(R + 1120, 4, PER_GROUP)[:, 0:nt, :]
                hotg = A(R + 1152, 4, GROUPS)[:, 0:nt, :]
                candg = A(R + 1168, 4, GROUPS)[:, 0:nt, :]
                m0, m1, m2, m3 = (A(R + 1200 + 4 * i, 4)[:, 0:nt] for i in range(4))
                sumg, den = (A(R + 1220 + 4 * i, 4)[:, 0:nt] for i in range(2))
                rank = A(R + 1232, 2, 4)[:, :, 0:nt]
                where = A(R + 1240, 2, 4)[:, :, 0:nt]
                count = A(R + 1260, 1)
                gap = A(R + 1408, nt, GROUPS)
                eg = A(R + 1424, nt, GROUPS)
                gap2, t2 = A(R + 1500, nt), A(R + 1504, nt)

                def wide(v, k):
                    return v.unsqueeze(2).to_broadcast([P, nt, k])

                def pick(hot, cand, values, best, idx, k):
                    step(tt(cand, values, wide(best, k), ALU.is_lt))
                    step(stt(cand, cand, BIG, idx.unsqueeze(1).to_broadcast([P, nt, k]), ALU.mult, ALU.add))
                    step(dve.tensor_reduce(m3, cand, AX_X, ALU.min))
                    step(tt(hot, cand, wide(m3, k), ALU.is_equal))

                n = job("logits", layer)
                done(dve, n)
                tt(logit, bank(n)[:, 0:64 * nt].rearrange("p (t c) -> p t c", c=64)[:, :, 0:36],
                   rb[:, :].unsqueeze(1).to_broadcast([P, nt, 36]), ALU.add).then_inc(free_s[n % BANKS], 1)
                taken(dve, n)
                step(dve.tensor_reduce(m0, logit[:, :, 0:GROUPS], AX_X, ALU.max))
                tt(gap, logit[:, :, 0:GROUPS], wide(m0, GROUPS), ALU.subtract).then_inc(s_gap, 1)
                pick(hotg, candg, logit[:, :, 0:GROUPS], m0, const("idx_group"), GROUPS)
                step(tt(in_group.rearrange("p t (g e) -> p t g e", g=GROUPS),
                        logit[:, :, GROUPS:36].rearrange("p t (g e) -> p t g e", g=GROUPS),
                        hotg.unsqueeze(3).to_broadcast([P, nt, GROUPS, PER_GROUP]), ALU.mult))
                step(dve.tensor_reduce(el, in_group.rearrange("p t (g e) -> p t e g", g=GROUPS), AX_X, ALU.add))
                step(dve.tensor_reduce(m1, el, AX_X, ALU.max))
                pick(hot1, cand, el, m1, const("idx_in_group"), PER_GROUP)
                step(stt(el, hot1, -BIG, el, ALU.mult, ALU.add))
                step(dve.tensor_reduce(m2, el, AX_X, ALU.max))
                tt(gap2, m2, m1, ALU.subtract).then_inc(s_gap, 1)
                pick(hot2, cand, el, m2, const("idx_in_group"), PER_GROUP)
                for hot, to in ((hot1, first), (hot2, second)):
                    step(tt(to.rearrange("p t (g e) -> p t g e", g=GROUPS),
                            hotg.unsqueeze(3).to_broadcast([P, nt, GROUPS, PER_GROUP]),
                            hot.unsqueeze(2).to_broadcast([P, nt, GROUPS, PER_GROUP]), ALU.mult))
                step(dve.memset(none, 0.0))
                tt(member, first, second, ALU.add).then_inc(s_members, 1)
                step(tt(valued, both,
                        const("ids").rearrange("p (k t) -> p k t", k=2)[:, :, 0:nt].unsqueeze(3).to_broadcast(
                            [P, 2, nt, EXPERTS]), ALU.mult))
                dve.wait_ge(s_rexp, 2 * layer + 2)
                step(dve.tensor_reduce(sumg, eg, AX_X, ALU.add))
                step(ts(den, t2, 1.0, None, ALU.add))
                step(tt(den, den, sumg, ALU.mult))
                step(dve.reciprocal(gates[:, 0, 0:nt], den))
                step(tt(gates[:, 1, 0:nt], gates[:, 0, 0:nt], t2, ALU.mult))
                n = job("ranks", layer)
                done(dve, n)
                ranks = bank(n)[:, 0:EXPERTS * nt].rearrange("p (t e) -> p t e", e=EXPERTS)
                for k, hot in enumerate((first, second)):
                    step(tt(scratch[:, k], ranks, hot, ALU.mult))
                step(dve.tensor_reduce(rank, scratch, AX_X, ALU.add))
                hot = A(A_HOT, 8, SLOTS)
                for block in range(SLOTS // EXPERTS):
                    for k in range(2):
                        ins = tt(hot[:, 4 * k:4 * k + nt, EXPERTS * block:EXPERTS * (block + 1)],
                                 const("idx_expert").unsqueeze(1).to_broadcast([P, nt, EXPERTS]),
                                 wide(rank[:, k], EXPERTS), ALU.is_equal)
                    if block == 0:
                        step(ins)
                        step(ts(rank, rank, float(EXPERTS), None, ALU.subtract))
                ins.then_inc(s_hot, 1)
                step(dve.tensor_reduce(count, bank(n)[:, EXPERTS * nt:EXPERTS * (nt + 1)], AX_X, ALU.max))
                stt(place, ranks, float(EXPERTS), const("idx_expert").unsqueeze(1).to_broadcast([P, nt, EXPERTS]),
                    ALU.mult, ALU.add).then_inc(free_s[n % BANKS], 1)
                n = job("table", layer)
                done(dve, n)
                step(ts(table[:, :], bank(n)[:, 0:EXPERTS], float(NO_ID), None, ALU.add))
                step(ts(gidx[:, :], table[0:SLOTS, :], 1, None, ALU.logical_shift_right))
                ts(sidx[:, :], bank(n)[:, 0:EXPERTS], 2.0, const("half"), ALU.mult, ALU.add
                   ).then_inc(free_s[n % BANKS], 1)
                taken(dve, n)
                dve.tensor_copy(fullest[:, :], count).then_inc(s_idx, 1)
                dve.wait_ge(s_idx, layer + 1)
                for k, hot in enumerate((first, second)):
                    step(tt(scratch[:, k], place, hot, ALU.mult))
                step(dve.tensor_reduce(where, scratch, AX_X, ALU.add))
                step(dve.tensor_copy(addr[:, :, 0:nt], where))
                ts(table[:, 0:8], const("ids"), float(NO_ID), None, ALU.add).then_inc(s_addr, 1)
                if layer == 0:
                    mod_block(1, 5)

            def experts(layer):
                n0 = job("moe", layer)
                with dve.Fori(0, TURNS) as it:
                    for u in range(EPI):
                        n = n0 + PER_EXPERT * u
                        b = u % 2
                        dve.wait_ge(s_silu, it * EPI + (EXPERTS * layer + u + 1))
                        tt(A(A_HID + b * 256, 256)[0:SLOTS, :], bank(n + 1)[SLOTS:P, 0:HIDDEN],
                           A(A_SL + b * 256, 256)[0:SLOTS, :], ALU.mult).then_inc(free_s[(n + 1) % BANKS], 1)
                        done(dve, n + 3, it)
                        dve.wait_ge(s_scat[u], it * 16 + 16 * (TURNS * layer + 1))
                        dve.tensor_copy(A(A_YS + u * 512, 512), bank(n + 3)[:, :]).then_inc(free_s[(n + 3) % BANKS], 1)

            def overflow(layer):
                dve.wait_ge(s_idx, layer + 1)
                count = dve.value_load(fullest[0:1, 0:1], min_val=0, max_val=4 * P)
                o = lambda k: ov[layer, k]
                with dve.If(count > SLOTS):
                    with dve.Fori(0, (TILES[layer] * P // SLOTS - 1) * EXPERTS) as n:
                        dve.wait_ge(o("ix"), n * 32 + 32)
                        ts(ov_idx[0:SLOTS, 0:1], ov_table[0:SLOTS, :], 1, None, ALU.logical_shift_right)
                        ts(ov_idx[:, 1:2], ov_table[:, :], 2.0, const("half"), ALU.mult, ALU.add).then_inc(o("idx"), 1)
                        dve.wait_ge(o("a2"), n + 1)
                        tt(A(A_HID, 256)[0:SLOTS, :], banks[1][SLOTS:P, 0:HIDDEN], A(A_SL, 256)[0:SLOTS, :], ALU.mult
                           ).then_inc(o("d2"), 1)

            def combine(layer, t):
                dve.wait_ge(s_gate, 32 * (layer + 1))
                dve.wait_ge(s_first, 4 * layer + t + 1)
                y = A(A_XG + t * 2 * D, 2, D)
                step(stt(y[:, 0, :], y[:, 1, :], gates[:, 1, t:t + 1], y[:, 0, :], ALU.mult, ALU.add))
                step(tt(y[:, 0, :], y[:, 0, :], bc_gate[:, t // 2, :], ALU.mult))
                tt(res[:, t, :], res[:, t, :], y[:, 0, :], ALU.add).then_inc(s_comb, 1)

            dve.wait_ge(s_gate, 16)
            dve.wait_ge(s_ab, 32)
            for i in range(8):
                add_mixer(0, i)
                if i in AFTER_WO:
                    mod_block(*AFTER_WO[i])
                if i == 3:
                    reciprocal_roots(0, 2)
                if i in (4, 5):
                    modulated(0, i - 4)
            h2_turned(0, 0)
            h2_turned(0, 1)
            reciprocal_roots(2, 4)
            modulated(0, 2)
            mod_block(1, 4)
            modulated(0, 3)
            h2_turned(0, 2)
            h2_turned(0, 3)
            route(0)
            experts(0)
            overflow(0)

            combine(0, 0)
            combine(0, 1)
            reciprocal_roots(0, 2)
            normed(1, 0)
            normed(1, 1)
            combine(0, 2)
            turn_rows(1, 0)
            turn_rows(1, 1)
            combine(0, 3)
            reciprocal_roots(2, 4)
            normed(1, 2)
            normed(1, 3)

            tab = lambda k: A(A_RTAB + 512 * k, 512)
            rope = lambda ch, k: A(A_ROPE + (2 * ch + k) * SEQ, SEQ)

            def rotate(to, ps, ch, n, last):
                ra, rb_ = A(A_RTMP, SEQ), A(A_RTMP + SEQ, SEQ)
                step(tt(ra, ps, rope(ch, 0), ALU.mult))
                step(tt(rb_[0:64, :], ps[64:128, :], rope(ch, 1)[0:64, :], ALU.mult))
                ins = tt(rb_[64:128, :], ps[0:64, :], rope(ch, 1)[64:128, :], ALU.mult)
                step(ins)
                ins = tt(to, ra, rb_, ALU.add)
                if last:
                    ins.then_inc(free_s[n % BANKS], 1)
                    taken(dve, n)
                else:
                    step(ins)

            def rotate_q(h):
                n = job("rq", h)
                done(dve, n)
                for ch in range(2):
                    rotate(A(A_RQ, 2, SEQ)[:, ch, :], bank(n)[:, SEQ * ch:SEQ * (ch + 1)], ch, n, ch == 1)

            dve.wait_ge(s_rope_in, 16)
            rotate_q(0)
            turn_rows(1, 2)
            turn_rows(1, 3)
            dve.wait_ge(s_ret_in, 16)
            for h in range(R_HEADS):
                for ch in range(2):
                    n = job("rk", h, ch)
                    done(dve, n)
                    dve.wait_ge(s_ctx_keys, 2 * h + ch + 1)
                    rotate(A(A_RK, 2, 512)[:, ch, 0:SEQ], bank(n)[:, 0:SEQ], ch, n, True)
                dk, e = A(A_RD, 512), A(A_EXP, 512)
                dve.wait_ge(s_rexps, 4 * h + 2)
                step(tt(dk, dk, tab(3), ALU.mult))
                step(tt(e, e, tab(4), ALU.mult))
                tt(dk, dk, e, ALU.add).then_inc(s_factors, 1)
                dc = A(A_RD + 512, 512)
                dve.wait_ge(s_rexps, 4 * h + 4)
                tt(dc, dc, e, ALU.add).then_inc(s_factors, 1)
                dve.wait_ge(s_factors, 2 * h + 2)
                for a in range(2):
                    n = job("rs", h, a)
                    d = A(A_RD + 512 * a, 512)
                    done(dve, n)
                    stt(d, bank(n)[:, :], float(R_QK) ** -0.5, d, ALU.mult, ALU.mult).then_inc(free_s[n % BANKS], 1)
                if h + 1 < R_HEADS:
                    rotate_q(h + 1)
                for t in range(2):
                    i = 2 * h + t
                    n = job("ro", h, t)
                    dve.wait_ge(s_yms, i + 1)
                    ts(soft[:, 2 + t:3 + t], soft[:, t:t + 1], 1.0 / R_V, EPS, ALU.mult, ALU.add).then_inc(s_yroot, 1)
                    dve.wait_ge(s_yroot, 2 * i + 2)
                    step(dve.reciprocal(soft[:, 6 + t:7 + t], soft[:, 4 + t:5 + t]))
                    g = ret_gate(h)[:, t, :]
                    taken(dve, job("rg", h, t))
                    stt(g, bank(n)[:, :], soft[:, 6 + t:7 + t], g, ALU.mult, ALU.mult).then_inc(free_s[n % BANKS], 1)
            dve.wait_ge(s_gate, 48)
            for i in range(4):
                add_mixer(1, i)
                if i == 1:
                    reciprocal_roots(0, 1)
                    dve.wait_ge(s_ab, 64)
                    modulated(1, 0)
            reciprocal_roots(1, 2)
            modulated(1, 1)
            h2_turned(1, 0)
            h2_turned(1, 1)
            route(1)
            experts(1)
            overflow(1)
            combine(1, 0)
            combine(1, 1)
            for t in range(2):
                reciprocal_roots(t, t + 1)
                if t == 0:
                    dve.wait_ge(s_fin_g, 16)
                stt(A(A_XG + t * D, D), res[:, t, :], stat[:, 2, t:t + 1], A(A_BCA, D), ALU.mult, ALU.mult
                    ).then_inc(s_fin, 1)


_INS = ["x", "c", "ctx", "c_ctx", "ada_w", "ada_b", "norm1_g", "norm2_g", "w_in_e", "conv_w", "na_rpb", "w_out_e",
        "w_in_o", "ret_decay_f", "ret_decay_b", "w_out_o", "router_gw", "router_gb", "router_ew", "router_eb",
        "moe_w1", "moe_w3", "moe_w2", "final_g"]


def kernel(**inputs):
    import numpy as _np
    import concourse.bacc as _bacc
    from concourse import mybir as _mybir
    from concourse.bass_utils import run_bass_kernel_spmd as _run

    nc = _bacc.Bacc("TRN2", target_bir_lowering=False, num_devices=1)
    arrays, args, consts = {}, [], []

    def declare(name, a):
        arrays[name] = a
        return nc.dram_tensor(name, a.shape, _mybir.dt.from_np(a.dtype), kind="ExternalInput").ap()

    for name in _INS:
        a = inputs[name]
        if name == "na_rpb":
            a = a[..., ::-1]
        args.append(declare(f"in_{name}_dram", _np.ascontiguousarray(a)))
    for i, a in enumerate(shape_constants()):
        consts.append(declare(f"const_{i}_dram", _np.ascontiguousarray(a)))
    out = nc.dram_tensor("out_0_dram", (1, SEQ, D), _mybir.dt.from_np(_np.dtype("float32")), kind="ExternalOutput").ap()
    backbone(nc, args, consts, out)
    r = _run(nc, [arrays], core_ids=[0])
    return r.results[0]["out_0_dram"]
```

```python
from contextlib import ExitStack

import numpy as np
import concourse.bass as bass
from concourse import mybir

F32 = mybir.dt.float32
F32R = mybir.dt.float32r
U32 = mybir.dt.uint32
I32 = mybir.dt.int32
ALU = mybir.AluOpType
ACT = mybir.ActivationFunctionType
AX_X = mybir.AxisListType.X

P = 128
D = 1024
KC = D // P
SEQ = 256
GRID_W = 64
ROWS = SEQ // GRID_W
WIN_W = 16
HEADS = 8
HEAD_DIM = 64
R_HEADS = 4
R_QK = 256
R_V = 512
ROPE_BASE = 10000.0
GROUPS = 4
PER_GROUP = 8
EXPERTS = GROUPS * PER_GROUP
HIDDEN = 256
EPS = 1e-6
BIG = 1.0e30
TILES = (4, 2)
SLOTS = (64, 32)
NO_ID = 2 * TILES[0] * P

UNIT = 2048
RING = 12
BANKS = 8
EPI = 4
TURNS = EXPERTS // EPI
PER_EXPERT = 4

CONST_COLS = {}
_at = 0
for _name, _n in (("ident", P), ("upper", P), ("ones", P), ("window", GRID_W), ("idx_group", GROUPS),
                  ("idx_in_group", PER_GROUP), ("idx_expert", EXPERTS), ("half", 2), ("ids", 8)):
    CONST_COLS[_name] = (_at, _n)
    _at += _n
CONST_N = _at
RET_N = 2 * SEQ * 3 + 4 * SEQ


def shape_constants():
    c = np.zeros((P, CONST_N), np.float32)

    def put(name, a):
        o, n = CONST_COLS[name]
        c[:, o:o + n] = a

    i = np.arange(P)
    put("ident", np.eye(P))
    put("upper", i[:, None] < i[None, :])
    put("ones", 1.0)
    col = i % GRID_W
    first = np.clip(col - WIN_W // 2, 0, GRID_W - WIN_W)
    j = np.arange(GRID_W)
    inside = (j[None, :] >= first[:, None]) & (j[None, :] < first[:, None] + WIN_W)
    put("window", np.where(inside, 0.0, -BIG)[:, ::-1])
    put("idx_group", np.arange(GROUPS))
    put("idx_in_group", np.arange(PER_GROUP))
    put("idx_expert", np.arange(EXPERTS))
    put("half", (i[:, None] % (2 * np.array(SLOTS)) >= SLOTS))
    ids = 2 * (np.arange(4)[None, None, :] * P + i[:, None, None]) + np.arange(2)[None, :, None]
    put("ids", ids.reshape(P, 8) - NO_ID)

    q = np.arange(SEQ, dtype=np.float32)
    dist = np.stack([q[None, :] - (t * P + i)[:, None] for t in range(2)], 1).astype(np.float32)
    parts = [dist, np.maximum(dist, 0), np.maximum(-dist, 0)]
    freq = (np.float32(ROPE_BASE) ** (-np.arange(64, dtype=np.float32) / np.float32(64))).astype(np.float32)
    pos = np.arange(SEQ)
    sign = np.where(i < 64, -1.0, 1.0).astype(np.float32)[:, None]
    for axis in (pos // GRID_W, pos % GRID_W):
        ang = (axis.astype(np.float32)[None, :] * freq[i % 64][:, None]).astype(np.float32)
        parts += [np.cos(ang), np.sin(ang) * sign]
    ret = np.concatenate([p.reshape(P, -1) for p in parts], 1).astype(np.float32)
    return c, ret


ITEMS = 4 * HEADS
AHEAD = 3
AFTER_ITEM = {2: ("ada", 0, 5), 6: ("ada", 1, 0), 10: ("ada", 1, 1), 14: ("modT", 1, 0), 15: ("modT", 1, 1),
              17: ("ada", 1, 2), 21: ("ada", 1, 3), 26: ("ada", 1, 4)}
AFTER_WO = {1: (1, 5)}


NORM2_GROUPS = (((0, 1), (2, 3)), ((0,), (1,)))


def plan_jobs():
    jobs = {}
    n = 0

    def add(*name):
        nonlocal n
        jobs[name] = n
        n += 1

    add("cT")
    add("cwT")
    for q in range(2):
        add("ada", 0, q)
    for q in range(2):
        add("modT", 0, q)
    for t in range(4):
        for half in range(2):
            add("hT", 0, t, half)
    for ch in range(4):
        add("ac", ch)
        add("ax", ch)
        add("ab", ch)
    add("ada", 0, 2)
    for ch in range(4):
        add("q", ch)
    add("ada", 0, 3)
    for ch in range(4):
        add("k", ch)
    add("ada", 0, 4)
    for t in range(4):
        add("v", t)
    for i in range(AHEAD):
        add("s", i)
    for i in range(ITEMS):
        if i + AHEAD < ITEMS:
            add("s", i + AHEAD)
        add("pt", i)
        if i % 2 and i > 1:
            add("pv", (i - 3) // 2)
        if i in AFTER_ITEM:
            add(*AFTER_ITEM[i])
    add("pv", ITEMS // 2 - 1)
    for i in range(8):
        add("wo", 0, i // 2, i % 2)
        if i in AFTER_WO:
            add("ada", *AFTER_WO[i])

    def experts(layer):
        for t in range(TILES[layer]):
            for half in range(2):
                add("rT", layer, t, half)
            if t % (TILES[layer] // 2) == TILES[layer] // 2 - 1:
                add("logitsT", layer, t // (TILES[layer] // 2))
        add("logits", layer)
        add("ranks", layer)
        add("table", layer)
        nonlocal n
        jobs[("moe", layer)] = n
        n += EXPERTS * PER_EXPERT

    experts(0)
    for t in range(2):
        for half in range(2):
            add("hT", 1, t, half)
    add("rq", 0)
    for t in range(2):
        add("rg", 0, t)
    for t in range(2, 4):
        for half in range(2):
            add("hT", 1, t, half)
    for t in range(2):
        add("rv", 0, t)
    for h in range(R_HEADS):
        for c in range(2):
            add("rk", h, c)
        for t in range(0 if h else 2, 4):
            add("rv", h, t)
        for a in range(2):
            add("rs", h, a)
        if h + 1 < R_HEADS:
            add("rq", h + 1)
        for t in range(2):
            add("ro", h, t)
        if h + 1 < R_HEADS:
            for t in range(2):
                add("rg", h + 1, t)
        else:
            for i in range(4):
                add("wo", 1, i // 2, i % 2)
        for t in range(2):
            add("ryT", h, t)
    experts(1)
    return jobs


JOBS = plan_jobs()

U_GROUPS_E = (8, 12, 16, 24, 32, 40)
U_ADA = (0, 4, 20, 28, 36, 44, 48, 52, 56, 60, 64, 68)
U_WOUT_E = 72
U_MOE0 = 76
U_WIN_O = U_MOE0 + 3 * EXPERTS
U_WOUT_O = U_WIN_O + 48
U_MOE1 = U_WOUT_O + 16


def split_unit(j):
    return U_GROUPS_E[j // 2] + j % 2 if j < 12 else U_WIN_O + 4 * ((j - 12) // 2) + j % 2


OUT_J = 36

ARENA = 15360
A_BCA, A_BCB = 0, 2048
A_BIAS = 0
A_Q, A_K, A_V, A_YC = 4096, 6144, 8192, 10240
A_PT = 13312
A_XN = 6144
A_CONV = 8192
A_HIGH = 12288
A_TMP = 14336
A_H2 = (4096, 10496)
A_XG, A_XGT, A_YS, A_SL, A_HID, A_HIDT, A_ROUTE = 4096, 8192, 9216, 11264, 11776, 12288, 12544
A_SQUARES = 13312
A_LOGITS = 8192
A_HOT, A_VALUED = 9216, 10240
A_RQ, A_RK, A_RV, A_RG, A_RY, A_RD = 0, 512, 1536, 3584, 4608, 8704
A_RTAB, A_ROPE, A_RTMP, A_RG_ODD, A_EXP = 9728, 12288, 13312, 13824, 14848
A_XN1 = (6144, 13824)
A_HIGH_ODD = (11264, 7680)
A_GATE_C = (13312, 14848)
A_Y = (0, 2048, 4096, 8704)


def backbone(nc, ins, consts, out):
    (x, c, ctx_in, c_ctx, ada_w, ada_b, norm1_g, norm2_g, w_in_e, conv_w, rpb_rev, w_out_e, w_in_o,
     decay_f, decay_b, w_out_o, router_gw, router_gb, router_ew, router_eb, moe_w1, moe_w3, moe_w2,
     final_g) = ins
    shape_c, ret_c = consts

    stack = ExitStack()
    with stack:
        def sb(name, shape, dt=F32):
            return stack.enter_context(nc.sbuf_tensor(name, shape, dt))

        def sem(name):
            return stack.enter_context(nc.semaphore(name))

        mod_rows_d = nc.dram_tensor("mod_rows_d", [12, 2, D], F32).ap()
        h2_d = [nc.dram_tensor(f"h2_d{l}", [TILES[l] * P, D], F32).ap() for l in range(2)]
        table_d = [nc.dram_tensor(f"table_d{l}", [TILES[l] * P * EXPERTS, 1], U32).ap() for l in range(2)]
        y_d = [nc.dram_tensor(f"y_d{l}", [TILES[l] * P * 4, D // 2], F32).ap() for l in range(2)]

        def both_types(name, shape):
            with nc.sbuf_tensor(name + "_parts", shape, F32R) as parts:
                pass
            return sb(name, shape), parts

        ring, ring_parts = both_types("ring", [P, RING, UNIT])
        arena, arena_parts = both_types("arena", [P, ARENA])
        res = sb("res", [P, 4, D])
        hT, hT_parts = both_types("hT", [P, KC, 4 * P])
        bc_gate, gate_parts = both_types("bc_gate", [P, 2, D])
        con = sb("con", [P, CONST_N])
        gate_parts = gate_parts[:, :, :].rearrange("p s (a n) -> p (s a) n", n=512)
        crow = bc_gate[0:16, 0, 0:P]
        csil = bc_gate[0:16, 0, P:2 * P]
        cwrow = bc_gate[0:12, 0, 2 * P:3 * P]
        cvec = sb("cvec", [P, KC, 32])
        cwT = sb("cwT", [P, 12])
        ada_rows = sb("ada_rows", [P, 2, 2, 256])
        mod_rows = sb("mod_rows", [P, 2, 256])
        modT = sb("modT", [P, 2, 2, KC, 2])
        stat = sb("stat", [P, 3, 4])
        rw = sb("rw", [P, KC, 36])
        rb = sb("rb", [P, 36])
        gates = sb("gates", [P, 2, 4])
        addr = sb("addr", [P, 2, 4], U32)
        table = sb("table", [P, EXPERTS], U32)
        gidx = sb("gidx", [SLOTS[0], EXPERTS], U32)
        sidx = sb("sidx", [P, EXPERTS], U32)
        gnow = sb("gnow", [SLOTS[0], 8], U32)
        snow = sb("snow", [P, 8], U32)
        ov_table = sb("ov_table", [P, 1], U32)
        ov_idx = sb("ov_idx", [P, 2], U32)
        fullest = sb("fullest", [P, 1], I32)
        soft = sb("soft", [P, 16])
        dec = sb("dec", [P, 8 * 5])

        def const(name):
            o, n = CONST_COLS[name]
            return con[:, o:o + n]

        ident = const("ident")

        def A(at, *shape):
            n = 1
            for s in shape:
                n *= s
            v = arena[:, at:at + n]
            if len(shape) == 2:
                v = v.rearrange("p (a b) -> p a b", b=shape[1])
            if len(shape) == 3:
                v = v.rearrange("p (a b c) -> p a b c", b=shape[1], c=shape[2])
            return v

        banks = [stack.enter_context(nc.psum_tensor(f"bank{b}", [P, 512], F32)) for b in range(BANKS)]

        arrived_s = [sem(f"weights_in{s}") for s in range(RING)]
        full_s = [sem(f"psum_full{b}") for b in range(BANKS)]
        free_s = [sem(f"psum_free{b}") for b in range(BANKS)]
        s_c, s_con, s_x, s_cw = sem("c_in"), sem("constants_in"), sem("x_in"), sem("conv_w_in")
        s_bias = sem("bias_in")
        s_csil, s_ms, s_root, s_rstd, s_xn = (sem("silu_c"), sem("mean_square"), sem("root"),
                                              sem("rstd_ready"), sem("normed_ready"))
        s_ada_in = [sem(f"ada_rows_in{i}") for i in range(2)]
        s_zero = sem("zeroed")
        s_stored = [sem(f"mod_rows_stored{i}") for i in range(2)]
        s_gate, s_ab = sem("gate_rows_in"), sem("scale_and_shift_in")
        s_high_rows, s_low_rows = sem("high_rows_ready"), sem("low_rows_ready")
        s_rows = sem("split_rows_ready")
        s_low, s_low_v = sem("low_weights_ready"), sem("low_value_weights_ready")
        s_wout = sem("output_weights_read")
        s_ry_high, s_ry_low = sem("high_outputs_ready"), sem("low_outputs_ready")
        s_exp, s_probs = sem("exp_ready"), sem("probs_ready")
        s_max = sem("max_ready")
        s_mixed = sem("mixer_added")
        s_h2, s_h2_out = sem("h2_ready"), sem("h2_stored")
        s_rw = sem("router_in")
        s_gap, s_rexp = sem("router_gap_ready"), sem("router_exp_ready")
        s_members, s_addr = sem("members_ready"), sem("addresses_ready")
        s_table_clear, s_hot = sem("table_cleared"), sem("slot_one_hots_ready")
        s_idx = sem("indices_ready")
        s_gath = [sem(f"rows_in{u}") for u in range(EPI)]
        s_scat = [sem(f"rows_out{u}") for u in range(EPI)]
        s_now = sem("index_column_ready")
        s_silu = sem("expert_silu_ready")
        s_y_in, s_comb = [sem(f"expert_rows_in{t}") for t in range(4)], sem("tile_combined")
        s_first = sem("first_expert_weighted")
        s_dec_in, s_dec = sem("decay_in"), sem("decay_ready")
        s_rope_in, s_ret_in = sem("rotary_tables_in"), sem("distances_in")
        s_pe_seen, s_pool_seen = sem("tensor_waits_seen"), sem("gpsimd_waits_seen")
        s_rexps = sem("decay_exp_ready")
        s_factors = sem("decay_factors_added")
        s_yms, s_yroot = sem("y_square_sum"), sem("y_root")
        s_ctx_keys = sem("context_keys_ready")
        s_fin, s_fin_g, s_out = sem("final_ready"), sem("final_g_in"), sem("output_stored")
        s_dve, s_pool = sem("vector_step"), sem("gpsimd_step")
        ov = {}
        for l in range(2):
            for k in ("set", "w", "ix", "idx", "g", "p1", "a1", "p2", "a2", "d2", "p3", "a3", "y", "a4", "scat"):
                ov[l, k] = sem(f"over{l}_{k}")

        def bank(n):
            return banks[n % BANKS]

        def job(*name):
            return JOBS[name]

        def begin(eng, n, turn=0):
            if isinstance(turn, int):
                v = n // BANKS + 2 * turn
                if v > 0:
                    eng.wait_ge(free_s[n % BANKS], v)
            else:
                eng.wait_ge(free_s[n % BANKS], turn * 2 + n // BANKS)

        def done(eng, n, turn=0):
            eng.wait_ge(full_s[n % BANKS], turn * 2 + (n // BANKS + 1))

        def taken(eng, n, turn=0):
            eng.wait_ge(free_s[n % BANKS], turn * 2 + (n // BANKS + 1))

        def arrived(eng, n, turn=0):
            eng.wait_ge(arrived_s[n % RING], turn * 16 + 16 * (n // RING + 1))

        def unit(n):
            return ring[:, n % RING, :]

        def parts(n):
            return ring_parts[:, n % RING, :]

        def ada_name(a):
            return a // 6, a % 6

        ada_in_count = [0, 0]
        ada_in_value = []
        for a in range(12):
            ada_in_count[a % 2] += 16 * (4 if a % 6 in (1, 4) else 2)
            ada_in_value.append(ada_in_count[a % 2])
        stored_count = [0, 0]
        stored_value = []
        for a in range(12):
            if a % 6 >= 2:
                stored_count[a % 2] += 32
            stored_value.append(stored_count[a % 2])

        def last_reader(n):
            group = n // 4 * 4
            if group in U_ADA:
                return job("ada", *ada_name(U_ADA.index(group)))
            if group in U_GROUPS_E:
                m = 2 * U_GROUPS_E.index(group) + n % 2
                if m < 6:
                    ch = 2 * (m // 3) + 1
                    return job(("ac", "ax", "ab")[m % 3], ch)
                if m < 10:
                    return job("q" if m < 8 else "k", 2 * (m % 2) + 1)
                return job("v", 3)
            if group == U_WOUT_E:
                return job("wo", 0, 3, 1)
            if n < U_WIN_O:
                return moe_reader(0, n - U_MOE0)
            if n < U_WOUT_O:
                h, m = divmod(2 * ((n - U_WIN_O) // 4) + n % 2, 6)
                return (job("rq", h), job("rk", h, 1), job("rg", h, 1), job("rg", h, 1),
                        job("rv", h, 3), job("rv", h, 3))[m]
            if n < U_MOE1:
                return job("wo", 1, 1, 1)
            return moe_reader(1, n - U_MOE1)

        def moe_reader(layer, m):
            e, part = divmod(m, 3)
            return job("moe", layer) + PER_EXPERT * e + (3 if part == 2 else 1)

        def room(eng, n):
            m = 2 * ((n - RING - U_WOUT_O) // 4) + n % 2
            if 0 <= m < 6:
                eng.wait_ge(s_wout, m + 1)
            elif n >= RING:
                done(eng, last_reader(n - RING))

        def probs(i):
            return hT[:, 4 + i % 4, 0:512 if i % 4 < 2 else 256]

        def high_rows(layer, k):
            if k < 4:
                return gate_parts[:, k:k + 2, :]
            at = A_HIGH + 512 * (k - 4) if layer == 0 else A_HIGH_ODD[k // 2 - 2]
            return arena_parts[:, at:at + 1024].rearrange("p (k n) -> p k n", k=2)

        hT_flat_parts = hT_parts[:, :, :].rearrange("p k n -> p (k n)")

        def norm_place(layer, t):
            return A_XN1[t % 2] if layer else A_XN + (t % 2) * D

        def ret_gate(h):
            return A((A_RG, A_RG_ODD)[h % 2], 2, 512)

        block = stack.enter_context(nc.Block())

        @block.sync
        def _(sp):
            sp.dma_start(crow[0:8, :], c.rearrange("a (k p) -> (a k) p", p=P)).then_inc(s_c, 16)
            sp.dma_start(crow[8:16, :], c_ctx.rearrange("(k p) -> k p", p=P)).then_inc(s_c, 16)
            sp.dma_start(con[:, :], shape_c).then_inc(s_con, 16)
            sp.dma_start(cwrow, conv_w[0].rearrange("w (k p) -> (w k) p", p=P)).then_inc(s_cw, 16)

            def ada_block(a):
                layer, q = ada_name(a)
                for m in range(4):
                    n = U_ADA[a] + m
                    room(sp, n)
                    sp.dma_start(unit(n).rearrange("p (k n) -> p k n", k=KC),
                                 ada_w[layer, :, q * D + 256 * m:q * D + 256 * m + 256].rearrange(
                                     "(k p) n -> p k n", p=P)).then_inc(arrived_s[n % RING], 16)

            for a in range(2):
                ada_block(a)
                if a == 0:
                    sp.dma_start(res[:, 0:2, :], x[0].rearrange("(t p) d -> p t d", p=P)).then_inc(s_x, 16)
                    sp.dma_start(res[:, 2:4, :], ctx_in[0].rearrange("(t p) d -> p t d", p=P)).then_inc(s_x, 16)

            def columns(w, n, col):
                room(sp, n)
                sp.dma_start(unit(n).rearrange("p (k n) -> p k n", k=KC),
                             w[0, :, col:col + 256].rearrange("(k p) n -> p k n", p=P)
                             ).then_inc(arrived_s[n % RING], 16)

            def rows(w, n, row):
                room(sp, n)
                sp.dma_start(unit(n).rearrange("p (k n) -> p k n", k=2),
                             w[0, row:row + 256, :].rearrange("(k p) n -> p k n", p=P)
                             ).then_inc(arrived_s[n % RING], 16)

            for pair in range(2):
                for i, part in enumerate((1, 2, 0)):
                    columns(w_in_e, split_unit(3 * pair + i), 512 * part + 256 * pair)
            for m in range(6):
                if m % 2 == 0:
                    ada_block(2 + m // 2)
                columns(w_in_e, split_unit(6 + m), 1536 + 256 * m)
            for a in range(5, 12):
                ada_block(a)
            for m in range(4):
                rows(w_out_e, U_WOUT_E + m, 256 * m)

            def moe_stream(layer, u0):
                for m in range(24):
                    if m in (8, 12):
                        for t in (range(2), range(2, 4))[m == 12] if layer == 0 else range(2) if m == 12 else ():
                            sp.wait_ge(s_h2, 4 * layer + t + 1)
                            sp.dma_start(h2_d[layer][t * P:(t + 1) * P, :], A(A_H2[layer] + t * D, D)
                                         ).then_inc(s_h2_out, 16)
                    room(sp, u0 + m) if m < RING else done(sp, moe_reader(layer, m - RING))
                    e, part = divmod(m, 3)
                    load_part(layer, 0, e, part, u0 + m, 0)
                with sp.Fori(1, GROUPS) as g:
                    for m in range(24):
                        back = moe_reader(layer, m + 12) if m < 12 else moe_reader(layer, m - 12)
                        turn = (g - 1) * 2 if m < 12 else g * 2
                        done(sp, back, turn)
                        e, part = divmod(m, 3)
                        load_part(layer, g, e, part, u0 + m, g * 2)

            def load_part(layer, g, e, part, n, turn):
                u = unit(n)
                if part < 2:
                    w = (moe_w1, moe_w3)[part]
                    src = w[layer, bass.ds(g, 1), :, HIDDEN * e:HIDDEN * (e + 1)].rearrange(
                        "a (k p) n -> p (a k) n", p=P)
                    dst = u.rearrange("p (k n) -> p k n", k=KC)
                else:
                    src = moe_w2[layer, bass.ds(g, 1), HIDDEN * e:HIDDEN * (e + 1), :].rearrange(
                        "a (k p) n -> p (a k) n", p=P)
                    dst = u.rearrange("p (k n) -> p k n", k=2)
                sp.dma_start(dst, src).then_inc(arrived_s[n % RING], 16)

            def overflow(layer):
                S = SLOTS[layer]
                sp.wait_ge(s_idx, layer + 1)
                count = sp.value_load(fullest[0:1, 0:1], min_val=0, max_val=4 * P)
                with sp.If(count > S):
                    done(sp, job("moe", layer) + EXPERTS * PER_EXPERT - 1)
                    with sp.Fori(0, TILES[layer] * P // S - 1) as b:
                        with sp.Fori(0, GROUPS) as g:
                            with sp.Fori(0, PER_GROUP) as e:
                                sp.wait_ge(ov[layer, "y"], b * EXPERTS + g * PER_GROUP + e + 1)
                                for w, place in ((moe_w1, 0), (moe_w3, 1)):
                                    sp.dma_start(
                                        unit(place).rearrange("p (k n) -> p k n", k=KC),
                                        w[layer, bass.ds(g, 1), :, bass.ds(e * HIDDEN, HIDDEN)].rearrange(
                                            "a (k p) n -> p (a k) n", p=P)).then_inc(ov[layer, "w"], 16)
                                sp.dma_start(
                                    unit(2).rearrange("p (k n) -> p k n", k=2),
                                    moe_w2[layer, bass.ds(g, 1), bass.ds(e * HIDDEN, HIDDEN), :].rearrange(
                                        "a (k p) n -> p (a k) n", p=P)).then_inc(ov[layer, "w"], 16)
                    sp.wait_ge(ov[layer, "y"], (TILES[layer] * P // S - 1) * EXPERTS + 1)
                    sp.wait_ge(ov[layer, "scat"], 16 * (TILES[layer] * P // S - 1) * EXPERTS)

            def load_results(layer):
                for u in range(EPI):
                    sp.wait_ge(s_scat[u], 16 * (TURNS * (layer + 1) + 1))
                for t in range(TILES[layer]):
                    sp.dma_start(A(A_Y[t], 2 * D),
                                 y_d[layer][t * P * 4:(t + 1) * P * 4, :].rearrange("(p a) n -> p (a n)", a=4)
                                 ).then_inc(s_y_in[t], 16)

            moe_stream(0, U_MOE0)
            overflow(0)
            for h in range(R_HEADS):
                j = 12 + 6 * h
                columns(w_in_o, split_unit(j), R_QK * h)
                columns(w_in_o, split_unit(j + 1), D + R_QK * h)
                if h == 0:
                    load_results(0)
                for m in range(2):
                    columns(w_in_o, split_unit(j + 2 + m), 2 * D + R_HEADS * R_V + R_V * h + 256 * m)
                for m in range(2):
                    columns(w_in_o, split_unit(j + 4 + m), 2 * D + R_V * h + 256 * m)
            for m in range(8):
                rows(w_out_o, split_unit(OUT_J + m), 256 * m)
            moe_stream(1, U_MOE1)
            overflow(1)
            load_results(1)
            for t in range(2):
                sp.wait_ge(s_fin, t + 1)
                sp.dma_start(out[0, t * P:(t + 1) * P, :], A(A_Y[t] + D, D)).then_inc(s_out, 16)
            sp.wait_ge(s_out, 32)

        @block.gpsimd
        def _(pool):
            steps = [0]

            def step(ins):
                steps[0] += 1
                ins.then_inc(s_pool, 1)
                pool.wait_ge(s_pool, steps[0])

            for i, d in enumerate((decay_f, decay_b)):
                pool.dma_start(dec[:, 4 * i:4 * i + 4], bass.AP(d.tensor, 0, [[0, P], [1, R_HEADS]])
                               ).then_inc(s_dec_in, 16)
            pool.memset(ada_rows[:, :, :, :], 0.0).then_inc(s_zero, 1)
            pool.memset(cvec[:, :, :], 0.0).then_inc(s_zero, 1)
            pool.wait_ge(s_zero, 2)

            def load_ada_rows(a):
                layer, q = ada_name(a)
                for s in range(2):
                    pool.dma_start(ada_rows[s:P:32, a % 2, 0, :],
                                   ada_b[layer, q * D:(q + 1) * D].rearrange("(j n) -> j n", n=256)
                                   ).then_inc(s_ada_in[a % 2], 16)
                    if q in (1, 4):
                        g = (norm1_g if q == 1 else norm2_g)[layer]
                        pool.dma_start(ada_rows[s:P:32, a % 2, 1, :], g.rearrange("(j n) -> j n", n=256)
                                       ).then_inc(s_ada_in[a % 2], 16)

            def store_mod_rows(a):
                taken(pool, job("ada", *ada_name(a)))
                if a % 6 >= 2:
                    for s in range(2):
                        pool.dma_start(mod_rows_d[a, s].rearrange("(j n) -> j n", n=256),
                                       mod_rows[s:P:32, a % 2, :]).then_inc(s_stored[a % 2], 16)

            def broadcast(to, a, landed):
                pool.wait_ge(s_stored[a % 2], stored_value[a])
                src = bass.AP(mod_rows_d.tensor, a * 2 * D, [[0, P], [1, 2 * D]])
                pool.dma_start(to, src).then_inc(landed, 16)

            load_ada_rows(0)
            load_ada_rows(1)
            def low_rows(layer, t):
                cols = slice(t * P, (t + 1) * P)
                pool.wait_ge(s_high_rows, 4 * layer + t + 1)
                for k in (0, 2):
                    ins = pool.tensor_tensor(hT_parts[:, k:k + 2, cols], hT[:, k:k + 2, cols],
                                             high_rows(layer, k)[:, :, cols], ALU.subtract)
                ins.then_inc(s_low_rows, 1)

            def low_values(h):
                for j in (16 + 6 * h, 17 + 6 * h):
                    n = split_unit(j)
                    arrived(pool, n + 2)
                    pool.tensor_tensor(parts(n), unit(n), parts(n + 2), ALU.subtract).then_inc(s_low_v, 1)

            for a in range(2):
                store_mod_rows(a)
                load_ada_rows(a + 2)
            for t in range(4):
                low_rows(0, t)
            for a in range(2, 4):
                store_mod_rows(a)
                load_ada_rows(a + 2)
            for r in range(ROWS):
                for i in range(ROWS):
                    src = bass.AP(rpb_rev.tensor, (i - r + 7) * 31 - 48, [[1, GRID_W], [15 * 31, HEADS], [1, GRID_W]])
                    dst = A(A_BIAS + (r // 2) * 2048, HEADS, ROWS, GRID_W)[
                        GRID_W * (r % 2):GRID_W * (r % 2) + GRID_W, :, i, :]
                    pool.dma_start(dst, src).then_inc(s_bias, 16)
            store_mod_rows(4)
            load_ada_rows(6)
            gate_rows = bc_gate[:, :, :].rearrange("p s d -> p (s d)")
            done(pool, job("v", 3))
            broadcast(gate_rows, 2, s_gate)

            def router_weights(layer):
                pool.dma_start(rw[:, :, 0:GROUPS], router_gw[layer].rearrange("(k p) n -> p k n", p=P)
                               ).then_inc(s_rw, 16)
                pool.dma_start(rw[:, :, GROUPS:36], router_ew[layer].rearrange("(k p) n -> p k n", p=P)
                               ).then_inc(s_rw, 16)
                pool.dma_start(rb[:, 0:GROUPS], bass.AP(router_gb.tensor, layer * GROUPS, [[0, P], [1, GROUPS]])
                               ).then_inc(s_rw, 16)
                pool.dma_start(rb[:, GROUPS:36], bass.AP(router_eb.tensor, layer * EXPERTS, [[0, P], [1, EXPERTS]])
                               ).then_inc(s_rw, 16)

            step(pool.memset(table[:, :], NO_ID))
            for layer in range(2):
                for m in range(TILES[layer]):
                    pool.dma_start(table_d[layer][m * P * EXPERTS:(m + 1) * P * EXPERTS, :].rearrange(
                        "(p n) a -> p (n a)", p=P), table[:, :]).then_inc(s_table_clear if layer else s_scat[m], 16)
            router_weights(0)

            def scale_and_shift(layer):
                if layer == 0:
                    taken(pool, job("s", 4 * HEADS - 1))
                else:
                    done(pool, job("ro", R_HEADS - 1, 1))
                broadcast(A(A_BCA, 2 * D), 6 * layer + 4, s_ab)
                broadcast(A(A_BCB, 2 * D), 6 * layer + 3, s_ab)

            def second_gate(layer):
                pool.wait_ge(s_mixed, 4 if layer == 0 else 6)
                if layer == 0:
                    pool.wait_ge(s_addr, 1)
                    for at, s_, c0, n in ((None, 0, 0, D), (A_GATE_C[0], 1, 0, D // 2),
                                          (A_GATE_C[1], 1, D // 2, D // 2)):
                        pool.wait_ge(s_stored[1], stored_value[5])
                        to = bc_gate[:, 0, :] if at is None else A(at, n)
                        pool.dma_start(to, bass.AP(mod_rows_d.tensor, (5 * 2 + s_) * D + c0, [[0, P], [1, n]])
                                       ).then_inc(s_gate, 16)
                else:
                    broadcast(gate_rows, 11, s_gate)

            def experts(layer):
                S = SLOTS[layer]
                nt = TILES[layer]
                n0 = job("moe", layer)
                rows_out = nt * P * 4
                done(pool, job("rT", layer, nt - 1, 1))
                pool.wait_ge(s_h2_out, 64 if layer == 0 else 96)
                pool.wait_ge(s_idx, layer + 1)

                def gather(expert, u, copies):
                    pool.tensor_copy(gnow[0:S, u:u + 1], gidx[0:S, bass.ds(expert, 1)]).then_inc(s_now, 1)
                    pool.wait_ge(s_now, copies)
                    pool.sem_inc(s_pool_seen, 1)
                    pool.indirect_dma_start(
                        A(A_XG + u * D, D)[0:S, :], None, h2_d[layer],
                        bass.IndirectOffsetOnAxis(gnow[0:S, u:u + 1], 0),
                        bounds_check=nt * P - 1, oob_is_err=False).then_inc(s_gath[u], 16)

                def scatter(expert, u, turn, copies):
                    taken(pool, n0 + PER_EXPERT * u + 3, turn)
                    pool.tensor_copy(snow[0:2 * S, u:u + 1], sidx[0:2 * S, bass.ds(expert, 1)]).then_inc(s_now, 1)
                    pool.wait_ge(s_now, copies)
                    pool.sem_inc(s_pool_seen, 1)
                    pool.indirect_dma_start(
                        y_d[layer], bass.IndirectOffsetOnAxis(snow[0:2 * S, u:u + 1], 0),
                        A(A_YS + u * 512, 512)[0:2 * S, :], None,
                        bounds_check=rows_out - 1, oob_is_err=False).then_inc(s_scat[u], 16)

                base = layer * 2 * EXPERTS
                for u in range(EPI):
                    gather(u, u, base + u + 1)
                base += EPI
                if layer == 0:
                    store_mod_rows(11)
                second_gate(layer)
                with pool.Fori(0, TURNS - 1) as it:
                    for u in range(EPI):
                        scatter(it * EPI + u, u, it, it * 2 * EPI + (base + 2 * u + 1))
                        gather(it * EPI + (EPI + u), u, it * 2 * EPI + (base + 2 * u + 2))
                base += (TURNS - 1) * 2 * EPI
                for u in range(EPI):
                    scatter(EXPERTS - EPI + u, u, TURNS - 1, base + u + 1)
                for u in range(EPI):
                    pool.wait_ge(s_scat[u], 16 * (TURNS * (layer + 1) + 1))

            def overflow(layer):
                S = SLOTS[layer]
                nt = TILES[layer]
                pool.wait_ge(s_idx, layer + 1)
                count = pool.value_load(fullest[0:1, 0:1], min_val=0, max_val=4 * P)
                passes = nt * P // S - 1
                with pool.If(count > S):
                    pool.wait_ge(s_addr, layer + 1)
                    pool.wait_ge(s_table_clear, 16 * TILES[1])
                    for t in range(nt):
                        for k in range(2):
                            pool.indirect_dma_start(table_d[layer], bass.IndirectOffsetOnAxis(addr[:, k, t:t + 1], 0),
                                                    table[:, 4 * k + t:4 * k + t + 1], None,
                                                    bounds_check=nt * P * EXPERTS - 1, oob_is_err=False
                                                    ).then_inc(ov[layer, "set"], 16)
                    pool.wait_ge(ov[layer, "set"], 16 * 2 * nt)
                    with pool.Fori(0, passes) as b:
                        with pool.Fori(0, EXPERTS) as e:
                            n = b * EXPERTS + e
                            for half in range(2):
                                pool.dma_start(
                                    ov_table[half * S:(half + 1) * S, :],
                                    table_d[layer].rearrange("(r e) a -> r (e a)", e=EXPERTS)[
                                        bass.ds(b * S + S, S), bass.ds(e, 1)],
                                    allow_slow_non_contiguous=True).then_inc(ov[layer, "ix"], 16)
                            pool.wait_ge(ov[layer, "idx"], n + 1)
                            pool.sem_inc(s_pool_seen, 1)
                            pool.indirect_dma_start(A(A_XG, D)[0:S, :], None, h2_d[layer],
                                                    bass.IndirectOffsetOnAxis(ov_idx[0:S, 0:1], 0),
                                                    bounds_check=nt * P - 1, oob_is_err=False
                                                    ).then_inc(ov[layer, "g"], 16)
                            pool.wait_ge(ov[layer, "a4"], n + 1)
                            pool.sem_inc(s_pool_seen, 1)
                            pool.indirect_dma_start(y_d[layer], bass.IndirectOffsetOnAxis(ov_idx[0:2 * S, 1:2], 0),
                                                    A(A_YS, 512)[0:2 * S, :], None,
                                                    bounds_check=nt * P * 4 - 1, oob_is_err=False
                                                    ).then_inc(ov[layer, "scat"], 16)
                            pool.wait_ge(ov[layer, "scat"], n * 16 + 16)
                            pool.sem_inc(s_pool_seen, 1)

            for a in range(5, 10):
                store_mod_rows(a)
                load_ada_rows(a + 2)
            scale_and_shift(0)
            store_mod_rows(10)
            experts(0)
            overflow(0)
            pool.dma_start(A(A_ROPE, 4 * SEQ), ret_c[:, 6 * SEQ:RET_N]).then_inc(s_rope_in, 16)
            for t in range(2):
                low_rows(1, t)
            pool.wait_ge(s_comb, 4)
            pool.dma_start(A(A_RTAB, 6 * SEQ), ret_c[:, 0:6 * SEQ]).then_inc(s_ret_in, 16)
            low_values(0)
            for t in range(2, 4):
                low_rows(1, t)
            for h in range(1, R_HEADS):
                low_values(h)
            done(pool, job("rv", R_HEADS - 1, 3))
            broadcast(gate_rows, 8, s_gate)
            router_weights(1)
            scale_and_shift(1)
            experts(1)
            overflow(1)
            pool.dma_start(A(A_SQUARES, D), bass.AP(final_g.tensor, 0, [[0, P], [1, D]])).then_inc(s_fin_g, 16)

        @block.scalar
        def _(act):
            act.wait_ge(s_c, 32)
            act.activation(csil, crow, ACT.Silu).then_inc(s_csil, 1)

            act.wait_ge(s_dec_in, 32)
            act.activation(dec[:, 8:16], dec[:, 0:8], ACT.Exp).then_inc(s_dec, 1)
            act.wait_ge(s_dec, 2)
            act.activation(dec[:, 24:32], dec[:, 16:24], ACT.Ln).then_inc(s_dec, 1)

            ms_count = [0]
            root_count = [0]

            def mean_squares(tiles, squares, wait=None):
                for t in tiles:
                    if wait:
                        wait(t)
                    act.activation(squares or A(A_Y[t], D), res[:, t, :], ACT.Square,
                                   accum_out=stat[:, 0, t:t + 1]).then_inc(s_ms, 1)
                    ms_count[0] += 1
                    act.wait_ge(s_ms, ms_count[0])

            def roots(a, b):
                root_count[0] += 1
                act.wait_ge(s_rstd, root_count[0])
                act.activation(stat[:, 1, a:b], stat[:, 0, a:b], ACT.Sqrt).then_inc(s_root, 1)

            idle_hT = hT[:, 4:6, :].rearrange("p a b -> p (a b)")
            act.wait_ge(s_x, 32)
            mean_squares(range(4), idle_hT)
            roots(0, 4)

            def high_weights(*js):
                for j in js:
                    n = split_unit(j)
                    arrived(act, n)
                    room(act, n + 2)
                    act.activation(parts(n + 2), unit(n), ACT.Copy).then_inc(arrived_s[(n + 2) % RING], 16)

            def turn_rows(layer, tiles):
                for t in tiles:
                    n = job("hT", layer, t, 0)
                    taken(act, job("modT", layer, 1))
                    done(act, n)
                    s = t // 2
                    for k in range(4):
                        ins = act.activation(hT[:, k, t * P:(t + 1) * P], bank(n)[:, k * P:(k + 1) * P], ACT.Identity,
                                             bias=modT[:, layer, 0, k, s:s + 1], scale=modT[:, layer, 1, k, s:s + 1])
                    ins.then_inc(free_s[n % BANKS], 1)
                    taken(act, n)
                    if layer:
                        act.wait_ge(s_comb, 2)
                    act.activation(gate_parts[:, :, t * P:(t + 1) * P], hT[:, 0:4, t * P:(t + 1) * P],
                                   ACT.Copy).then_inc(s_high_rows, 1)

            high_weights(0)
            turn_rows(0, range(4))
            high_weights(1, 2)
            for ch in range(4):
                n = job("ac", ch)
                done(act, n)
                if ch:
                    taken(act, job("ax", ch - 1))
                act.activation(A(A_CONV, 512), bank(n)[:, :], ACT.Copy).then_inc(free_s[n % BANKS], 1)
                high_weights(*((3,), (4, 5), (6, 7), (8, 9))[ch])
            for ch in range(4):
                n = job("q", ch)
                done(act, n)
                act.activation(A(A_Q, 4, 512)[:, ch, :], bank(n)[:, :], ACT.Copy).then_inc(free_s[n % BANKS], 1)
            high_weights(10, 11)
            for ch in range(4):
                n = job("k", ch)
                done(act, n)
                act.activation(A(A_K, 4, 512)[:, ch, :], bank(n)[:, :], ACT.Copy).then_inc(free_s[n % BANKS], 1)
            for t in range(4):
                n = job("v", t)
                done(act, n)
                act.activation(A(A_V, 4, 512)[:, t, :], bank(n)[:, :], ACT.Copy).then_inc(free_s[n % BANKS], 1)

            def turned(i):
                n = job("pt", i)
                h, qt = divmod(i, 4)
                keys = 4 if qt < 2 else 2
                done(act, n)
                act.activation(A(A_PT + (i // 2 % 2) * 1024, 4, SEQ)[:, 0:keys, (qt % 2) * P:(qt % 2 + 1) * P],
                               bank(n)[:, 0:keys * P].rearrange("p (k q) -> p k q", q=P), ACT.Copy
                               ).then_inc(free_s[n % BANKS], 1)

            for i in range(ITEMS):
                p, s0 = probs(i), 4 * (i % 4)
                act.wait_ge(s_max, i + 1)
                act.activation(p, p, ACT.Exp, bias=soft[:, s0:s0 + 1], accum_out=soft[:, s0 + 1:s0 + 2]
                               ).then_inc(s_exp, 1)
                if i > 1:
                    turned(i - 2)
            turned(ITEMS - 2)
            turned(ITEMS - 1)

            def expert_rows_turned(layer):
                nt = TILES[layer]
                base = 0 if layer == 0 else 4
                for tiles in NORM2_GROUPS[layer]:
                    mean_squares(tiles, A(A_SQUARES, D), wait=lambda t: act.wait_ge(s_mixed, base + t + 1))
                    roots(tiles[0], tiles[-1] + 1)
                for t in range(nt):
                    n = job("rT", layer, t, 0)
                    done(act, n)
                    act.activation(hT[:, 0:4, t * P:(t + 1) * P],
                                   bank(n)[:, :].rearrange("p (k q) -> p k q", q=P), ACT.Copy
                                   ).then_inc(free_s[n % BANKS], 1)
                for k in range(2):
                    act.wait_ge(s_gap, 2 * layer + k + 1)
                    src, dst = ((A_ROUTE + 1408, A_ROUTE + 1424), (A_ROUTE + 1500, A_ROUTE + 1504))[k]
                    w = (nt * GROUPS, nt)[k]
                    act.activation(A(dst, w), A(src, w), ACT.Exp).then_inc(s_rexp, 1)

            def experts(layer):
                S = SLOTS[layer]
                n0 = job("moe", layer)
                with act.Fori(0, TURNS) as it:
                    for u in range(EPI):
                        n = n0 + PER_EXPERT * u
                        b = u % 2
                        done(act, n, it)
                        act.activation(A(A_XGT + b * 512, KC * S), bank(n)[:, 0:KC * S],
                                       ACT.Copy).then_inc(free_s[n % BANKS], 1)
                        done(act, n + 1, it)
                        act.activation(A(A_SL + b * 256, 256)[0:S, :], bank(n + 1)[0:S, 0:HIDDEN], ACT.Silu
                                       ).then_inc(s_silu, 1)
                        done(act, n + 2, it)
                        act.activation(A(A_HIDT + b * 128, 2 * S), bank(n + 2)[:, 0:2 * S], ACT.Copy
                                       ).then_inc(free_s[(n + 2) % BANKS], 1)

            def overflow(layer):
                S = SLOTS[layer]
                act.wait_ge(s_idx, layer + 1)
                count = act.value_load(fullest[0:1, 0:1], min_val=0, max_val=4 * P)
                o = lambda k: ov[layer, k]
                with act.If(count > S):
                    for u in range(EPI):
                        act.wait_ge(s_scat[u], 16 * (TURNS * (layer + 1) + 1))
                    with act.Fori(0, (TILES[layer] * P // S - 1) * EXPERTS) as n:
                        act.wait_ge(o("p1"), n + 1)
                        act.activation(A(A_XGT, KC * S), banks[0][:, 0:KC * S], ACT.Copy).then_inc(o("a1"), 1)
                        act.wait_ge(o("p2"), n + 1)
                        act.activation(A(A_SL, 256)[0:S, :], banks[1][0:S, 0:HIDDEN], ACT.Silu
                                       ).then_inc(o("a2"), 1)
                        act.wait_ge(o("p3"), n + 1)
                        act.activation(A(A_HIDT, 2 * S), banks[2][:, 0:2 * S], ACT.Copy).then_inc(o("a3"), 1)
                        act.wait_ge(o("y"), n + 2)
                        act.activation(A(A_YS, 512)[0:2 * S, :], banks[3][0:2 * S, :], ACT.Copy).then_inc(o("a4"), 1)

            expert_rows_turned(0)
            experts(0)
            overflow(0)

            def weigh_first(layer, t):
                act.wait_ge(s_y_in[t], 16 * (layer + 1))
                y = A(A_Y[t], D)
                act.activation(y, y, ACT.Copy, scale=gates[:, 0, t:t + 1]).then_inc(s_first, 1)

            def combined(base):
                return lambda t: act.wait_ge(s_comb, base + t + 1)

            high_weights(12, 13)
            for t in range(3):
                weigh_first(0, t)
            mean_squares(range(2), None, combined(0))
            roots(0, 2)
            weigh_first(0, 3)
            turn_rows(1, range(2))
            high_weights(14, 15, 16, 17)
            mean_squares(range(2, 4), None, combined(0))
            roots(2, 4)

            def silu_gate(h):
                for t in range(2):
                    n = job("rg", h, t)
                    done(act, n)
                    act.activation(ret_gate(h)[:, t, :], bank(n)[:, :], ACT.Silu).then_inc(free_s[n % BANKS], 1)

            def keep_values(h, tiles):
                for t in tiles:
                    n = job("rv", h, t)
                    done(act, n)
                    act.activation(A(A_RV, 4, 512)[:, t, :], bank(n)[:, :], ACT.Copy).then_inc(free_s[n % BANKS], 1)

            silu_gate(0)
            turn_rows(1, range(2, 4))
            keep_values(0, range(2))

            acts = [0]

            def mark(ins):
                acts[0] += 1
                ins.then_inc(s_rexps, 1)

            tab = lambda k: A(A_RTAB + 512 * k, 512)
            for h in range(R_HEADS):
                for ch in range(2):
                    n = job("rk", h, ch)
                    done(act, n)
                    act.activation(A(A_RK, 2, 512)[:, ch, SEQ:512], bank(n)[:, SEQ:512], ACT.Copy).then_inc(s_ctx_keys, 1)
                if h == 0:
                    act.wait_ge(s_ret_in, 16)
                    act.wait_ge(s_dec, 6)
                else:
                    done(act, job("ro", h - 1, 1))
                    act.wait_ge(s_yms, 2 * h)
                mark(act.activation(A(A_RD, 512), tab(1), ACT.Exp, scale=dec[:, 24 + h:25 + h]))
                mark(act.activation(A(A_EXP, 512), tab(2), ACT.Exp, scale=dec[:, 28 + h:29 + h]))
                act.wait_ge(s_factors, 2 * h + 1)
                mark(act.activation(A(A_RD + 512, 512), tab(0), ACT.Exp, scale=dec[:, 24 + h:25 + h],
                                    bias=dec[:, 32 + h:33 + h]))
                mark(act.activation(A(A_EXP, 512), tab(0), ACT.Exp, scale=dec[:, h:h + 1],
                                    bias=dec[:, 36 + h:37 + h]))
                high_weights(*range(18 + 6 * h, 22 + 6 * h))
                keep_values(h, range(0 if h else 2, 4))
                if h + 1 == R_HEADS:
                    act.activation(hT_flat_parts[:, 0:12 * SEQ], A(A_RY, 12 * SEQ), ACT.Copy).then_inc(s_ry_high, 1)
                for t in range(2):
                    i = 2 * h + t
                    n = job("ro", h, t)
                    done(act, n)
                    if t:
                        act.wait_ge(s_yms, i)
                    act.activation(A(A_EXP, 512), bank(n)[:, :], ACT.Square, accum_out=soft[:, t:t + 1]).then_inc(s_yms, 1)
                    act.wait_ge(s_yroot, 2 * i + 1)
                    act.activation(soft[:, 4 + t:5 + t], soft[:, 2 + t:3 + t], ACT.Sqrt).then_inc(s_yroot, 1)
                high_weights(22 + 6 * h, 23 + 6 * h)
                if h + 1 < R_HEADS:
                    silu_gate(h + 1)
                else:
                    high_weights(OUT_J + 6, OUT_J + 7)
                for t in range(2):
                    n = job("ryT", h, t)
                    done(act, n)
                    act.activation(A(A_RY, 16, SEQ)[:, 4 * h:4 * h + 4, t * P:(t + 1) * P],
                                   bank(n)[:, :].rearrange("p (k q) -> p k q", q=P), ACT.Copy
                                   ).then_inc(free_s[n % BANKS], 1)
            for t in range(2):
                taken(act, job("ryT", R_HEADS - 1, t))
            act.activation(hT_flat_parts[:, 12 * SEQ:], A(A_RY + 12 * SEQ, 4 * SEQ), ACT.Copy).then_inc(s_ry_high, 1)
            expert_rows_turned(1)
            experts(1)
            overflow(1)
            for t in range(2):
                weigh_first(1, t)
            for t in range(2):
                mean_squares([t], idle_hT, combined(4))
                roots(t, t + 1)

        @block.tensor
        def _(pe):
            def product(n, where, pairs, start=True, last=True, mark=True):
                for i, (stationary, moving) in enumerate(pairs):
                    ins = pe.matmul(where, stationary, moving, start=(start and i == 0), stop=(last and i == len(pairs) - 1))
                if mark:
                    ins.then_inc(full_s[n % BANKS], 1)
                return ins

            def turn(n, to, what, size, mark):
                ins = pe.transpose(to, what, ident[0:size, 0:size])
                if mark:
                    ins.then_inc(full_s[n % BANKS], 1)

            pe.wait_ge(s_con, 16)
            pe.wait_ge(s_csil, 1)
            n = job("cT")
            turn(n, bank(n)[:, 0:16], csil, 16, True)
            n = job("cwT")
            pe.wait_ge(s_cw, 16)
            turn(n, bank(n)[:, 0:12], cwrow, 12, True)

            def ada(layer, q, ks=range(KC)):
                u0 = U_ADA[6 * layer + q]
                n = job("ada", layer, q)
                if ks[0] == 0:
                    begin(pe, n)
                    for j in range(4):
                        arrived(pe, u0 + j)
                for k in ks:
                    for j in range(4):
                        ins = pe.matmul(bank(n)[32 * j:32 * j + 32, 0:256], cvec[:, k, :],
                                        unit(u0 + j)[:, 256 * k:256 * k + 256], start=(k == 0), stop=(k == KC - 1))
                if ks[-1] == KC - 1:
                    ins.then_inc(full_s[n % BANKS], 1)

            def mod_turn(layer, q):
                a = 6 * layer + q
                n = job("modT", layer, q)
                begin(pe, n)
                taken(pe, job("ada", layer, q))
                for half in range(2):
                    turn(n, bank(n)[:, half * P:(half + 1) * P], mod_rows[:, a % 2, half * P:(half + 1) * P], P, half == 1)

            taken(pe, job("cT"))
            for q in range(2):
                ada(0, q)
            for q in range(2):
                mod_turn(0, q)

            def turn_rows(layer, tiles):
                for t in tiles:
                    pe.wait_ge(s_xn, 4 * layer + t + 1)
                    for half in range(2):
                        n = job("hT", layer, t, half)
                        begin(pe, n)
                        xn = A(norm_place(layer, t), D)
                        for k in range(4):
                            turn(n, bank(n)[:, k * P:(k + 1) * P], xn[:, (4 * half + k) * P:(4 * half + k + 1) * P], P, k == 3)

            def rows_ready(layer, tiles):
                pe.wait_ge(s_rows, 4 * layer + tiles[-1] + 1)
                pe.wait_ge(s_low_rows, 4 * layer + tiles[-1] + 1)

            turn_rows(0, range(4))
            rows_ready(0, range(4))

            def row_parts(layer, k, t0, w):
                return (high_rows(layer, k // 2 * 2)[:, k % 2, t0:t0 + w], hT_parts[:, k, t0:t0 + w])

            def w_parts(j, k, c0, w):
                n = split_unit(j)
                return tuple(parts(i)[:, 256 * k + c0:256 * k + c0 + w] for i in (n + 2, n))

            def three(a, b):
                return [(a[0], b[0]), (a[0], b[1]), (a[1], b[0])]

            def weights_ready(j):
                h, m = divmod(j - 12, 6)
                if j >= OUT_J:
                    pe.wait_ge(s_low, 28 + j - OUT_J + 1)
                elif j < 12:
                    pe.wait_ge(s_low, j + 1)
                elif m < 4:
                    pe.wait_ge(s_low, 12 + 4 * h + m + 1)
                else:
                    pe.wait_ge(s_low_v, 2 * h + m - 4 + 1)

            def by_weights(n, layer, j, c0, t0, w, to, mark=True):
                product(n, to, [p for k in range(KC) for p in three(w_parts(j, k, c0, P), row_parts(layer, k, t0, w))],
                        mark=mark)

            def by_rows(n, layer, j, t):
                product(n, bank(n)[:, :], [p for k in range(KC) for p in three(
                    row_parts(layer, k, t * P, P),
                    tuple(two_units(split_unit(j) + i, k) for i in (2, 0)))])

            for ch in range(4):
                for m, name in enumerate(("ac", "ax", "ab")):
                    n = job(name, ch)
                    j = 3 * (ch // 2) + m
                    begin(pe, n)
                    weights_ready(j)
                    by_weights(n, 0, j, P * (ch % 2), 0, 4 * P, bank(n)[:, :])
            for name, j0 in (("q", 6), ("k", 8)):
                ada(0, j0 // 2 - 1)
                for ch in range(4):
                    n = job(name, ch)
                    begin(pe, n)
                    weights_ready(j0 + ch // 2)
                    by_weights(n, 0, j0 + ch // 2, P * (ch % 2), 0, 4 * P, bank(n)[:, :])

            def two_units(u0, k):
                a = u0 % RING
                return ring_parts[:, a:a + 2, 256 * k:256 * k + 256]

            ada(0, 4)
            for t in range(4):
                n = job("v", t)
                begin(pe, n)
                weights_ready(11)
                by_rows(n, 0, 10, t)

            def scores(i):
                h, qt = divmod(i, 4)
                b = HEAD_DIM * (h % 2)
                n = job("s", i)
                begin(pe, n)
                k0 = 0 if qt < 2 else SEQ
                product(n, bank(n)[:, 0:512 - k0],
                        [(A(A_Q, 4, 512)[b:b + HEAD_DIM, h // 2, qt * P:(qt + 1) * P],
                          A(A_K, 4, 512)[b:b + HEAD_DIM, h // 2, k0:512])])

            def turn_probs(i):
                n = job("pt", i)
                begin(pe, n)
                pe.wait_ge(s_probs, i + 1)
                keys = 4 if i % 4 < 2 else 2
                for k in range(keys):
                    turn(n, bank(n)[:, k * P:(k + 1) * P], probs(i)[:, k * P:(k + 1) * P], P, k == keys - 1)

            def mix_values(j):
                h, s = divmod(j, 2)
                n = job("pv", j)
                begin(pe, n)
                taken(pe, job("pt", 2 * j))
                taken(pe, job("pt", 2 * j + 1))
                b = HEAD_DIM * (h % 2)
                kts = range(4) if s == 0 else range(2, 4)
                product(n, bank(n)[b:b + HEAD_DIM, 0:SEQ],
                        [(A(A_V, 4, 512)[:, kt, h * HEAD_DIM:(h + 1) * HEAD_DIM],
                          A(A_PT + (j % 2) * 1024, 4, SEQ)[:, kt - kts[0], :]) for kt in kts])

            for ch in range(4):
                taken(pe, job("q", ch))
                taken(pe, job("k", ch))
                taken(pe, job("v", ch))
            for i in range(AHEAD):
                scores(i)
            for i in range(ITEMS):
                if i + AHEAD < ITEMS:
                    scores(i + AHEAD)
                turn_probs(i)
                if i % 2 and i > 1:
                    mix_values((i - 3) // 2)
                for part, ks in enumerate((range(3), range(3, 6), range(6, KC))):
                    name, layer, q = AFTER_ITEM.get(i - part, ("", 0, 0))
                    if name == "ada":
                        ada(layer, q, ks)
                if AFTER_ITEM.get(i, ("",))[0] == "modT":
                    mod_turn(*AFTER_ITEM[i][1:])
            mix_values(ITEMS // 2 - 1)

            def mixed(k):
                return A(A_YC, 4, 512)[:, k, :] if k < 4 else hT[:, k - 4, :]

            def project_out(i):
                t, half = divmod(i, 2)
                n = job("wo", 0, t, half)
                begin(pe, n)
                for m in range(4):
                    arrived(pe, U_WOUT_E + m)
                product(n, bank(n)[:, :],
                        [(mixed(k)[:, t * P:(t + 1) * P],
                          unit(U_WOUT_E + k // 2)[:, D * (k % 2) + 512 * half:D * (k % 2) + 512 * half + 512])
                         for k in range(8)])

            for ch in range(4):
                taken(pe, job("ab", ch))
            for j in range(2 * HEADS):
                taken(pe, job("pv", j))
            for i in range(8):
                project_out(i)
                if i in AFTER_WO:
                    ada(*AFTER_WO[i])

            def route(layer):
                S = SLOTS[layer]
                nt = TILES[layer]
                w = nt * P // 2
                for part in range(2):
                    tiles = range(nt // 2 * part, nt // 2 * (part + 1))
                    for t in tiles:
                        pe.wait_ge(s_h2, (0 if layer == 0 else 4) + t + 1)
                        for half in range(2):
                            n = job("rT", layer, t, half)
                            begin(pe, n)
                            for k in range(4):
                                at = (4 * half + k) * P
                                turn(n, bank(n)[:, k * P:(k + 1) * P], A(A_H2[layer] + t * D, D)[:, at:at + P], P, k == 3)
                    n = job("logitsT", layer, part)
                    begin(pe, n)
                    pe.wait_ge(s_rw, 64 * (layer + 1))
                    for t in tiles:
                        for half in range(2):
                            taken(pe, job("rT", layer, t, half))
                    product(n, bank(n)[0:36, 0:w],
                            [(rw[:, k, :], hT[:, k, w * part:w * (part + 1)]) for k in range(KC)])
                n = job("logits", layer)
                begin(pe, n)
                for part in range(2):
                    taken(pe, job("logitsT", layer, part))
                for t in range(nt):
                    ins = pe.transpose(bank(n)[:, 64 * t:64 * t + 36], A(A_LOGITS, 4 * P)[0:36, t * P:(t + 1) * P],
                                       ident[0:36, 0:36])
                ins.then_inc(full_s[n % BANKS], 1)
                n = job("ranks", layer)
                begin(pe, n)
                pe.wait_ge(s_members, layer + 1)
                member = A(A_ROUTE + 640, 5 * EXPERTS)
                w = (nt + 1) * EXPERTS
                product(n, bank(n)[:, 0:w], [(const("upper"), member[:, 0:w])], last=False, mark=False)
                for back in range(1, nt + 1):
                    product(n, bank(n)[:, EXPERTS * back:w], [(const("ones"), member[:, 0:w - EXPERTS * back])],
                            start=False, last=back == nt, mark=back == nt)
                n = job("table", layer)
                begin(pe, n)
                pe.wait_ge(s_hot, layer + 1)
                hot, valued = A(A_HOT, 8, S), A(A_VALUED, 8, EXPERTS)
                for i in range(2 * nt):
                    for half in range(2):
                        at = 4 * (i // nt) + i % nt
                        ins = pe.matmul(bank(n)[S * half:S * (half + 1), 0:EXPERTS], hot[:, at, :],
                                        valued[:, at, :], start=(i == 0), stop=(i == 2 * nt - 1))
                ins.then_inc(full_s[n % BANKS], 1)

            def experts(layer):
                S = SLOTS[layer]
                n0 = job("moe", layer)
                u0 = (U_MOE0, U_MOE1)[layer]
                with pe.Fori(0, TURNS) as it:
                    for u in range(EPI):
                        n = n0 + PER_EXPERT * u
                        b = u % 2
                        begin(pe, n, it)
                        pe.wait_ge(s_gath[u], it * 16 + 16 * (TURNS * layer + 1))
                        pe.sem_inc(s_pe_seen, 1)
                        for k in range(KC):
                            turn(n, bank(n)[:, S * k:S * (k + 1)],
                                 A(A_XG + u * D, D)[0:S, k * P:(k + 1) * P], S, k == KC - 1)
                        begin(pe, n + 1, it)
                        arrived(pe, u0 + 3 * u, it)
                        arrived(pe, u0 + 3 * u + 1, it)
                        taken(pe, n, it)
                        for k in range(KC):
                            for w in range(2):
                                ins = pe.matmul(bank(n + 1)[S * w:S * (w + 1), 0:HIDDEN],
                                                A(A_XGT + b * 512 + S * k, S),
                                                unit(u0 + 3 * u + w)[:, 256 * k:256 * (k + 1)],
                                                start=(k == 0), stop=(k == KC - 1))
                        ins.then_inc(full_s[(n + 1) % BANKS], 1)
                        begin(pe, n + 2, it)
                        taken(pe, n + 1, it)
                        pe.sem_inc(s_pe_seen, 1)
                        for k in range(2):
                            turn(n + 2, bank(n + 2)[:, S * k:S * (k + 1)],
                                 A(A_HID + b * 256, 256)[0:S, k * P:(k + 1) * P], S, k == 1)
                        begin(pe, n + 3, it)
                        arrived(pe, u0 + 3 * u + 2, it)
                        taken(pe, n + 2, it)
                        for k in range(2):
                            for w in range(2):
                                ins = pe.matmul(bank(n + 3)[S * w:S * (w + 1), :],
                                                A(A_HIDT + b * 128 + S * k, S),
                                                unit(u0 + 3 * u + 2)[:, D * k + 512 * w:D * k + 512 * (w + 1)],
                                                start=(k == 0), stop=(k == 1))
                        ins.then_inc(full_s[(n + 3) % BANKS], 1)

            def overflow(layer):
                S = SLOTS[layer]
                n0 = job("moe", layer)
                pe.wait_ge(s_idx, layer + 1)
                count = pe.value_load(fullest[0:1, 0:1], min_val=0, max_val=4 * P)
                o = lambda k: ov[layer, k]
                total = (TILES[layer] * P // S - 1) * EXPERTS
                with pe.If(count > S):
                    for b in range(BANKS):
                        taken(pe, n0 + EXPERTS * PER_EXPERT - BANKS + b)
                    pe.nop().then_inc(o("y"), 1)
                    with pe.Fori(0, total) as n:
                        pe.wait_ge(o("g"), n * 16 + 16)
                        pe.sem_inc(s_pe_seen, 1)
                        for k in range(KC):
                            ins = pe.transpose(banks[0][:, S * k:S * (k + 1)],
                                               A(A_XG, D)[0:S, k * P:(k + 1) * P], ident[0:S, 0:S])
                        ins.then_inc(o("p1"), 1)
                        pe.wait_ge(o("w"), n * 48 + 48)
                        pe.wait_ge(o("a1"), n + 1)
                        for k in range(KC):
                            for w in range(2):
                                ins = pe.matmul(banks[1][S * w:S * (w + 1), 0:HIDDEN],
                                                A(A_XGT + S * k, S), unit(w)[:, 256 * k:256 * (k + 1)],
                                                start=(k == 0), stop=(k == KC - 1))
                        ins.then_inc(o("p2"), 1)
                        pe.wait_ge(o("d2"), n + 1)
                        pe.sem_inc(s_pe_seen, 1)
                        for k in range(2):
                            ins = pe.transpose(banks[2][:, S * k:S * (k + 1)],
                                               A(A_HID, 256)[0:S, k * P:(k + 1) * P], ident[0:S, 0:S])
                        ins.then_inc(o("p3"), 1)
                        pe.wait_ge(o("a3"), n + 1)
                        for k in range(2):
                            for w in range(2):
                                ins = pe.matmul(banks[3][S * w:S * (w + 1), :], A(A_HIDT + S * k, S),
                                                unit(2)[:, D * k + 512 * w:D * k + 512 * (w + 1)],
                                                start=(k == 0), stop=(k == 1))
                        ins.then_inc(o("y"), 1)
                        pe.wait_ge(o("a4"), n + 1)

            route(0)
            experts(0)
            overflow(0)
            def ret_q(h):
                n = job("rq", h)
                begin(pe, n)
                weights_ready(12 + 6 * h)
                for ch in range(2):
                    by_weights(n, 1, 12 + 6 * h, P * ch, 0, SEQ, bank(n)[:, SEQ * ch:SEQ * (ch + 1)], mark=(ch == 1))

            def ret_g(h):
                weights_ready(15 + 6 * h)
                for t in range(2):
                    n = job("rg", h, t)
                    begin(pe, n)
                    by_rows(n, 1, 14 + 6 * h, t)

            turn_rows(1, range(2))
            rows_ready(1, range(2))
            def ret_v(h, tiles):
                weights_ready(17 + 6 * h)
                for t in tiles:
                    n = job("rv", h, t)
                    begin(pe, n)
                    by_rows(n, 1, 16 + 6 * h, t)

            ret_q(0)
            ret_g(0)
            turn_rows(1, range(2, 4))
            ret_v(0, range(2))
            rows_ready(1, range(2, 4))

            def output_part(i, m, last):
                t, half = divmod(i, 2)
                n = job("wo", 1, t, half)
                pairs = []
                for k in (2 * m, 2 * m + 1):
                    at = SEQ * k + t * P
                    cols = slice(D * (k % 2) + 512 * half, D * (k % 2) + 512 * half + 512)
                    u = split_unit(OUT_J + m)
                    pairs += three((hT_flat_parts[:, at:at + P], arena_parts[:, A_RY + at:A_RY + at + P]),
                                   (parts(u + 2)[:, cols], parts(u)[:, cols]))
                return product(n, bank(n)[:, :], pairs, start=m == 0, last=last, mark=last)

            for h in range(R_HEADS):
                for ch in range(2):
                    n = job("rk", h, ch)
                    begin(pe, n)
                    weights_ready(13 + 6 * h)
                    by_weights(n, 1, 13 + 6 * h, P * ch, 0, 4 * P, bank(n)[:, :])
                ret_v(h, range(0 if h else 2, 4))
                taken(pe, job("rq", h))
                for ch in range(2):
                    taken(pe, job("rk", h, ch))
                pe.wait_ge(s_ctx_keys, 2 * (h + 1))
                for a in range(2):
                    n = job("rs", h, a)
                    begin(pe, n)
                    for b in range(2):
                        kt = 2 * a + b
                        product(n, bank(n)[:, SEQ * b:SEQ * (b + 1)],
                                [(A(A_RK, 2, 512)[:, ch, kt * P:(kt + 1) * P], A(A_RQ, 2, SEQ)[:, ch, :])
                                 for ch in range(2)], mark=(b == 1))
                if h + 1 < R_HEADS:
                    ret_q(h + 1)
                for t in range(4):
                    taken(pe, job("rv", h, t))
                for a in range(2):
                    taken(pe, job("rs", h, a))
                for t in range(2):
                    n = job("ro", h, t)
                    begin(pe, n)
                    product(n, bank(n)[:, :], [(A(A_RD, 4, SEQ)[:, kt, t * P:(t + 1) * P], A(A_RV, 4, 512)[:, kt, :])
                                               for kt in range(4)])
                if h + 1 < R_HEADS:
                    ret_g(h + 1)
                else:
                    pe.wait_ge(s_ry_low, 1)
                    for i in range(4):
                        begin(pe, job("wo", 1, i // 2, i % 2))
                    for m in range(6):
                        weights_ready(OUT_J + m)
                        for i in range(4):
                            ins = output_part(i, m, last=False)
                        ins.then_inc(s_wout, 1)
                for t in range(2):
                    n = job("ryT", h, t)
                    begin(pe, n)
                    taken(pe, job("ro", h, t))
                    for k in range(4):
                        turn(n, bank(n)[:, k * P:(k + 1) * P], ret_gate(h)[:, t, k * P:(k + 1) * P], P, k == 3)
            pe.wait_ge(s_ry_low, 2)
            weights_ready(OUT_J + 7)
            for i in range(4):
                for m in (6, 7):
                    output_part(i, m, last=m == 7)
            route(1)
            experts(1)
            overflow(1)

        @block.vector
        def _(dve):
            steps = [0]

            def step(ins):
                steps[0] += 1
                ins.then_inc(s_dve, 1)
                dve.wait_ge(s_dve, steps[0])

            tt, ts, stt = dve.tensor_tensor, dve.tensor_scalar, dve.scalar_tensor_tensor

            dve.wait_ge(s_zero, 2)
            n = job("cT")
            done(dve, n)
            dve.tensor_copy(cvec[:, :, 0:2], bank(n)[:, 0:16].rearrange("p (s k) -> p k s", s=2)).then_inc(free_s[n % BANKS], 1)
            n = job("cwT")
            done(dve, n)
            dve.tensor_copy(cwT[:, :], bank(n)[:, 0:12]).then_inc(free_s[n % BANKS], 1)
            taken(dve, n)

            dve.wait_ge(s_dec, 1)
            ts(dec[:, 16:24], dec[:, 8:16], -1.0, 1.0, ALU.mult, ALU.add).then_inc(s_dec, 1)
            dve.wait_ge(s_dec, 3)
            step(ts(dec[:, 32:40], dec[:, 16:24], -1.0, 1.0, ALU.mult, ALU.add))
            step(ts(dec[:, 32:40], dec[:, 32:40], 1.0e-30, None, ALU.max))
            step(dve.reciprocal(dec[:, 32:40], dec[:, 32:40]))
            step(tt(dec[:, 32:40], dec[:, 32:40], dec[:, 8:16], ALU.mult))
            tt(dec[:, 24:32], dec[:, 24:32], dec[:, 32:40], ALU.mult).then_inc(s_dec, 1)
            dve.wait_ge(s_dec, 4)
            ts(dec[:, 32:40], dec[:, 24:32], float(SEQ), None, ALU.mult).then_inc(s_dec, 1)
            ts(dec[:, 0:4], dec[:, 28:32], -1.0, None, ALU.mult).then_inc(s_dec, 1)

            ms_count = [0]
            root_count = [0]

            def reciprocal_roots(a, b):
                ms_count[0] += b - a
                root_count[0] += 1
                dve.wait_ge(s_ms, ms_count[0])
                ts(stat[:, 0, a:b], stat[:, 0, a:b], 1.0 / D, EPS, ALU.mult, ALU.add).then_inc(s_rstd, 1)
                dve.wait_ge(s_root, root_count[0])
                step(dve.reciprocal(stat[:, 2, a:b], stat[:, 1, a:b]))
                step(tt(stat[:, 1, a:b], stat[:, 2, a:b], stat[:, 2, a:b], ALU.mult))
                step(tt(stat[:, 1, a:b], stat[:, 1, a:b], stat[:, 0, a:b], ALU.mult))
                step(ts(stat[:, 1, a:b], stat[:, 1, a:b], -0.5, 1.5, ALU.mult, ALU.add))
                step(tt(stat[:, 2, a:b], stat[:, 2, a:b], stat[:, 1, a:b], ALU.mult))

            reciprocal_roots(0, 4)

            def mod_block(layer, q):
                a = 6 * layer + q
                n = job("ada", layer, q)
                rows = mod_rows[:, a % 2, :]
                bias = ada_rows[:, a % 2, 0, :]
                done(dve, n)
                dve.wait_ge(s_ada_in[a % 2], ada_in_value[a])
                if a >= 2 and stored_value[a - 2]:
                    dve.wait_ge(s_stored[a % 2], stored_value[a - 2])
                if q in (2, 3):
                    done(dve, job("modT", layer, q - 2))
                if q in (1, 4):
                    step(stt(rows, bank(n)[:, 0:256], 1.0, bias, ALU.add, ALU.add))
                    tt(rows, rows, ada_rows[:, a % 2, 1, :], ALU.mult).then_inc(free_s[n % BANKS], 1)
                else:
                    tt(rows, bank(n)[:, 0:256], bias, ALU.add).then_inc(free_s[n % BANKS], 1)

            def mod_columns(layer, q):
                n = job("modT", layer, q)
                done(dve, n)
                dve.tensor_copy(modT[:, layer, q, :, :].rearrange("p (j h) s -> p h j s", h=2),
                                bank(n)[:, 0:256].rearrange("p (h j r) -> p h j r", h=2, j=4)[:, :, :, 0:2]
                                ).then_inc(free_s[n % BANKS], 1)

            mod_block(0, 0)
            mod_block(0, 1)
            mod_columns(0, 0)
            mod_columns(0, 1)

            def normed(layer, t):
                if t >= 2:
                    done(dve, job("hT", layer, t - 2, 1))
                ts(A(norm_place(layer, t), D), res[:, t, :], stat[:, 2, t:t + 1], None, ALU.mult
                   ).then_inc(s_xn, 1)

            def turn_rows(layer, t):
                n = job("hT", layer, t, 1)
                s = t // 2
                if t == 0:
                    taken(dve, job("modT", layer, 1))
                done(dve, n)
                for k in range(4):
                    ins = ts(hT[:, 4 + k, t * P:(t + 1) * P], bank(n)[:, k * P:(k + 1) * P],
                             modT[:, layer, 1, 4 + k, s:s + 1], modT[:, layer, 0, 4 + k, s:s + 1], ALU.mult, ALU.add)
                ins.then_inc(free_s[n % BANKS], 1)
                taken(dve, n)
                cols = slice(t * P, (t + 1) * P)
                for k in (4, 6):
                    ins = dve.tensor_copy(high_rows(layer, k)[:, :, cols], hT[:, k:k + 2, cols])
                step(ins)
                for k in (4, 6):
                    ins = tt(hT_parts[:, k:k + 2, cols], hT[:, k:k + 2, cols], high_rows(layer, k)[:, :, cols],
                             ALU.subtract)
                ins.then_inc(s_rows, 1)

            def low_weights(*js):
                for j in js:
                    n = split_unit(j)
                    arrived(dve, n + 2)
                    tt(parts(n), unit(n), parts(n + 2), ALU.subtract).then_inc(s_low, 1)

            normed(0, 0)
            normed(0, 1)
            low_weights(0)
            for t in range(4):
                turn_rows(0, t)
                if t + 2 < 4:
                    normed(0, t + 2)
            low_weights(1, 2)

            padded = A(A_CONV + 512, 2, SEQ + 2)
            total = A(A_CONV + 1028, 2, SEQ)
            step(dve.memset(padded[:, :, 0:SEQ + 2:SEQ + 1], 0.0))
            for ch in range(4):
                taken(dve, job("ac", ch))
                n = job("ax", ch)
                done(dve, n)
                tt(padded[:, :, 1:SEQ + 1], A(A_CONV, 2, SEQ), bank(n)[:, :].rearrange("p (s t) -> p s t", s=2),
                   ALU.mult).then_inc(free_s[n % BANKS], 1)
                taken(dve, n)
                step(ts(total, padded[:, :, 0:SEQ], cwT[:, ch:ch + 1], None, ALU.mult))
                step(stt(total, padded[:, :, 1:SEQ + 1], cwT[:, 4 + ch:5 + ch], total, ALU.mult, ALU.add))
                step(stt(total, padded[:, :, 2:SEQ + 2], cwT[:, 8 + ch:9 + ch], total, ALU.mult, ALU.add))
                n = job("ab", ch)
                done(dve, n)
                tt(A(A_YC, 4, 512)[:, ch, :], total.rearrange("p s t -> p (s t)"), bank(n)[:, :], ALU.mult
                   ).then_inc(free_s[n % BANKS], 1)
                low_weights(*((3,), (4, 5), (6, 7), ())[ch])
            mod_block(0, 2)
            low_weights(8, 9)
            mod_block(0, 3)
            low_weights(10, 11)
            mod_block(0, 4)
            dve.wait_ge(s_bias, 16 * ROWS * ROWS)
            for qt in range(2):
                b = A(A_BIAS + qt * 2048, HEADS * ROWS, GRID_W)
                ins = tt(b, b, const("window").unsqueeze(1).to_broadcast([P, HEADS * ROWS, GRID_W]), ALU.add)
            step(ins)

            scale = float(HEAD_DIM) ** -0.5

            def attention_scores(i):
                h, qt = divmod(i, 4)
                n = job("s", i)
                p, s0 = probs(i), 4 * (i % 4)
                done(dve, n)
                if i >= 4:
                    done(dve, job("pt", i - 4))
                if qt < 2:
                    by_row = lambda v: v[:, 0:SEQ].rearrange("p (r c) -> p r c", c=GRID_W)
                    step(stt(by_row(p), by_row(bank(n)), scale,
                             A(A_BIAS + qt * 2048, HEADS, ROWS, GRID_W)[:, h, :, ::-1], ALU.mult, ALU.add))
                    ts(p[:, SEQ:512], bank(n)[:, SEQ:512], scale, None, ALU.mult).then_inc(free_s[n % BANKS], 1)
                else:
                    ts(p, bank(n)[:, 0:SEQ], scale, None, ALU.mult).then_inc(free_s[n % BANKS], 1)
                taken(dve, n)
                dve.tensor_reduce(soft[:, s0:s0 + 1], p, AX_X, ALU.max, negate=True).then_inc(s_max, 1)

            def attention_divide(i):
                p, s0 = probs(i), 4 * (i % 4)
                dve.wait_ge(s_exp, i + 1)
                step(dve.reciprocal(soft[:, s0 + 2:s0 + 3], soft[:, s0 + 1:s0 + 2]))
                ts(p, p, soft[:, s0 + 2:s0 + 3], None, ALU.mult).then_inc(s_probs, 1)

            def head_out(j):
                h, s = divmod(j, 2)
                n = job("pv", j)
                b = HEAD_DIM * (h % 2)
                done(dve, n)
                dve.tensor_copy(hT[b:b + HEAD_DIM, h // 2, s * SEQ:(s + 1) * SEQ], bank(n)[b:b + HEAD_DIM, 0:SEQ]
                                ).then_inc(free_s[n % BANKS], 1)

            for i in range(AHEAD - 1):
                attention_scores(i)
            for i in range(ITEMS):
                if i + AHEAD - 1 < ITEMS:
                    attention_scores(i + AHEAD - 1)
                attention_divide(i)
                if i % 2 == 0 and i >= 4:
                    head_out(i // 2 - 2)
                if i - 3 in AFTER_ITEM:
                    name, layer, q = AFTER_ITEM[i - 3]
                    (mod_block if name == "ada" else mod_columns)(layer, q)
            head_out(ITEMS // 2 - 2)
            head_out(ITEMS // 2 - 1)

            def add_mixer(layer, i):
                t, half = divmod(i, 2)
                n = job("wo", layer, t, half)
                done(dve, n)
                cols = slice(512 * half, 512 * half + 512)
                tmp = A(A_TMP + 512 * half, 512)
                tt(tmp, bank(n)[:, :], bc_gate[:, t // 2, cols], ALU.mult).then_inc(free_s[n % BANKS], 1)
                taken(dve, n)
                ins = tt(res[:, t, cols], res[:, t, cols], tmp, ALU.add)
                if half == 0:
                    step(ins)
                else:
                    ins.then_inc(s_mixed, 1)

            def modulated(layer, t):
                h2 = A(A_H2[layer] + t * D, D)
                step(stt(h2, res[:, t, :], stat[:, 2, t:t + 1], A(A_BCA + t // 2 * D, D), ALU.mult, ALU.mult))
                tt(h2, h2, A(A_BCB + t // 2 * D, D), ALU.add).then_inc(s_h2, 1)

            def h2_turned(layer, t):
                n = job("rT", layer, t, 1)
                done(dve, n)
                dve.tensor_copy(hT[:, 4:8, t * P:(t + 1) * P], bank(n)[:, :].rearrange("p (k q) -> p k q", q=P)
                                ).then_inc(free_s[n % BANKS], 1)

            def keep_logits(layer, part):
                n = job("logitsT", layer, part)
                w = TILES[layer] * P // 2
                done(dve, n)
                dve.tensor_copy(A(A_LOGITS, 4 * P)[0:36, w * part:w * (part + 1)], bank(n)[0:36, 0:w]
                                ).then_inc(free_s[n % BANKS], 1)

            def route(layer):
                S = SLOTS[layer]
                nt = TILES[layer]
                R = A_ROUTE
                logit = A(R, 4, 36)[:, 0:nt, :]
                in_group = A(R + 160, 4, EXPERTS)[:, 0:nt, :]
                first = A(R + 288, 4, EXPERTS)[:, 0:nt, :]
                second = A(R + 416, 4, EXPERTS)[:, 0:nt, :]
                member = A(R + 640, 4, EXPERTS)[:, 0:nt, :]
                none = A(R + 640, 5, EXPERTS)[:, nt, :]
                both = A(R + 288, 8, EXPERTS).rearrange("p (k t) e -> p k t e", k=2)[:, :, 0:nt, :]
                place = A(R + 1536, 4, EXPERTS)[:, 0:nt, :]
                scratch = A(R + 1664, 8, EXPERTS).rearrange("p (k t) e -> p k t e", k=2)[:, :, 0:nt, :]
                valued = A(A_VALUED, 8, EXPERTS).rearrange("p (k t) e -> p k t e", k=2)[:, :, 0:nt, :]
                el = A(R + 1024, 4, PER_GROUP)[:, 0:nt, :]
                cand = A(R + 1056, 4, PER_GROUP)[:, 0:nt, :]
                hot1 = A(R + 1088, 4, PER_GROUP)[:, 0:nt, :]
                hot2 = A(R + 1120, 4, PER_GROUP)[:, 0:nt, :]
                hotg = A(R + 1152, 4, GROUPS)[:, 0:nt, :]
                candg = A(R + 1168, 4, GROUPS)[:, 0:nt, :]
                m0, m1, m2, m3 = (A(R + 1200 + 4 * i, 4)[:, 0:nt] for i in range(4))
                sumg, den = (A(R + 1220 + 4 * i, 4)[:, 0:nt] for i in range(2))
                rank = A(R + 1232, 2, 4)[:, :, 0:nt]
                where = A(R + 1240, 2, 4)[:, :, 0:nt]
                count = A(R + 1260, 1)
                gap = A(R + 1408, nt, GROUPS)
                eg = A(R + 1424, nt, GROUPS)
                gap2, t2 = A(R + 1500, nt), A(R + 1504, nt)

                def wide(v, k):
                    return v.unsqueeze(2).to_broadcast([P, nt, k])

                def pick(hot, cand, values, best, idx, k):
                    step(tt(cand, values, wide(best, k), ALU.is_lt))
                    step(stt(cand, cand, BIG, idx.unsqueeze(1).to_broadcast([P, nt, k]), ALU.mult, ALU.add))
                    step(dve.tensor_reduce(m3, cand, AX_X, ALU.min))
                    step(tt(hot, cand, wide(m3, k), ALU.is_equal))

                n = job("logits", layer)
                done(dve, n)
                tt(logit, bank(n)[:, 0:64 * nt].rearrange("p (t c) -> p t c", c=64)[:, :, 0:36],
                   rb[:, :].unsqueeze(1).to_broadcast([P, nt, 36]), ALU.add).then_inc(free_s[n % BANKS], 1)
                taken(dve, n)
                step(dve.tensor_reduce(m0, logit[:, :, 0:GROUPS], AX_X, ALU.max))
                tt(gap, logit[:, :, 0:GROUPS], wide(m0, GROUPS), ALU.subtract).then_inc(s_gap, 1)
                pick(hotg, candg, logit[:, :, 0:GROUPS], m0, const("idx_group"), GROUPS)
                step(tt(in_group.rearrange("p t (g e) -> p t g e", g=GROUPS),
                        logit[:, :, GROUPS:36].rearrange("p t (g e) -> p t g e", g=GROUPS),
                        hotg.unsqueeze(3).to_broadcast([P, nt, GROUPS, PER_GROUP]), ALU.mult))
                step(dve.tensor_reduce(el, in_group.rearrange("p t (g e) -> p t e g", g=GROUPS), AX_X, ALU.add))
                step(dve.tensor_reduce(m1, el, AX_X, ALU.max))
                pick(hot1, cand, el, m1, const("idx_in_group"), PER_GROUP)
                step(stt(el, hot1, -BIG, el, ALU.mult, ALU.add))
                step(dve.tensor_reduce(m2, el, AX_X, ALU.max))
                tt(gap2, m2, m1, ALU.subtract).then_inc(s_gap, 1)
                pick(hot2, cand, el, m2, const("idx_in_group"), PER_GROUP)
                for hot, to in ((hot1, first), (hot2, second)):
                    step(tt(to.rearrange("p t (g e) -> p t g e", g=GROUPS),
                            hotg.unsqueeze(3).to_broadcast([P, nt, GROUPS, PER_GROUP]),
                            hot.unsqueeze(2).to_broadcast([P, nt, GROUPS, PER_GROUP]), ALU.mult))
                step(dve.memset(none, 0.0))
                tt(member, first, second, ALU.add).then_inc(s_members, 1)
                step(tt(valued, both,
                        const("ids").rearrange("p (k t) -> p k t", k=2)[:, :, 0:nt].unsqueeze(3).to_broadcast(
                            [P, 2, nt, EXPERTS]), ALU.mult))
                dve.wait_ge(s_rexp, 2 * layer + 2)
                step(dve.tensor_reduce(sumg, eg, AX_X, ALU.add))
                step(ts(den, t2, 1.0, None, ALU.add))
                step(tt(den, den, sumg, ALU.mult))
                step(dve.reciprocal(gates[:, 0, 0:nt], den))
                step(tt(gates[:, 1, 0:nt], gates[:, 0, 0:nt], t2, ALU.mult))
                n = job("ranks", layer)
                done(dve, n)
                ranks = bank(n)[:, 0:EXPERTS * nt].rearrange("p (t e) -> p t e", e=EXPERTS)
                for k, hot in enumerate((first, second)):
                    step(tt(scratch[:, k], ranks, hot, ALU.mult))
                step(dve.tensor_reduce(rank, scratch, AX_X, ALU.add))
                hot = A(A_HOT, 8, S)
                for block in range(S // EXPERTS):
                    for k in range(2):
                        ins = tt(hot[:, 4 * k:4 * k + nt, EXPERTS * block:EXPERTS * (block + 1)],
                                 const("idx_expert").unsqueeze(1).to_broadcast([P, nt, EXPERTS]),
                                 wide(rank[:, k], EXPERTS), ALU.is_equal)
                    if block + 1 < S // EXPERTS:
                        step(ins)
                        step(ts(rank, rank, float(EXPERTS), None, ALU.subtract))
                ins.then_inc(s_hot, 1)
                step(dve.tensor_reduce(count, bank(n)[:, EXPERTS * nt:EXPERTS * (nt + 1)], AX_X, ALU.max))
                stt(place, ranks, float(EXPERTS), const("idx_expert").unsqueeze(1).to_broadcast([P, nt, EXPERTS]),
                    ALU.mult, ALU.add).then_inc(free_s[n % BANKS], 1)
                n = job("table", layer)
                done(dve, n)
                half = const("half")[0:2 * S, layer:layer + 1]
                ts(table[0:2 * S, :], bank(n)[0:2 * S, 0:EXPERTS], float(NO_ID), None,
                   ALU.add).then_inc(free_s[n % BANKS], 1)
                taken(dve, n)
                ts(gidx[0:S, :], table[0:S, :], 1, None, ALU.logical_shift_right)
                step(ts(sidx[0:2 * S, :], table[0:2 * S, :], 2.0, half, ALU.mult, ALU.add))
                dve.tensor_copy(fullest[:, :], count).then_inc(s_idx, 1)
                dve.wait_ge(s_idx, layer + 1)
                for k, hot in enumerate((first, second)):
                    step(tt(scratch[:, k], place, hot, ALU.mult))
                step(dve.tensor_reduce(where, scratch, AX_X, ALU.add))
                step(dve.tensor_copy(addr[:, :, 0:nt], where))
                ts(table[:, 0:8], const("ids"), float(NO_ID), None, ALU.add).then_inc(s_addr, 1)

            def experts(layer):
                S = SLOTS[layer]
                n0 = job("moe", layer)
                with dve.Fori(0, TURNS) as it:
                    for u in range(EPI):
                        n = n0 + PER_EXPERT * u
                        b = u % 2
                        dve.wait_ge(s_silu, it * EPI + (EXPERTS * layer + u + 1))
                        tt(A(A_HID + b * 256, 256)[0:S, :], bank(n + 1)[S:2 * S, 0:HIDDEN],
                           A(A_SL + b * 256, 256)[0:S, :], ALU.mult).then_inc(free_s[(n + 1) % BANKS], 1)
                        done(dve, n + 3, it)
                        dve.wait_ge(s_scat[u], it * 16 + 16 * (TURNS * layer + 1))
                        dve.tensor_copy(A(A_YS + u * 512, 512)[0:2 * S, :],
                                        bank(n + 3)[0:2 * S, :]).then_inc(free_s[(n + 3) % BANKS], 1)

            def overflow(layer):
                S = SLOTS[layer]
                dve.wait_ge(s_idx, layer + 1)
                count = dve.value_load(fullest[0:1, 0:1], min_val=0, max_val=4 * P)
                o = lambda k: ov[layer, k]
                with dve.If(count > S):
                    with dve.Fori(0, (TILES[layer] * P // S - 1) * EXPERTS) as n:
                        dve.wait_ge(o("ix"), n * 32 + 32)
                        ts(ov_idx[0:S, 0:1], ov_table[0:S, :], 1, None, ALU.logical_shift_right)
                        ts(ov_idx[0:2 * S, 1:2], ov_table[0:2 * S, :], 2.0, const("half")[0:2 * S, layer:layer + 1],
                           ALU.mult, ALU.add).then_inc(o("idx"), 1)
                        dve.wait_ge(o("a2"), n + 1)
                        tt(A(A_HID, 256)[0:S, :], banks[1][S:2 * S, 0:HIDDEN], A(A_SL, 256)[0:S, :], ALU.mult
                           ).then_inc(o("d2"), 1)

            def combine(layer, t):
                dve.wait_ge(s_gate, (64, 96)[layer])
                dve.wait_ge(s_first, 4 * layer + t + 1)
                y = A(A_Y[t], 2, D)
                step(stt(y[:, 0, :], y[:, 1, :], gates[:, 1, t:t + 1], y[:, 0, :], ALU.mult, ALU.add))
                if t < 2:
                    step(tt(y[:, 0, :], y[:, 0, :], bc_gate[:, 0, :], ALU.mult))
                else:
                    for i in range(2):
                        half = y[:, 0, D // 2 * i:D // 2 * (i + 1)]
                        ins = tt(half, half, A(A_GATE_C[i], D // 2), ALU.mult)
                    step(ins)
                tt(res[:, t, :], res[:, t, :], y[:, 0, :], ALU.add).then_inc(s_comb, 1)

            dve.wait_ge(s_gate, 16)
            dve.wait_ge(s_ab, 32)
            for i in range(8):
                add_mixer(0, i)
                if i in AFTER_WO:
                    mod_block(*AFTER_WO[i])
                if i == 3:
                    reciprocal_roots(0, 2)
                if i in (4, 5):
                    modulated(0, i - 4)
            h2_turned(0, 0)
            h2_turned(0, 1)
            reciprocal_roots(2, 4)
            modulated(0, 2)
            modulated(0, 3)
            keep_logits(0, 0)
            h2_turned(0, 2)
            h2_turned(0, 3)
            keep_logits(0, 1)
            route(0)
            experts(0)
            overflow(0)

            low_weights(12, 13)
            combine(0, 0)
            combine(0, 1)
            reciprocal_roots(0, 2)
            normed(1, 0)
            normed(1, 1)
            turn_rows(1, 0)
            turn_rows(1, 1)
            combine(0, 2)
            low_weights(14, 15)
            combine(0, 3)
            reciprocal_roots(2, 4)
            normed(1, 2)
            normed(1, 3)

            tab = lambda k: A(A_RTAB + 512 * k, 512)
            rope = lambda ch, k: A(A_ROPE + (2 * ch + k) * SEQ, SEQ)

            def rotate(to, ps, ch, n, last):
                ra, rb_ = A(A_RTMP, SEQ), A(A_RTMP + SEQ, SEQ)
                step(tt(ra, ps, rope(ch, 0), ALU.mult))
                step(tt(rb_[0:64, :], ps[64:128, :], rope(ch, 1)[0:64, :], ALU.mult))
                ins = tt(rb_[64:128, :], ps[0:64, :], rope(ch, 1)[64:128, :], ALU.mult)
                step(ins)
                ins = tt(to, ra, rb_, ALU.add)
                if last:
                    ins.then_inc(free_s[n % BANKS], 1)
                    taken(dve, n)
                else:
                    step(ins)

            def low_outputs(k0, k1):
                cols = slice(A_RY + SEQ * k0, A_RY + SEQ * k1)
                dve.wait_ge(s_ry_high, 1 if k0 == 0 else 2)
                tt(arena_parts[:, cols], arena[:, cols], hT_flat_parts[:, SEQ * k0:SEQ * k1], ALU.subtract
                   ).then_inc(s_ry_low, 1)

            def rotate_q(h):
                n = job("rq", h)
                done(dve, n)
                for ch in range(2):
                    rotate(A(A_RQ, 2, SEQ)[:, ch, :], bank(n)[:, SEQ * ch:SEQ * (ch + 1)], ch, n, ch == 1)

            dve.wait_ge(s_rope_in, 16)
            rotate_q(0)
            turn_rows(1, 2)
            turn_rows(1, 3)
            dve.wait_ge(s_ret_in, 16)
            for h in range(R_HEADS):
                for ch in range(2):
                    n = job("rk", h, ch)
                    done(dve, n)
                    dve.wait_ge(s_ctx_keys, 2 * h + ch + 1)
                    rotate(A(A_RK, 2, 512)[:, ch, 0:SEQ], bank(n)[:, 0:SEQ], ch, n, True)
                dk, e = A(A_RD, 512), A(A_EXP, 512)
                dve.wait_ge(s_rexps, 4 * h + 2)
                step(stt(dk, tab(0), 0.0, dk, ALU.is_ge, ALU.mult))
                step(stt(e, tab(0), 0.0, e, ALU.is_le, ALU.mult))
                tt(dk, dk, e, ALU.add).then_inc(s_factors, 1)
                dc = A(A_RD + 512, 512)
                dve.wait_ge(s_rexps, 4 * h + 4)
                tt(dc, dc, e, ALU.add).then_inc(s_factors, 1)
                dve.wait_ge(s_factors, 2 * h + 2)
                low_weights(*range(18 + 6 * h, 22 + 6 * h))
                for a in range(2):
                    n = job("rs", h, a)
                    d = A(A_RD + 512 * a, 512)
                    done(dve, n)
                    stt(d, bank(n)[:, :], float(R_QK) ** -0.5, d, ALU.mult, ALU.mult).then_inc(free_s[n % BANKS], 1)
                if h + 1 < R_HEADS:
                    rotate_q(h + 1)
                else:
                    low_outputs(0, 12)
                for t in range(2):
                    i = 2 * h + t
                    n = job("ro", h, t)
                    dve.wait_ge(s_yms, i + 1)
                    ts(soft[:, 2 + t:3 + t], soft[:, t:t + 1], 1.0 / R_V, EPS, ALU.mult, ALU.add).then_inc(s_yroot, 1)
                    dve.wait_ge(s_yroot, 2 * i + 2)
                    step(dve.reciprocal(soft[:, 6 + t:7 + t], soft[:, 4 + t:5 + t]))
                    g = ret_gate(h)[:, t, :]
                    taken(dve, job("rg", h, t))
                    stt(g, bank(n)[:, :], soft[:, 6 + t:7 + t], g, ALU.mult, ALU.mult).then_inc(free_s[n % BANKS], 1)
            low_weights(*range(OUT_J + 4, OUT_J + 8))
            low_outputs(12, 16)
            dve.wait_ge(s_gate, 80)
            for i in range(4):
                add_mixer(1, i)
                if i == 1:
                    reciprocal_roots(0, 1)
                    dve.wait_ge(s_ab, 64)
                    modulated(1, 0)
            h2_turned(1, 0)
            reciprocal_roots(1, 2)
            modulated(1, 1)
            keep_logits(1, 0)
            h2_turned(1, 1)
            keep_logits(1, 1)
            route(1)
            experts(1)
            overflow(1)
            combine(1, 0)
            combine(1, 1)
            for t in range(2):
                reciprocal_roots(t, t + 1)
                if t == 0:
                    dve.wait_ge(s_fin_g, 16)
                stt(A(A_Y[t] + D, D), res[:, t, :], stat[:, 2, t:t + 1], A(A_SQUARES, D), ALU.mult, ALU.mult
                    ).then_inc(s_fin, 1)


_INS = ["x", "c", "ctx", "c_ctx", "ada_w", "ada_b", "norm1_g", "norm2_g", "w_in_e", "conv_w", "na_rpb", "w_out_e",
        "w_in_o", "ret_decay_f", "ret_decay_b", "w_out_o", "router_gw", "router_gb", "router_ew", "router_eb",
        "moe_w1", "moe_w3", "moe_w2", "final_g"]


def kernel(**inputs):
    import numpy as _np
    import concourse.bacc as _bacc
    from concourse import mybir as _mybir
    from concourse.bass_utils import run_bass_kernel_spmd as _run

    nc = _bacc.Bacc("TRN2", target_bir_lowering=False, num_devices=1)
    arrays, args, consts = {}, [], []

    def declare(name, a):
        arrays[name] = a
        return nc.dram_tensor(name, a.shape, _mybir.dt.from_np(a.dtype), kind="ExternalInput").ap()

    for name in _INS:
        a = inputs[name]
        if name == "na_rpb":
            a = a[..., ::-1]
        args.append(declare(f"in_{name}_dram", _np.ascontiguousarray(a)))
    for i, a in enumerate(shape_constants()):
        consts.append(declare(f"const_{i}_dram", _np.ascontiguousarray(a)))
    out = nc.dram_tensor("out_0_dram", (1, SEQ, D), _mybir.dt.from_np(_np.dtype("float32")), kind="ExternalOutput").ap()
    backbone(nc, args, consts, out)
    r = _run(nc, [arrays], core_ids=[0])
    return r.results[0]["out_0_dram"]
```
